# Optimizing a Trainium2 kernel written in Bass

```python
import jax, jax.numpy as jnp
from jax import lax
import numpy as np
import math

D_MODEL = 1024
BATCH = 1
SEQ = 256
DEPTH = 1

MEM_LEN = 256
ROPE_THETA = 10000.0
EPS = 1e-6
Q_BLOCK = 128

DSA_HEADS = 8
DSA_HEAD_DIM = 64
IDX_HEADS = 8
IDX_DIM = 64
TOPK_MAX = 256
MLA_HEADS = 8
MLA_NOPE = 64
MLA_ROPE = 32
MLA_QK = MLA_NOPE + MLA_ROPE
MLA_V = 64
MLA_Q_RANK = 256
MLA_KV_RANK = 128
MEM_HEADS = 4
MEM_HEAD_DIM = 64
N_GROUPS = 4
EXPERTS_PER_GROUP = 4
N_EXPERTS = N_GROUPS * EXPERTS_PER_GROUP
TOPK_IN_GROUP = 2
D_EXPERT = 256

DSA_WIDTH = DSA_HEADS * DSA_HEAD_DIM
MLA_WIDTH = MLA_HEADS * MLA_V
IN_SIZES = (DSA_WIDTH, DSA_HEAD_DIM, DSA_HEAD_DIM, IDX_HEADS * IDX_DIM, IDX_DIM, IDX_HEADS,
            MLA_Q_RANK, MLA_KV_RANK, MLA_ROPE, D_MODEL, D_MODEL)
IN_OFFSETS = tuple(int(v) for v in np.cumsum(IN_SIZES)[:-1])
N_IN = int(sum(IN_SIZES))


def rms_norm(x, g):
    xf = x.astype(jnp.float32)
    y = xf * lax.rsqrt(jnp.mean(xf * xf, axis=-1, keepdims=True) + EPS)
    return (y * g.astype(jnp.float32)).astype(x.dtype)

def rope(x, pos):
    d = x.shape[-1]
    half = d // 2
    inv_freq = ROPE_THETA ** (-jnp.arange(half, dtype=jnp.float32) / half)
    ang = pos.astype(jnp.float32)[..., None] * inv_freq
    ang = ang.reshape(ang.shape[:2] + (1,) * (x.ndim - 3) + (half,))
    cos, sin = jnp.cos(ang), jnp.sin(ang)
    xf = x.astype(jnp.float32)
    x1, x2 = xf[..., :half], xf[..., half:]
    return jnp.concatenate([x1 * cos - x2 * sin, x2 * cos + x1 * sin], axis=-1).astype(x.dtype)

def to_blocks(a):
    b, s = a.shape[:2]
    return jnp.moveaxis(a.reshape((b, s // Q_BLOCK, Q_BLOCK) + a.shape[2:]), 1, 0)

def from_blocks(a):
    nb, b, q = a.shape[:3]
    return jnp.moveaxis(a, 0, 1).reshape((b, nb * q) + a.shape[3:])

def gather_rows(table, idx):
    return jax.vmap(lambda tb, ib: tb[ib])(table, idx)

def dsa_attention(q, k, v, q_idx, k_idx, w_idx):
    s_len = q.shape[1]
    topk = min(TOPK_MAX, s_len // 4)
    key_pos = jnp.arange(s_len, dtype=jnp.int32)
    idx_scale = IDX_DIM ** -0.5 * IDX_HEADS ** -0.5
    att_scale = DSA_HEAD_DIM ** -0.5

    def block(args):
        qb, qib, wb, start = args
        qpos = start + jnp.arange(Q_BLOCK, dtype=jnp.int32)
        rel = jax.nn.relu(jnp.einsum('bqhd,bkd->bqhk', qib, k_idx).astype(jnp.float32))
        score = jnp.einsum('bqhk,bqh->bqk', rel, wb.astype(jnp.float32)) * idx_scale
        causal = key_pos[None, :] <= qpos[:, None]
        score = jnp.where(causal[None], score, -jnp.inf)
        _, sel = lax.top_k(score, topk)
        valid = sel <= qpos[None, :, None]
        ks = gather_rows(k, sel)
        vs = gather_rows(v, sel)
        logits = jnp.einsum('bqhd,bqkd->bqhk', qb, ks).astype(jnp.float32) * att_scale
        logits = jnp.where(valid[:, :, None, :], logits, -jnp.inf)
        p = jax.nn.softmax(logits, axis=-1).astype(vs.dtype)
        return jnp.einsum('bqhk,bqkd->bqhd', p, vs)

    starts = jnp.arange(s_len // Q_BLOCK, dtype=jnp.int32) * Q_BLOCK
    out = lax.map(block, (to_blocks(q), to_blocks(q_idx), to_blocks(w_idx), starts))
    return from_blocks(out)

def causal_block_attention(q, k, v, scale):
    s_len = q.shape[1]
    key_pos = jnp.arange(s_len, dtype=jnp.int32)

    def block(args):
        qb, start = args
        qpos = start + jnp.arange(Q_BLOCK, dtype=jnp.int32)
        logits = jnp.einsum('bqhd,bkhd->bhqk', qb, k).astype(jnp.float32) * scale
        mask = key_pos[None, :] <= qpos[:, None]
        logits = jnp.where(mask[None, None], logits, -jnp.inf)
        p = jax.nn.softmax(logits, axis=-1).astype(v.dtype)
        return jnp.einsum('bhqk,bkhd->bqhd', p, v)

    starts = jnp.arange(s_len // Q_BLOCK, dtype=jnp.int32) * Q_BLOCK
    return from_blocks(lax.map(block, (to_blocks(q), starts)))

def parallel_mixer(h, pos, w_in, dsa_q_g, dsa_k_g, mla_cq_g, mla_ckv_g, mla_w_uq, mla_w_ukv,
                   mla_q_g, mla_k_g, w_br_dsa, w_br_mla, w_out):
    b, s, _ = h.shape
    proj = h @ w_in
    dq, dk, dv, iq, ik, iw, cq, ckv, kpe, gd, gm = jnp.split(proj, IN_OFFSETS, axis=-1)

    q_a = rope(rms_norm(dq.reshape(b, s, DSA_HEADS, DSA_HEAD_DIM), dsa_q_g), pos)
    k_a = rope(rms_norm(dk, dsa_k_g), pos)
    q_i = rope(iq.reshape(b, s, IDX_HEADS, IDX_DIM), pos)
    k_i = rope(ik, pos)
    out_a = dsa_attention(q_a, k_a, dv, q_i, k_i, iw).reshape(b, s, DSA_WIDTH)

    q_b = (rms_norm(cq, mla_cq_g) @ mla_w_uq).reshape(b, s, MLA_HEADS, MLA_QK)
    kv_b = (rms_norm(ckv, mla_ckv_g) @ mla_w_ukv).reshape(b, s, MLA_HEADS, MLA_NOPE + MLA_V)
    k_nope, v_b = kv_b[..., :MLA_NOPE], kv_b[..., MLA_NOPE:]
    k_pe = jnp.broadcast_to(kpe[:, :, None, :], (b, s, MLA_HEADS, MLA_ROPE))
    k_b = jnp.concatenate([k_nope, k_pe], axis=-1)
    q_b = rms_norm(q_b, mla_q_g)
    k_b = rms_norm(k_b, mla_k_g)
    q_b = jnp.concatenate([q_b[..., :MLA_NOPE], rope(q_b[..., MLA_NOPE:], pos)], axis=-1)
    k_b = jnp.concatenate([k_b[..., :MLA_NOPE], rope(k_b[..., MLA_NOPE:], pos)], axis=-1)
    out_b = causal_block_attention(q_b, k_b, v_b, MLA_QK ** -0.5).reshape(b, s, MLA_WIDTH)

    merged = jax.nn.sigmoid(gd) * (out_a @ w_br_dsa) + jax.nn.sigmoid(gm) * (out_b @ w_br_mla)
    return merged @ w_out

def memory_cross_attention(h, mem, mem_g, w_q, w_kv, q_g, k_g, w_o):
    b, s, _ = h.shape
    m = mem.shape[1]
    q = rms_norm((h @ w_q).reshape(b, s, MEM_HEADS, MEM_HEAD_DIM), q_g)
    kv = (rms_norm(mem, mem_g) @ w_kv).reshape(b, m, 2, MEM_HEADS, MEM_HEAD_DIM)
    k = rms_norm(kv[:, :, 0], k_g)
    v = kv[:, :, 1]
    logits = jnp.einsum('bshd,bmhd->bhsm', q, k).astype(jnp.float32) * MEM_HEAD_DIM ** -0.5
    p = jax.nn.softmax(logits, axis=-1).astype(v.dtype)
    out = jnp.einsum('bhsm,bmhd->bshd', p, v).reshape(b, s, MEM_HEADS * MEM_HEAD_DIM)
    return out @ w_o

def hierarchical_moe(h, w_group, w_expert, expert_bias, w_gate, w_up, w_down):
    b, s, _ = h.shape
    p_group = jax.nn.softmax((h @ w_group).astype(jnp.float32), axis=-1)
    g_sel = jnp.argmax(p_group, axis=-1)
    p_g = jnp.take_along_axis(p_group, g_sel[..., None], axis=-1)
    aff = jax.nn.sigmoid((h @ w_expert).astype(jnp.float32)).reshape(b, s, N_GROUPS, EXPERTS_PER_GROUP)
    aff_grp = jnp.take_along_axis(aff, g_sel[..., None, None], axis=2)[..., 0, :]
    bias_grp = expert_bias.astype(jnp.float32).reshape(N_GROUPS, EXPERTS_PER_GROUP)[g_sel]
    _, local = lax.top_k(aff_grp + bias_grp, TOPK_IN_GROUP)
    a_sel = jnp.take_along_axis(aff_grp, local, axis=-1)
    w_sel = p_g * a_sel / jnp.sum(a_sel, axis=-1, keepdims=True)
    expert_id = g_sel[..., None] * EXPERTS_PER_GROUP + local
    combine = jnp.sum(jax.nn.one_hot(expert_id, N_EXPERTS, dtype=jnp.float32) * w_sel[..., None], axis=-2)
    y = jnp.zeros(h.shape, jnp.float32)
    for e in range(N_EXPERTS):
        act = jax.nn.silu(h @ w_gate[e]) * (h @ w_up[e])
        y = y + combine[..., e:e + 1] * (act @ w_down[e]).astype(jnp.float32)
    return y.astype(h.dtype)

def first_inputs(seed: int = 0) -> dict:
    key = jax.random.key(seed)
    ks = iter(jax.random.split(key, 40))

    def w(shape, fan_in):
        return jax.random.normal(next(ks), shape, jnp.float32) * fan_in ** -0.5

    def gain(shape):
        return 1.0 + 0.02 * jax.random.normal(next(ks), shape, jnp.float32)

    L = DEPTH
    x = jax.random.normal(next(ks), (BATCH, SEQ, D_MODEL), jnp.float32)
    mem = jax.random.normal(next(ks), (BATCH, MEM_LEN, D_MODEL), jnp.float32)
    offsets = jax.random.randint(next(ks), (BATCH, 1), 0, 128, dtype=jnp.int32)
    positions = offsets + jnp.arange(SEQ, dtype=jnp.int32)[None, :]
    return {
        'x': x,
        'mem': mem,
        'positions': positions,
        'attn_norm_g': gain((L, D_MODEL)),
        'w_in': w((L, D_MODEL, N_IN), D_MODEL),
        'dsa_q_norm_g': gain((L, DSA_HEAD_DIM)),
        'dsa_k_norm_g': gain((L, DSA_HEAD_DIM)),
        'mla_cq_norm_g': gain((L, MLA_Q_RANK)),
        'mla_ckv_norm_g': gain((L, MLA_KV_RANK)),
        'mla_w_uq': w((L, MLA_Q_RANK, MLA_HEADS * MLA_QK), MLA_Q_RANK),
        'mla_w_ukv': w((L, MLA_KV_RANK, MLA_HEADS * (MLA_NOPE + MLA_V)), MLA_KV_RANK),
        'mla_q_norm_g': gain((L, MLA_QK)),
        'mla_k_norm_g': gain((L, MLA_QK)),
        'w_branch_dsa': w((L, DSA_WIDTH, D_MODEL), DSA_WIDTH),
        'w_branch_mla': w((L, MLA_WIDTH, D_MODEL), MLA_WIDTH),
        'w_out': w((L, D_MODEL, D_MODEL), D_MODEL),
        'mem_x_norm_g': gain((L, D_MODEL)),
        'mem_norm_g': gain((L, D_MODEL)),
        'mem_w_q': w((L, D_MODEL, MEM_HEADS * MEM_HEAD_DIM), D_MODEL),
        'mem_w_kv': w((L, D_MODEL, 2 * MEM_HEADS * MEM_HEAD_DIM), D_MODEL),
        'mem_q_norm_g': gain((L, MEM_HEAD_DIM)),
        'mem_k_norm_g': gain((L, MEM_HEAD_DIM)),
        'mem_w_o': w((L, MEM_HEADS * MEM_HEAD_DIM, D_MODEL), MEM_HEADS * MEM_HEAD_DIM),
        'moe_norm_g': gain((L, D_MODEL)),
        'moe_w_group': w((L, D_MODEL, N_GROUPS), D_MODEL),
        'moe_w_expert': w((L, D_MODEL, N_EXPERTS), D_MODEL),
        'moe_expert_bias': 0.01 * jax.random.normal(next(ks), (L, N_EXPERTS), jnp.float32),
        'moe_w_gate': w((L, N_EXPERTS, D_MODEL, D_EXPERT), D_MODEL),
        'moe_w_up': w((L, N_EXPERTS, D_MODEL, D_EXPERT), D_MODEL),
        'moe_w_down': w((L, N_EXPERTS, D_EXPERT, D_MODEL), D_EXPERT),
    }

def first_block(x, mem, positions, attn_norm_g, w_in, dsa_q_norm_g, dsa_k_norm_g, mla_cq_norm_g,
              mla_ckv_norm_g, mla_w_uq, mla_w_ukv, mla_q_norm_g, mla_k_norm_g, w_branch_dsa,
              w_branch_mla, w_out, mem_x_norm_g, mem_norm_g, mem_w_q, mem_w_kv, mem_q_norm_g,
              mem_k_norm_g, mem_w_o, moe_norm_g, moe_w_group, moe_w_expert, moe_expert_bias,
              moe_w_gate, moe_w_up, moe_w_down):
    for l in range(DEPTH):
        h = rms_norm(x, attn_norm_g[l])
        x = x + parallel_mixer(h, positions, w_in[l], dsa_q_norm_g[l], dsa_k_norm_g[l],
                               mla_cq_norm_g[l], mla_ckv_norm_g[l], mla_w_uq[l], mla_w_ukv[l],
                               mla_q_norm_g[l], mla_k_norm_g[l], w_branch_dsa[l], w_branch_mla[l],
                               w_out[l])
        h = rms_norm(x, mem_x_norm_g[l])
        x = x + memory_cross_attention(h, mem, mem_norm_g[l], mem_w_q[l], mem_w_kv[l],
                                       mem_q_norm_g[l], mem_k_norm_g[l], mem_w_o[l])
        h = rms_norm(x, moe_norm_g[l])
        x = x + hierarchical_moe(h, moe_w_group[l], moe_w_expert[l], moe_expert_bias[l],
                                 moe_w_gate[l], moe_w_up[l], moe_w_down[l])
    return x


DEPTH_2 = 2

GRID_W = 64
CTX_LEN = 256
N_MIXERS = 2
N_SSD_LAYERS = (DEPTH_2 + N_MIXERS - 1) // N_MIXERS
N_ATTN_LAYERS = DEPTH_2 // N_MIXERS
SSD_EXPAND = 2
D_INNER = SSD_EXPAND * D_MODEL
SSD_HEADDIM = 64
SSD_HEADS = D_INNER // SSD_HEADDIM
SSD_GROUPS = 8
SSD_HPG = SSD_HEADS // SSD_GROUPS
D_STATE = 128
CONV_W = 5
SSD_CHUNK = 128
CONV_DIM = D_INNER + 2 * SSD_GROUPS * D_STATE
SSD_IN_DIM = 2 * D_INNER + 2 * SSD_GROUPS * D_STATE + 2 * SSD_HEADS
HEAD_DIM = 64
N_Q_HEADS = D_MODEL // HEAD_DIM
N_KV_HEADS = 4
Q_PER_KV = N_Q_HEADS // N_KV_HEADS
D_ATTN = N_Q_HEADS * HEAD_DIM
QKV_DIM = (N_Q_HEADS + 2 * N_KV_HEADS) * HEAD_DIM
ROPE_AXIS_DIM = HEAD_DIM // 2
N_EXPERTS_2 = 16
D_EXPERT_2 = D_MODEL
EC_CAPACITY = 2


def rmsnorm(x, w):
    xf = x.astype(jnp.float32)
    y = xf * lax.rsqrt(jnp.mean(xf * xf, axis=-1, keepdims=True) + EPS)
    return (y * w.astype(jnp.float32)).astype(x.dtype)

def dwconv_centred(u, w, b):
    out = lax.conv_general_dilated(
        u, w[:, None, :].astype(u.dtype), window_strides=(1,),
        padding=[(CONV_W // 2, CONV_W // 2)],
        dimension_numbers=('NWC', 'WIO', 'NWC'), feature_group_count=u.shape[-1])
    return out + b.astype(u.dtype)

def ssd_chunked(xs, dt, A, Bm, Cm, h0):
    b, L = xs.shape[:2]
    Q = SSD_CHUNK
    nc = L // Q
    x = xs.reshape(b, nc, Q, SSD_GROUPS, SSD_HPG, SSD_HEADDIM)
    dtc = dt.reshape(b, nc, Q, SSD_GROUPS, SSD_HPG)
    Bc = Bm.reshape(b, nc, Q, SSD_GROUPS, D_STATE)
    Cc = Cm.reshape(b, nc, Q, SSD_GROUPS, D_STATE)
    a = jnp.moveaxis(dtc * A.reshape(SSD_GROUPS, SSD_HPG), 2, -1)
    acum = jnp.cumsum(a, axis=-1)
    tri = jnp.tril(jnp.ones((Q, Q), dtype=bool))
    seg = jnp.exp(jnp.where(tri, acum[..., :, None] - acum[..., None, :], -jnp.inf))
    xdt = x * dtc[..., None].astype(x.dtype)
    cb = jnp.einsum('bclgn,bcsgn->bcgls', Cc, Bc)
    y_diag = jnp.einsum('bcgrls,bcsgrp->bclgrp', cb[:, :, :, None] * seg, xdt)
    decay_end = jnp.exp(acum[..., -1:] - acum)
    states = jnp.einsum('bcsgn,bcgrs,bcsgrp->bcgrpn', Bc, decay_end, xdt)
    chunk_decay = jnp.exp(acum[..., -1])

    def step(h, inp):
        dec, st = inp
        return dec[..., None, None] * h + st, h

    h_last, h_prev = lax.scan(step, h0, (jnp.moveaxis(chunk_decay, 1, 0), jnp.moveaxis(states, 1, 0)))
    h_prev = jnp.moveaxis(h_prev, 0, 1)
    y_off = jnp.einsum('bclgn,bcgrpn,bcgrl->bclgrp', Cc, h_prev, jnp.exp(acum))
    y = (y_diag + y_off).reshape(b, L, SSD_HEADS, SSD_HEADDIM)
    return y, h_last

def ssd_mixer(h_ctx, h_lat, in_w, conv_w, conv_b, dt_bias, A_log, D_skip, norm_w, out_w, ctx_out):
    def project(u):
        b, L = u.shape[:2]
        z, xbc, dtr = jnp.split(u @ in_w, [D_INNER, D_INNER + CONV_DIM], axis=-1)
        xbc = jax.nn.silu(dwconv_centred(xbc, conv_w, conv_b))
        xs, Bm, Cm = jnp.split(xbc, [D_INNER, D_INNER + SSD_GROUPS * D_STATE], axis=-1)
        dt = jax.nn.softplus(dtr.astype(jnp.float32).reshape(b, L, 2, SSD_HEADS) + dt_bias)
        return (z, xs.reshape(b, L, SSD_HEADS, SSD_HEADDIM),
                Bm.reshape(b, L, SSD_GROUPS, D_STATE), Cm.reshape(b, L, SSD_GROUPS, D_STATE), dt)

    zc, xc, Bc, Cc, dtc = project(h_ctx)
    zl, xl, Bl, Cl, dtl = project(h_lat)
    A = -jnp.exp(A_log.astype(jnp.float32))
    b = h_lat.shape[0]
    h0 = jnp.zeros((b, SSD_GROUPS, SSD_HPG, SSD_HEADDIM, D_STATE), jnp.float32)
    flip = lambda t: jnp.flip(t, axis=1)
    yc_f, hc_f = ssd_chunked(xc, dtc[:, :, 0], A[0], Bc, Cc, h0)
    yl_f, _ = ssd_chunked(xl, dtl[:, :, 0], A[0], Bl, Cl, hc_f)
    yc_b, hc_b = ssd_chunked(flip(xc), flip(dtc[:, :, 1]), A[1], flip(Bc), flip(Cc), h0)
    yl_b, _ = ssd_chunked(flip(xl), flip(dtl[:, :, 1]), A[1], flip(Bl), flip(Cl), hc_b)

    def finish(y_f, y_b, xs, z):
        bb, L = xs.shape[:2]
        y = y_f + flip(y_b) + D_skip[:, None] * xs
        y = y.reshape(bb, L, D_INNER).astype(z.dtype)
        return rmsnorm(y * jax.nn.silu(z), norm_w) @ out_w

    out_lat = finish(yl_f, yl_b, xl, zl)
    out_ctx = finish(yc_f, yc_b, xc, zc) if ctx_out else None
    return out_ctx, out_lat

def rope_2d(t, cos, sin):
    half = t.shape[-1] // 2
    t1, t2 = t[..., :half], t[..., half:]
    return jnp.concatenate([t1 * cos - t2 * sin, t2 * cos + t1 * sin], axis=-1)

def attn_mixer(h_ctx, h_lat, qkv_w, q_norm_w, k_norm_w, out_w, cos, sin, ctx_out):
    scale = 1.0 / math.sqrt(HEAD_DIM)

    def project(u):
        b, L = u.shape[:2]
        q, k, v = jnp.split(u @ qkv_w, [D_ATTN, D_ATTN + N_KV_HEADS * HEAD_DIM], axis=-1)
        q = rmsnorm(q.reshape(b, L, N_KV_HEADS, Q_PER_KV, HEAD_DIM), q_norm_w)
        k = rmsnorm(k.reshape(b, L, N_KV_HEADS, HEAD_DIM), k_norm_w)
        return q, k, v.reshape(b, L, N_KV_HEADS, HEAD_DIM)

    qc, kc, vc = project(h_ctx)
    ql, kl, vl = project(h_lat)
    cos = cos.astype(ql.dtype)
    sin = sin.astype(ql.dtype)
    ql = rope_2d(ql, cos[:, None, None], sin[:, None, None])
    kl = rope_2d(kl, cos[:, None], sin[:, None])
    k_all = jnp.concatenate([kl, kc], axis=1)
    v_all = jnp.concatenate([vl, vc], axis=1)

    def attend(q_blk, k, v):
        s = jnp.einsum('bqkgd,bskd->bkgqs', q_blk, k, preferred_element_type=jnp.float32) * scale
        p = jax.nn.softmax(s, axis=-1).astype(v.dtype)
        return jnp.einsum('bkgqs,bskd->bqkgd', p, v)

    b, S = h_lat.shape[:2]
    nb = S // Q_BLOCK
    qb = jnp.moveaxis(ql.reshape(b, nb, Q_BLOCK, N_KV_HEADS, Q_PER_KV, HEAD_DIM), 1, 0)
    o = lax.map(lambda q_blk: attend(q_blk, k_all, v_all), qb)
    out_lat = jnp.moveaxis(o, 0, 1).reshape(b, S, D_ATTN) @ out_w
    out_ctx = None
    if ctx_out:
        bc, Lc = h_ctx.shape[:2]
        out_ctx = attend(qc, kc, vc).reshape(bc, Lc, D_ATTN) @ out_w
    return out_ctx, out_lat

def moe_ec(h, router_w, w1, w3, w2):
    b, T, _ = h.shape
    cap = EC_CAPACITY * T // N_EXPERTS_2
    logits = jnp.einsum('btd,de->bte', h, router_w, preferred_element_type=jnp.float32)
    aff = jax.nn.softmax(logits, axis=-1)
    gate, idx = lax.top_k(jnp.swapaxes(aff, 1, 2), cap)
    bidx = jnp.arange(b)[:, None, None]
    xg = h[bidx, idx]
    a = jnp.einsum('becd,edf->becf', xg, w1)
    g = jnp.einsum('becd,edf->becf', xg, w3)
    y = jnp.einsum('becf,efd->becd', jax.nn.silu(a) * g, w2)
    y = y * gate[..., None].astype(y.dtype)
    return jnp.zeros_like(h).at[bidx, idx].add(y.astype(h.dtype))

def second_inputs(seed: int = 0) -> dict:
    key = jax.random.key(seed)
    ks = jax.random.split(key, 26)
    f32 = jnp.float32
    nrm = lambda k, shape, s: jax.random.normal(k, shape, f32) * s
    dt0 = jnp.exp(jax.random.uniform(ks[11], (N_SSD_LAYERS, 2, SSD_HEADS), f32, math.log(1e-3), math.log(1e-1)))
    return {
        "x": nrm(ks[0], (BATCH, SEQ, D_MODEL), 1.0),
        "c": nrm(ks[1], (BATCH, D_MODEL), 1.0),
        "ctx": nrm(ks[2], (BATCH, CTX_LEN, D_MODEL), 1.0),
        "c_ctx": nrm(ks[3], (D_MODEL,), 1.0),
        "ada_w": nrm(ks[4], (DEPTH_2, D_MODEL, 6 * D_MODEL), D_MODEL ** -0.5),
        "ada_b": nrm(ks[5], (DEPTH_2, 6 * D_MODEL), 0.02),
        "norm1_w": 1.0 + nrm(ks[6], (DEPTH_2, D_MODEL), 0.02),
        "norm2_w": 1.0 + nrm(ks[7], (DEPTH_2, D_MODEL), 0.02),
        "ssd_in_w": nrm(ks[8], (N_SSD_LAYERS, D_MODEL, SSD_IN_DIM), D_MODEL ** -0.5),
        "ssd_conv_w": nrm(ks[9], (N_SSD_LAYERS, CONV_W, CONV_DIM), CONV_W ** -0.5),
        "ssd_conv_b": nrm(ks[10], (N_SSD_LAYERS, CONV_DIM), 0.02),
        "ssd_dt_bias": dt0 + jnp.log(-jnp.expm1(-dt0)),
        "ssd_A_log": jnp.log(jax.random.uniform(ks[12], (N_SSD_LAYERS, 2, SSD_HEADS), f32, 1.0, 16.0)),
        "ssd_D": 1.0 + nrm(ks[13], (N_SSD_LAYERS, SSD_HEADS), 0.1),
        "ssd_norm_w": 1.0 + nrm(ks[14], (N_SSD_LAYERS, D_INNER), 0.02),
        "ssd_out_w": nrm(ks[15], (N_SSD_LAYERS, D_INNER, D_MODEL), D_INNER ** -0.5),
        "attn_qkv_w": nrm(ks[16], (N_ATTN_LAYERS, D_MODEL, QKV_DIM), D_MODEL ** -0.5),
        "attn_q_norm_w": 1.0 + nrm(ks[17], (N_ATTN_LAYERS, HEAD_DIM), 0.02),
        "attn_k_norm_w": 1.0 + nrm(ks[18], (N_ATTN_LAYERS, HEAD_DIM), 0.02),
        "attn_out_w": nrm(ks[19], (N_ATTN_LAYERS, D_ATTN, D_MODEL), D_ATTN ** -0.5),
        "moe_router_w": nrm(ks[20], (DEPTH_2, D_MODEL, N_EXPERTS_2), D_MODEL ** -0.5),
        "moe_w1": nrm(ks[21], (DEPTH_2, N_EXPERTS_2, D_MODEL, D_EXPERT_2), D_MODEL ** -0.5),
        "moe_w3": nrm(ks[22], (DEPTH_2, N_EXPERTS_2, D_MODEL, D_EXPERT_2), D_MODEL ** -0.5),
        "moe_w2": nrm(ks[23], (DEPTH_2, N_EXPERTS_2, D_EXPERT_2, D_MODEL), D_EXPERT_2 ** -0.5),
        "final_norm_w": 1.0 + nrm(ks[24], (D_MODEL,), 0.02),
    }

def second_block(x, c, ctx, c_ctx, ada_w, ada_b, norm1_w, norm2_w, ssd_in_w, ssd_conv_w, ssd_conv_b,
              ssd_dt_bias, ssd_A_log, ssd_D, ssd_norm_w, ssd_out_w, attn_qkv_w, attn_q_norm_w,
              attn_k_norm_w, attn_out_w, moe_router_w, moe_w1, moe_w3, moe_w2, final_norm_w):
    S = x.shape[1]
    rows = S // GRID_W
    row = jnp.repeat(jnp.arange(rows), GRID_W, total_repeat_length=S).astype(jnp.float32)
    col = jnp.tile(jnp.arange(GRID_W), rows).astype(jnp.float32)
    inv_freq = ROPE_THETA ** (-jnp.arange(0, ROPE_AXIS_DIM, 2, dtype=jnp.float32) / ROPE_AXIS_DIM)
    ang = jnp.concatenate([row[:, None] * inv_freq, col[:, None] * inv_freq], axis=-1)
    cos, sin = jnp.cos(ang), jnp.sin(ang)

    silu_c = jax.nn.silu(c)
    silu_cc = jax.nn.silu(c_ctx)
    for i in range(DEPTH_2):
        last = i == DEPTH_2 - 1
        j = i // N_MIXERS
        sh1l, sc1l, g1l, sh2l, sc2l, g2l = [m[:, None, :] for m in jnp.split(silu_c @ ada_w[i] + ada_b[i], 6, axis=-1)]
        sh1c, sc1c, g1c, sh2c, sc2c, g2c = jnp.split(silu_cc @ ada_w[i] + ada_b[i], 6, axis=-1)
        h_lat = rmsnorm(x, norm1_w[i]) * (1.0 + sc1l) + sh1l
        h_ctx = rmsnorm(ctx, norm1_w[i]) * (1.0 + sc1c) + sh1c
        if i % N_MIXERS == 0:
            o_ctx, o_lat = ssd_mixer(h_ctx, h_lat, ssd_in_w[j], ssd_conv_w[j], ssd_conv_b[j], ssd_dt_bias[j],
                                     ssd_A_log[j], ssd_D[j], ssd_norm_w[j], ssd_out_w[j], not last)
        else:
            o_ctx, o_lat = attn_mixer(h_ctx, h_lat, attn_qkv_w[j], attn_q_norm_w[j], attn_k_norm_w[j],
                                      attn_out_w[j], cos, sin, not last)
        x = x + g1l * o_lat
        x = x + g2l * moe_ec(rmsnorm(x, norm2_w[i]) * (1.0 + sc2l) + sh2l,
                             moe_router_w[i], moe_w1[i], moe_w3[i], moe_w2[i])
        if not last:
            ctx = ctx + g1c * o_ctx
            ctx = ctx + g2c * moe_ec(rmsnorm(ctx, norm2_w[i]) * (1.0 + sc2c) + sh2c,
                                     moe_router_w[i], moe_w1[i], moe_w3[i], moe_w2[i])
    return rmsnorm(x, final_norm_w)


def setup_inputs(seed=0):
    out = dict(first_inputs(seed))
    for name, value in second_inputs(seed + 1).items():
        if name != "x":
            out[name + "_2"] = value
    return out


def reference(
    x, mem, positions, attn_norm_g, w_in, dsa_q_norm_g, dsa_k_norm_g, mla_cq_norm_g,
    mla_ckv_norm_g, mla_w_uq, mla_w_ukv, mla_q_norm_g, mla_k_norm_g, w_branch_dsa, w_branch_mla,
    w_out, mem_x_norm_g, mem_norm_g, mem_w_q, mem_w_kv, mem_q_norm_g, mem_k_norm_g, mem_w_o,
    moe_norm_g, moe_w_group, moe_w_expert, moe_expert_bias, moe_w_gate, moe_w_up, moe_w_down,
    c_2, ctx_2, c_ctx_2, ada_w_2, ada_b_2, norm1_w_2, norm2_w_2, ssd_in_w_2, ssd_conv_w_2,
    ssd_conv_b_2, ssd_dt_bias_2, ssd_A_log_2, ssd_D_2, ssd_norm_w_2, ssd_out_w_2, attn_qkv_w_2,
    attn_q_norm_w_2, attn_k_norm_w_2, attn_out_w_2, moe_router_w_2, moe_w1_2, moe_w3_2,
    moe_w2_2, final_norm_w_2,
):
    x = first_block(
        x, mem, positions, attn_norm_g, w_in, dsa_q_norm_g, dsa_k_norm_g, mla_cq_norm_g,
        mla_ckv_norm_g, mla_w_uq, mla_w_ukv, mla_q_norm_g, mla_k_norm_g, w_branch_dsa,
        w_branch_mla, w_out, mem_x_norm_g, mem_norm_g, mem_w_q, mem_w_kv, mem_q_norm_g,
        mem_k_norm_g, mem_w_o, moe_norm_g, moe_w_group, moe_w_expert, moe_expert_bias,
        moe_w_gate, moe_w_up, moe_w_down,
    )
    return second_block(
        x, c_2, ctx_2, c_ctx_2, ada_w_2, ada_b_2, norm1_w_2, norm2_w_2, ssd_in_w_2,
        ssd_conv_w_2, ssd_conv_b_2, ssd_dt_bias_2, ssd_A_log_2, ssd_D_2, ssd_norm_w_2,
        ssd_out_w_2, attn_qkv_w_2, attn_q_norm_w_2, attn_k_norm_w_2, attn_out_w_2,
        moe_router_w_2, moe_w1_2, moe_w3_2, moe_w2_2, final_norm_w_2,
    )


_drawn_inputs = setup_inputs


def setup_inputs(seed=0):
    import zlib

    import numpy as np

    out = dict(_drawn_inputs(seed))
    spreads = {}
    factors = {'dsa_q_norm_g': 4.666,
     'dsa_k_norm_g': 3.98,
     'mla_cq_norm_g': 3.119,
     'mla_ckv_norm_g': 2.966,
     'mla_q_norm_g': 3.672,
     'mla_k_norm_g': 4.041,
     'mem_q_norm_g': 3.121,
     'mem_k_norm_g': 5.445,
     'moe_expert_bias': 3.394,
     'ssd_conv_b_2': 3.141,
     'ssd_D_2': 2.719,
     'ssd_norm_w_2': 3.165,
     'attn_q_norm_w_2': 8.0,
     'attn_k_norm_w_2': 8.0,
     'final_norm_w_2': 2.848}
    for name, (base, spread) in spreads.items():
        noise = np.random.default_rng([zlib.crc32(name.encode()), seed]).standard_normal(out[name].shape)
        drawn = base * np.exp(spread * noise) if base else spread * noise
        out[name] = __import__('jax').numpy.asarray(drawn.astype(out[name].dtype))
    for name, factor in factors.items():
        out[name] = (out[name] * factor).astype(out[name].dtype)
    return out
```

```python
import numpy as np
import concourse.bass as bass
from concourse import mybir
from contextlib import ExitStack

F32 = mybir.dt.float32
I32 = mybir.dt.int32
ALU = mybir.AluOpType
ACT = mybir.ActivationFunctionType
AX = mybir.AxisListType

P = 128
D = 1024
KD = D // P
S = 256
NT = S // P
EPS = 1e-6
DSA_H, HD = 8, 64
MLA_H, MLA_QK, MLA_NOPE, MLA_ROPE, MLA_V = 8, 96, 64, 32, 64
MLA_QR, MLA_KVR = 256, 128
MEM_H = 4
N_IN = 3688
O_IQ, O_IW, O_CQ, O_CKV, O_KPE, O_GD, O_GM = 640, 1216, 1224, 1480, 1608, 1640, 2664
TOPK = 64
N_EXP, GROUPS, D_EXP = 16, 4, 256
NEG = -3.0e38
TAKEN = -3.3e38
BIG = 1.0e30

D_INNER, SSD_G, HPG, SSD_HD, D_STATE = 2048, 8, 4, 64, 128
SSD_H = SSD_G * HPG
GW = HPG * SSD_HD
CONV_W = 5
SSD_IN = 6208
O_XS, O_B, O_C, O_DT = 2048, 4096, 5120, 6144
QH, KVH, QPK = 16, 4, 4
CAP = 32

SLOTS, SLOT = 6, 4096

CONSTS = {}


def constant_table():
    p = np.arange(P)
    parts = {
        "ident": np.eye(P),
        "upto": p[:, None] <= p[None, :],
        "from": p[:, None] >= p[None, :],
        "ones": np.ones((P, P)),
        "causal": np.stack([(np.arange(S)[None, :] <= (p + t * P)[:, None]) for t in range(NT)], 1),
        "inv_freq": np.broadcast_to(np.concatenate([
            np.float32(10000.0) ** (-np.arange(32, dtype=np.float32) / np.float32(32)),
            np.float32(10000.0) ** (-np.arange(16, dtype=np.float32) / np.float32(16))]), (P, 48)),
        "down16": np.broadcast_to(np.arange(16, 0, -1), (P, 16)),
        "slot": np.broadcast_to(np.arange(CAP), (P, CAP)),
    }
    f = np.float32(10000.0) ** (-np.arange(0, 32, 2, dtype=np.float32) / np.float32(32))
    tok = p[:, None] + np.arange(NT)[None, :] * P
    ang = np.concatenate([(tok // 64)[..., None].astype(np.float32) * f,
                          (tok % 64)[..., None].astype(np.float32) * f], -1)
    parts["cos2d"], parts["sin2d"] = np.cos(ang), np.sin(ang)
    at, cols = 0, []
    for name, a in parts.items():
        a = np.asarray(a, np.float32).reshape(P, -1)
        CONSTS[name] = (at, at + a.shape[1])
        at += a.shape[1]
        cols.append(a)
    return np.ascontiguousarray(np.concatenate(cols, 1))


VECTORS = [
    (0, 0, "attn_norm_g", 8), (0, 8, "mem_x_norm_g", 8), (0, 16, "mem_norm_g", 8), (0, 24, "moe_norm_g", 8),
    (0, 32, "norm1_w_2", 16), (0, 48, "norm2_w_2", 16), (0, 64, "ssd_norm_w_2", 16),
    (0, 80, "mla_cq_norm_g", 2), (0, 82, "mla_ckv_norm_g", 1), (0, 83, "c_2", 8), (0, 91, "c_ctx_2", 8),
    (1, 0, "ssd_conv_w_2", 128), (2, 0, "ssd_conv_w_2", 32), (2, 32, "ssd_conv_b_2", 32)]
VCOL = {name: tile * P + row for tile, row, name, _ in VECTORS if not (name == "ssd_conv_w_2" and tile == 2)}

DVE, ACTE = "dve", "act"


class Bank:

    def __init__(self, ap, full, by, done, emptied):
        self.ap, self.full, self.by, self.done, self.emptied = ap, full, by, done, emptied


class Banks:

    def __init__(self, psum, emptied):
        self.psum, self.sem = psum, emptied
        self.order, self.names, self.count = [], {}, {k: 0 for k in emptied}

    def open(self, name, by):
        n = len(self.order)
        self.count[by] += 1
        before = None
        if n >= 8:
            b = self.order[n - 8]
            before = (self.sem[b.by], b.done)
        bank = Bank(self.psum[n % 8], n + 1, by, self.count[by], before)
        self.order.append(bank)
        assert name not in self.names, name
        self.names[name] = bank
        return bank

    def __getitem__(self, name):
        return self.names[name]


class Piece:

    def __init__(self, ap, sem, full, before):
        self.ap, self.sem, self.full = ap, sem, full
        self.before = before
        self.freed = None


class Ring:

    def __init__(self, slots, loaded):
        self.slots, self.loaded = slots, loaded
        self.total = [0] * SLOTS
        self.last = [None] * SLOTS
        self.pieces = {}

    def add(self, name, slot, dmas=1):
        self.total[slot] += 16 * dmas
        piece = Piece(self.slots[:, slot, :], self.loaded[slot], self.total[slot], self.last[slot])
        self.pieces[name] = self.last[slot] = piece
        return piece

    def __getitem__(self, name):
        return self.pieces[name]


def build(nc, A, out):
    ctx = ExitStack()
    sem_names = set()

    def sem(name):
        assert name not in sem_names, name
        sem_names.add(name)
        return ctx.enter_context(nc.semaphore(name))

    def sb(name, shape, dt=F32, scope=None):
        return (scope or ctx).enter_context(nc.sbuf_tensor(name, shape, dt))

    def flat(name):
        a = A[name]
        return a.rearrange("a b -> (a b)") if len(a.shape) == 2 else a.rearrange("a b c -> (a b c)") if len(a.shape) == 3 else a

    with ctx:
        slots = sb("slots", [P, SLOTS, SLOT])
        X = sb("X", [P, NT, D])
        C = sb("C", [P, NT, D])
        consts = sb("consts", [P, CONSTS["sin2d"][1]])
        vcols = sb("vcols", [P, 3 * P])
        modcol = sb("modcol", [P, 2, 12, 4, 2])
        eps_rows = sb("eps_rows", [P, 64])
        rstd = sb("rstd", [P, 64])
        minus_half = sb("minus_half", [P, 64])
        routers = sb("routers", [P, 2, KD, N_EXP])
        psum = [ctx.enter_context(nc.psum_tensor(f"bank{i}", [P, 512], F32)) for i in range(8)]

        def const(name):
            a, b = CONSTS[name]
            return consts[:, a:b]

        ident = const("ident")

        bank_full = sem("bank_full")
        emptied = {DVE: sem("emptied_by_dve"), ACTE: sem("emptied_by_act")}
        banks = Banks(psum, emptied)
        slot_loaded = [sem(f"slot_loaded{i}") for i in range(SLOTS)]
        ring = Ring(slots, slot_loaded)
        stored = sem("stored")
        routers_loaded = sem("routers_loaded")
        dve_step, act_step, pool_step = sem("dve_step"), sem("act_step"), sem("pool_step")
        steps = {}

        def chain(eng, own):
            def link(ins):
                steps[own.name] = steps.get(own.name, 0) + 1
                ins.then_inc(own, 1)
                eng.wait_ge(own, steps[own.name])
            return link

        def w(name, k, n, c0, c1, k0=0, k1=None):
            return A[name].rearrange("(k p) n -> p k n", p=P)[:, k0:k1 or k, c0:c1]

        stream = []

        def weights(name, parts, among=SLOTS):
            slot = 0 if not stream else (stream[-1][2] + 1) % among
            piece = ring.add(name, slot, len(parts))
            stream.append((piece, parts, slot))

        def view(piece, at, k, n):
            return piece.ap[:, at:at + k * n].rearrange("p (k n) -> p k n", n=n)

        w_in = A["w_in"].rearrange("a r c -> (a r) c").rearrange("(k p) n -> p k n", p=P)
        def rows(name):
            return A[name].rearrange("a r c -> (a r) c").rearrange("(k p) n -> p k n", p=P)
        CI = N_IN // 8
        for n in range(8):
            weights(("in", n), [(0, KD, CI, w_in[:, :, n * CI:(n + 1) * CI])])
        weights("mla", [(0, 2, 768, rows("mla_w_uq")), (1536, 1, 1024, rows("mla_w_ukv"))])
        weights("br_dsa", [(0, 4, D, rows("w_branch_dsa"))])
        weights("br_mla", [(0, 4, D, rows("w_branch_mla"))])
        for h in range(2):
            weights(("w_out", h), [(0, 4, D, rows("w_out")[:, 4 * h:4 * h + 4, :])])
        weights("mem_q", [(0, KD, 256, rows("mem_w_q"))])
        weights("mem_kv", [(0, KD, 512, rows("mem_w_kv"))])
        weights("mem_o", [(0, 2, D, rows("mem_w_o"))])
        gate_v = A["moe_w_gate"].rearrange("a e (k p) n -> p (a e) k n", p=P)
        up_v = A["moe_w_up"].rearrange("a e (k p) n -> p (a e) k n", p=P)
        down_v = A["moe_w_down"].rearrange("a e (k p) n -> p (a e) k n", p=P)
        MOE1 = []
        for j in range(6):
            e = (0, 1, 0, 2, 3, 2)[j]
            if j % 3 < 2:
                weights(("moe1", j), [(0, KD, D_EXP, gate_v[:, e]), (2048, KD, D_EXP, up_v[:, e])])
            else:
                weights(("moe1", j), [(2048 * i, 2, D, down_v[:, e + i]) for i in range(2)])
            MOE1.append((stream[-1][2], e))
        MOE1_TURNS = N_EXP // 4
        for j in range(6):
            ring.total[MOE1[j][0]] += 32 * (MOE1_TURNS - 1)
        ada_v = A["ada_w_2"].rearrange("l (k p) (c n) -> p l c k n", p=P, n=512)
        for c in range(24):
            weights(("ada", c), [(0, KD, 512, ada_v[:, c // 12, c % 12])])
        scratch_use = Piece(None, None, 0, None)
        for slot in range(3, SLOTS):
            ring.last[slot] = scratch_use
        ssd_v = rows("ssd_in_w_2")
        weights("dt", [(0, KD, 64, ssd_v[:, :, O_DT:])], among=3)
        for g in range(SSD_G):
            weights(("grp", g), [(0, KD, 256, ssd_v[:, :, O_XS + g * 256:O_XS + (g + 1) * 256]),
                                 (2048, KD, 128, ssd_v[:, :, O_B + g * 128:O_B + (g + 1) * 128]),
                                 (3072, KD, 128, ssd_v[:, :, O_C + g * 128:O_C + (g + 1) * 128])], among=3)
        for n in range(4):
            weights(("z", n), [(0, KD, 512, ssd_v[:, :, n * 512:(n + 1) * 512])], among=3)
        for n in range(4):
            weights(("ssd_out", n), [(0, 4, D, rows("ssd_out_w_2")[:, 4 * n:4 * n + 4, :])], among=3)
        w_v = [A[f"moe_w{m}_2"].rearrange("l e (k p) n -> p (l e) k n", p=P) for m in (1, 3, 2)]

        def moe2_weights(l):
            for j in range(6):
                weights(("moe2", l, j), [(0, 4, D, w_v[j // 2][:, l * N_EXP, 4 * (j % 2):4 * (j % 2) + 4])])
            for j in range(6):
                ring.total[stream[-1 - j][2]] += 16 * (N_EXP - 1)

        moe2_weights(0)
        for n in range(3):
            weights(("qkv", n), [(0, KD, 512, rows("attn_qkv_w_2")[:, :, n * 512:(n + 1) * 512])])
        for n in range(2):
            weights(("attn_out", n), [(0, 4, D, rows("attn_out_w_2")[:, 4 * n:4 * n + 4, :])])
        moe2_weights(1)
        issued = [0]

        def load_weights(sp, upto=1000):
            while issued[0] < min(upto, len(stream)):
                piece, parts, _ = stream[issued[0]]
                if piece.before is not None:
                    if piece.before.freed is None:
                        return
                    sp.wait_ge(*piece.before.freed)
                for at, k, n, src in parts:
                    sp.dma_start(view(piece, at, k, n), src).then_inc(piece.sem, 16)
                issued[0] += 1

        def root(pool, at, n, width, done=None):
            link = chain(pool, pool_step)
            c = slice(at, at + n)
            link(pool.tensor_scalar(rstd[:, c], eps_rows[:, c], float(width * EPS), None, ALU.add))
            i = pool.tensor_tensor(rstd[:, c], rstd[:, c], minus_half[:, 0:n], ALU.pow)
            if done is not None:
                i.then_inc(done, 1)

        ld = {k: sem("ld_" + k) for k in ("consts", "vec", "x", "misc", "pos")}
        vrow_zeroed = sem("vrow_zeroed")
        trig_ready = sem("trig_ready")
        cs = sb("cs", [P, 2, NT, 48])
        MISC = ["dsa_q_norm_g", "dsa_k_norm_g", "mla_q_norm_g", "mla_k_norm_g", "mem_q_norm_g", "mem_k_norm_g",
                "moe_expert_bias", "attn_q_norm_w_2", "attn_k_norm_w_2", "ssd_D_2", "ssd_dt_bias_2", "ssd_A_log_2"]
        GAIN, at = {}, 0
        for name in MISC:
            n = int(np.prod(A[name].shape))
            GAIN[name] = (at, at + n)
            at += n
        gains = sb("gains", [P, at])

        def gain(name):
            a, b = GAIN[name]
            return gains[:, a:b]

        with ExitStack() as scope:
            vrows = sb("vrows", [P, 3, P], scope=scope)
            pos_i = sb("pos_i", [P, NT], I32, scope)
            pos_f = sb("pos_f", [P, NT], scope=scope)
            ang = sb("ang", [P, NT, 48], scope=scope)
            turns = sb("turns", [P, NT, 48], scope=scope)
            half_sin = sb("half_sin", [P, NT, 48], scope=scope)
            block = scope.enter_context(nc.Block())

            @block.sync
            def _(sp):
                sp.dma_start(X[:, :, :], A["x"].rearrange("b (t p) d -> p (b t) d", p=P)).then_inc(ld["x"], 16)
                sp.dma_start(consts[:, :], A["consts"]).then_inc(ld["consts"], 16)
                sp.dma_start(pos_i[:, :], A["positions"].rearrange("b (t p) -> p (b t)", p=P),
                             allow_slow_non_contiguous=True).then_inc(ld["pos"], 16)
                load_weights(sp, 2)
                sp.wait_ge(vrow_zeroed, 1)
                for tile, row, name, n in VECTORS:
                    src = flat(name).rearrange("(r c) -> r c", c=P)
                    if name == "ssd_conv_w_2" and tile == 2:
                        src = src[P:, :]
                    sp.dma_start(vrows[row:row + n, tile, :], src[0:n, :]).then_inc(ld["vec"], 16)
                for name in MISC:
                    a, b = GAIN[name]
                    sp.dma_start(gains[:, a:b], flat(name).partition_broadcast(P)).then_inc(ld["misc"], 16)
                load_weights(sp)
                sp.wait_ge(ld["misc"], 16 * len(MISC))
                sp.wait_ge(ld["x"], 16)

            @block.gpsimd
            def _(pool):
                pool.memset(minus_half[:, :], -0.5)

            @block.tensor
            def _(pe):
                pe.wait_ge(ld["consts"], 16)
                pe.wait_ge(ld["vec"], 16 * len(VECTORS))
                b = banks.open("vec", DVE)
                for t in range(3):
                    ins = pe.transpose(b.ap[:, t * P:(t + 1) * P], vrows[:, t, :], ident)
                ins.then_inc(bank_full, 1)

            @block.vector
            def _(dve):
                link = chain(dve, dve_step)
                dve.memset(vrows[:, :, :], 0.0).then_inc(vrow_zeroed, 1)
                dve.wait_ge(ld["pos"], 16)
                dve.wait_ge(ld["consts"], 16)
                link(dve.tensor_copy(pos_f[:, :], pos_i[:, :]))
                for t in range(NT):
                    i = dve.tensor_scalar(ang[:, t, :], const("inv_freq"), pos_f[:, t:t + 1], None, ALU.mult)
                link(i)
                link(dve.tensor_scalar(turns[:, :, :], ang[:, :, :], float(1 / (2 * np.pi)), 12582912.0,
                                       ALU.mult, ALU.add))
                link(dve.tensor_scalar(turns[:, :, :], turns[:, :, :], 12582912.0, None, ALU.subtract))
                rest = 2 * np.pi
                for bits in (6.28125, None, None):
                    part = bits if bits else float(np.float32(rest))
                    if bits is None and rest > 1e-4:
                        part = float(np.float32(np.round(rest * 2**20) / 2**20))
                    link(dve.scalar_tensor_tensor(ang[:, :, :], turns[:, :, :], -part, ang[:, :, :],
                                                  ALU.mult, ALU.add))
                    rest -= part
                link(dve.tensor_scalar(ang[:, :, :], ang[:, :, :], 3.1415925, -3.1415925, ALU.min, ALU.max))
                link(dve.tensor_scalar(turns[:, :, :], ang[:, :, :], 0.5, None, ALU.mult))
                dve.tensor_copy(cs[:, 1, :, :], ang[:, :, :]).then_inc(trig_ready, 1)
                b = banks["vec"]
                dve.wait_ge(bank_full, b.full)
                dve.tensor_copy(vcols[:, :], b.ap[:, 0:3 * P]).then_inc(emptied[b.by], 1)
                dve.wait_ge(trig_ready, 3)
                link(dve.tensor_tensor(half_sin[:, :, :], half_sin[:, :, :], half_sin[:, :, :], ALU.mult))
                dve.tensor_scalar(cs[:, 0, :, :], half_sin[:, :, :], -2.0, 1.0, ALU.mult, ALU.add).then_inc(trig_ready, 1)

            @block.scalar
            def _(act):
                act.wait_ge(trig_ready, 1)
                act.activation(cs[:, 1, :, :], ang[:, :, :], ACT.Sin).then_inc(trig_ready, 1)
                act.activation(half_sin[:, :, :], turns[:, :, :], ACT.Sin).then_inc(trig_ready, 1)

        def cos(rope):
            return cs[:, 0, :, 0:32] if rope == 32 else cs[:, 0, :, 32:48]

        def sin(rope):
            return cs[:, 1, :, 0:32] if rope == 32 else cs[:, 1, :, 32:48]

        normed, squared, rooted = sem("normed"), sem("squared"), sem("rooted")
        heads_summed, heads_rooted = sem("heads_summed"), sem("heads_rooted")
        counted = {"streams": 0, "norms": 0, "head_norms": 0}

        class NormT:

            def __init__(self, tag, srcs, xn, hT, gain_col, bias_col=None):
                self.tag, self.srcs, self.xn, self.hT = tag, srcs, xn, hT
                self.gain_col, self.bias_col = gain_col, bias_col
                self.T = len(srcs)
                self.before, self.nth = counted["streams"], counted["norms"] + 1
                counted["streams"] += self.T
                counted["norms"] += 1

            def scalar_squares(self, act):
                for t, src in enumerate(self.srcs):
                    act.activation(self.xn[:, t, :], src, ACT.Square,
                                   accum_out=eps_rows[:, t:t + 1]).then_inc(squared, 1)

            def pool(self, pool):
                pool.wait_ge(squared, self.before + self.T)
                root(pool, 0, self.T, D, rooted)

            def vector_scale(self, dve):
                dve.wait_ge(rooted, self.nth)
                for t, src in enumerate(self.srcs):
                    dve.tensor_scalar(self.xn[:, t, :], src, rstd[:, t:t + 1], float(D) ** 0.5,
                                      ALU.mult, ALU.mult).then_inc(normed, 1)

            def per_bank(self):
                return 4 // self.T

            def tensor(self, pe):
                pe.wait_ge(normed, self.before + self.T)
                m = self.per_bank()
                for n in range(KD // m):
                    b = banks.open((self.tag, n), (DVE, ACTE)[n % 2])
                    if b.emptied:
                        pe.wait_ge(*b.emptied)
                    for j in range(m):
                        for t in range(self.T):
                            k = n * m + j
                            i = pe.transpose(b.ap[:, (j * self.T + t) * P:(j * self.T + t + 1) * P],
                                             self.xn[:, t, k * P:(k + 1) * P], ident)
                    i.then_inc(bank_full, 1)

            def evacuate(self, eng, by):
                m = self.per_bank()
                W = self.T * P
                for n in range(KD // m):
                    b = banks[self.tag, n]
                    if b.by != by:
                        continue
                    eng.wait_ge(bank_full, b.full)
                    for j in range(m):
                        k = n * m + j
                        src = b.ap[:, j * W:(j + 1) * W]
                        segs = self.gain_col(k)
                        for a, z, g, bias in segs:
                            if by == DVE:
                                if bias is None:
                                    i = eng.tensor_scalar(self.hT[:, k, a:z], src[:, a:z], g, None, ALU.mult)
                                else:
                                    i = eng.tensor_scalar(self.hT[:, k, a:z], src[:, a:z], g, bias, ALU.mult, ALU.add)
                            else:
                                i = eng.activation(self.hT[:, k, a:z], src[:, a:z], ACT.Identity, scale=g,
                                                   **({} if bias is None else {"bias": bias}))
                    i.then_inc(emptied[by], 1)

            def wait_chunk(self, pe, k):
                b = banks[self.tag, k // self.per_bank()]
                pe.wait_ge(emptied[b.by], b.done)

        def plain_gain(name, first=0, W=S):
            c = VCOL[name] + first
            return lambda k: [(0, W, vcols[:, c + k:c + k + 1], None)]

        class Transpose:

            def __init__(self, tag, src, n, width, dst, gain=None, by=(DVE, ACTE), tiles=NT):
                self.tag, self.src, self.n, self.width, self.dst, self.gain, self.by = tag, src, n, width, dst, gain, by
                self.T = tiles
                self.per = 4 // tiles

            def groups(self):
                return [(g, range(g, min(g + self.per, self.n))) for g in range(0, self.n, self.per)]

            def tensor(self, pe):
                for q, (g, blocks) in enumerate(self.groups()):
                    b = banks.open((self.tag, g), self.by[q % len(self.by)])
                    if b.emptied:
                        pe.wait_ge(*b.emptied)
                    for j, n in enumerate(blocks):
                        for t in range(self.T):
                            i = pe.transpose(b.ap[0:self.width, (j * self.T + t) * P:(j * self.T + t + 1) * P],
                                             self.src(n, t), ident)
                    i.then_inc(bank_full, 1)

            def evacuate(self, eng, by):
                W = self.T * P
                for g, blocks in self.groups():
                    b = banks[self.tag, g]
                    if b.by != by:
                        continue
                    eng.wait_ge(bank_full, b.full)
                    m = len(blocks)
                    if self.gain is None:
                        src = b.ap[0:self.width, 0:m * W].rearrange("p (m w) -> p m w", m=m)
                        if by == DVE:
                            i = eng.tensor_copy(self.dst(g, m), src)
                        else:
                            i = eng.activation(self.dst(g, m), src, ACT.Copy)
                    else:
                        for j, n in enumerate(blocks):
                            src = b.ap[0:self.width, j * W:(j + 1) * W].rearrange("p (m w) -> p m w", m=1)
                            if by == DVE:
                                i = eng.tensor_scalar(self.dst(n, 1), src, self.gain(n), None, ALU.mult)
                            else:
                                i = eng.activation(self.dst(n, 1), src, ACT.Identity, scale=self.gain(n))
                    i.then_inc(emptied[by], 1)

            def wait_all(self, pe):
                for g, _ in self.groups()[-len(self.by):]:
                    b = banks[self.tag, g]
                    pe.wait_ge(emptied[b.by], b.done)

        def gemm(pe, tag, lhsT, K, T, rhs, width, by, wait_k=None, first=None, last=None):
            b = banks.open(tag, by)
            if b.emptied:
                pe.wait_ge(*b.emptied)
            for k in range(K):
                i = pe.matmul(b.ap[:, 0:width], lhsT(k), rhs(k), start=(k == 0), stop=(k == K - 1))
            i.then_inc(bank_full, 1)
            return b, i

        def copy_out(eng, by, tag, dst, width):
            b = banks[tag]
            if b.by != by:
                return
            eng.wait_ge(bank_full, b.full)
            if by == DVE:
                i = eng.tensor_copy(dst, b.ap[:, 0:width])
            else:
                i = eng.activation(dst, b.ap[:, 0:width], ACT.Copy)
            i.then_inc(emptied[by], 1)

        def rope(dve, link, dst, src, tmp, H, half, width, off, c, s):
            for t in range(NT):
                x1 = src[:, t, :, off:off + half]
                x2 = src[:, t, :, off + half:off + 2 * half]
                y1 = dst[:, t, :, off:off + half]
                y2 = dst[:, t, :, off + half:off + 2 * half]
                cb = c[:, t, :].unsqueeze(1).broadcast_to([P, H, half])
                sbb = s[:, t, :].unsqueeze(1).broadcast_to([P, H, half])
                dve.tensor_tensor(tmp[:, 0, 0:H, 0:half], x1, sbb, ALU.mult)
                dve.tensor_tensor(tmp[:, 1, 0:H, 0:half], x2, sbb, ALU.mult)
                dve.tensor_tensor(y1, x1, cb, ALU.mult)
                link(dve.tensor_tensor(y2, x2, cb, ALU.mult))
                dve.tensor_tensor(y1, y1, tmp[:, 1, 0:H, 0:half], ALU.subtract)
                link(dve.tensor_tensor(y2, y2, tmp[:, 0, 0:H, 0:half], ALU.add))

        class HeadNorm:

            def __init__(self, tag):
                counted["head_norms"] += 1
                self.nth = counted["head_norms"]

            def vector_sum(self, dve, link, src, sq, H, width, T=NT):
                n = T * H
                link(dve.tensor_tensor(sq, src, src, ALU.mult))
                dve.tensor_reduce(eps_rows[:, 0:n], sq, AX.X, ALU.add).then_inc(heads_summed, 1)

            def pool(self, pool, H, width, T=NT):
                n = T * H
                pool.wait_ge(heads_summed, self.nth)
                root(pool, 0, n, width, heads_rooted)

            def vector_scale(self, dve, link, dst, src, gains_of, H, width, T=NT):
                dve.wait_ge(heads_rooted, self.nth)
                n = T * H
                link(dve.tensor_scalar(rstd[:, 0:n], rstd[:, 0:n], float(width) ** 0.5, None, ALU.mult))
                for t in range(T):
                    r = rstd[:, t * H:(t + 1) * H].unsqueeze(2).broadcast_to([P, H, width])
                    i = dve.tensor_tensor(dst[:, t, :, :], src[:, t, :, :], r, ALU.mult)
                link(i)
                for t in range(T):
                    for a, z, g in gains_of:
                        gb = g.unsqueeze(1).broadcast_to([P, z - a, width])
                        i = dve.tensor_tensor(dst[:, t, a:z, :], dst[:, t, a:z, :], gb, ALU.mult)
                link(i)

        class Attention:
            RING, LAG = 4, 3

            def __init__(self, tag, heads, qT, kT, v, keys, scale, outT, bufs, bias=None):
                self.tag, self.heads, self.qT, self.kT, self.v, self.keys = tag, heads, qT, kT, v, keys
                self.scale, self.outT, self.bias = scale, outT, bias
                self.KT = keys // P
                self.hp = 512 // keys
                self.items = [(t, h) for h in range(0, heads, self.hp) for t in range(NT)]
                self.per_pair = 2 * NT // self.hp
                self.probs, self.pT, self.negmax, self.sums = bufs
                self.max_ready, self.scaled = sem("max_ready_" + tag), sem("scaled_" + tag)
                self.exped = sem("exped_" + tag) if bias is not None else None

            def wait_exped(self, eng, n):
                if self.bias is None:
                    eng.wait_ge(emptied[ACTE], banks[self.tag, "qk", n].done)
                else:
                    eng.wait_ge(self.exped, n + 1)

            def wait_transposed(self, eng, n):
                eng.wait_ge(bank_full, banks[self.tag, "pT", n].full)

            def pair_done(self, m):
                return m // self.per_pair if m >= 0 and m % self.per_pair == self.per_pair - 1 else None

            def tensor(self, pe):
                N, LAG = len(self.items), self.LAG
                for i in range(N + LAG + 1):
                    if i < N:
                        t, h = self.items[i]
                        b = banks.open((self.tag, "qk", i), ACTE if self.bias is None else DVE)
                        if b.emptied:
                            pe.wait_ge(*b.emptied)
                        for j in range(self.hp):
                            ins = pe.matmul(b.ap[:, j * self.keys:(j + 1) * self.keys],
                                            self.qT(h + j)[:, t * P:(t + 1) * P], self.kT(h + j),
                                            start=True, stop=True)
                        ins.then_inc(bank_full, 1)
                    n = i - LAG
                    if 0 <= n < N:
                        b = banks.open((self.tag, "pT", n), ACTE)
                        if b.emptied:
                            pe.wait_ge(*b.emptied)
                        pe.wait_ge(self.scaled, n + 1)
                        for c in range(0, 512, P):
                            ins = pe.transpose(b.ap[:, c:c + P], self.probs[:, n % self.RING, c:c + P], ident)
                        ins.then_inc(bank_full, 1)
                    p = self.pair_done(n - 1)
                    if p is not None:
                        o = banks.open((self.tag, "pv", p), DVE)
                        if o.emptied:
                            pe.wait_ge(*o.emptied)
                        pe.wait_ge(emptied[ACTE], banks[self.tag, "pT", n - 1].done)
                        for kt in range(self.KT):
                            for j in range(2):
                                c = (j * self.KT + kt) * S
                                ins = pe.matmul(o.ap[64 * j:64 * j + 64, 0:S], self.v(2 * p + j, kt),
                                                self.pT[p % 2][:, c:c + S], start=(kt == 0), stop=(kt == self.KT - 1),
                                                tile_position=(0, 64 * j), skip_group_check=True)
                        ins.then_inc(bank_full, 1)

            def vector(self, dve, link):
                N, LAG = len(self.items), self.LAG
                hp, K = self.hp, self.keys
                for i in range(N + LAG + 1):
                    if i < N:
                        t, h = self.items[i]
                        b = banks[self.tag, "qk", i]
                        dve.wait_ge(bank_full, b.full)
                        L = b.ap[:, 0:hp * K].rearrange("p (h k) -> p h k", h=hp)
                        mx = self.negmax[:, i * hp:(i + 1) * hp]
                        if self.bias is None:
                            link(dve.tensor_reduce(mx, L, AX.X, ALU.max))
                            dve.tensor_scalar(mx, mx, -self.scale, None, ALU.mult).then_inc(self.max_ready, 1)
                        else:
                            if i >= self.RING:
                                self.wait_transposed(dve, i - self.RING)
                            B = self.probs[:, i % self.RING, :].rearrange("p (h k) -> p h k", h=hp)
                            bb = self.bias(t).unsqueeze(1).broadcast_to([P, hp, K])
                            dve.scalar_tensor_tensor(B, L, self.scale, bb, ALU.mult, ALU.add).then_inc(emptied[DVE], 1)
                            dve.wait_ge(emptied[DVE], b.done)
                            dve.tensor_reduce(mx, B, AX.X, ALU.max, negate=True).then_inc(self.max_ready, 1)
                    n = i - 1
                    if 0 <= n < N:
                        self.wait_exped(dve, n)
                        s = self.sums[:, n * hp:(n + 1) * hp]
                        link(dve.reciprocal(s, s))
                        for j in range(hp):
                            B = self.probs[:, n % self.RING, j * K:(j + 1) * K]
                            ins = dve.tensor_scalar(B, B, s[:, j:j + 1], None, ALU.mult)
                        ins.then_inc(self.scaled, 1)
                    p = self.pair_done(i - LAG - 1)
                    if p is not None:
                        o = banks[self.tag, "pv", p]
                        dve.wait_ge(bank_full, o.full)
                        dve.tensor_copy(self.outT(p), o.ap[:, 0:S]).then_inc(emptied[DVE], 1)

            def scalar(self, act):
                N = len(self.items)
                hp, K = self.hp, self.keys
                for i in range(N + self.LAG):
                    if i < N:
                        b = banks[self.tag, "qk", i]
                        act.wait_ge(self.max_ready, i + 1)
                        if self.bias is None and i >= self.RING:
                            self.wait_transposed(act, i - self.RING)
                        for j in range(hp):
                            c = i * hp + j
                            B = self.probs[:, i % self.RING, j * K:(j + 1) * K]
                            if self.bias is None:
                                ins = act.activation(B, b.ap[:, j * K:(j + 1) * K], ACT.Exp, scale=self.scale,
                                                     bias=self.negmax[:, c:c + 1], accum_out=self.sums[:, c:c + 1])
                                if j == hp - 1:
                                    ins.then_inc(emptied[ACTE], 1)
                            else:
                                ins = act.activation(B, B, ACT.Exp, bias=self.negmax[:, c:c + 1],
                                                     accum_out=self.sums[:, c:c + 1])
                                if j == hp - 1:
                                    ins.then_inc(self.exped, 1)
                    n = i - self.LAG
                    if n >= 0:
                        t, h = self.items[n]
                        p = n // self.per_pair
                        b = banks[self.tag, "pT", n]
                        act.wait_ge(bank_full, b.full)
                        if p >= 2:
                            act.wait_ge(bank_full, banks[self.tag, "pv", p - 2].full)
                        j = h % 2
                        dst = self.pT[p % 2].rearrange("p (c q) -> p c q", q=S)[:, j * self.KT:(j + hp) * self.KT, t * P:(t + 1) * P]
                        act.activation(dst, b.ap[:, :].rearrange("p (c q) -> p c q", q=P), ACT.Copy).then_inc(emptied[ACTE], 1)

        hT = sb("hT", [P, KD, 2 * S])
        mix = ExitStack()
        proj = sb("proj", [P, NT, N_IN], scope=mix)
        with ExitStack() as scope:
            xn = sb("xn", [P, NT, D], scope=scope)
            norm = NormT("n1", [X[:, t, :] for t in range(NT)], xn, hT, plain_gain("attn_norm_g"))
            block = scope.enter_context(nc.Block())

            @block.tensor
            def _(pe):
                norm.tensor(pe)
                for n in range(8):
                    piece = ring["in", n]
                    pe.wait_ge(piece.sem, piece.full)
                    wv = view(piece, 0, KD, CI)
                    for t in range(NT):
                        b = banks.open(("proj", n, t), (DVE, ACTE)[t])
                        if b.emptied:
                            pe.wait_ge(*b.emptied)
                        for k in range(KD):
                            if n == 0 and t == 0:
                                norm.wait_chunk(pe, k)
                            i = pe.matmul(b.ap[:, 0:CI], hT[:, k, t * P:(t + 1) * P], wv[:, k, :],
                                          start=(k == 0), stop=(k == KD - 1))
                        i.then_inc(bank_full, 1)
                    piece.freed = (bank_full, b.full)

            @block.sync
            def _(sp):
                for l in range(2):
                    sp.dma_start(routers[:, l], A["moe_router_w_2"][l].rearrange("(k p) n -> p k n", p=P)).then_inc(routers_loaded, 16)
                load_weights(sp)

            @block.gpsimd
            def _(pool):
                norm.pool(pool)

            @block.vector
            def _(dve):
                norm.vector_scale(dve)
                norm.evacuate(dve, DVE)
                for n in range(8):
                    copy_out(dve, DVE, ("proj", n, 0), proj[:, 0, n * CI:(n + 1) * CI], CI)

            @block.scalar
            def _(act):
                norm.scalar_squares(act)
                norm.evacuate(act, ACTE)
                for n in range(8):
                    copy_out(act, ACTE, ("proj", n, 1), proj[:, 1, n * CI:(n + 1) * CI], CI)

        def heads(buf, off, H, width):
            return buf[:, :, off:off + H * width].rearrange("p t (h d) -> p t h d", d=width)

        spare = C[:, :, :].rearrange("p t d -> p (t d)")
        probs = spare.rearrange("p (n k) -> p n k", n=4)
        negmax, sums = sb("negmax", [P, 32], scope=mix), sb("sums", [P, 32], scope=mix)
        outA = sb("outA", [P, 4, S], scope=mix)
        outB = sb("outB", [P, 4, S], scope=mix)
        attn_bias = sb("attn_bias", [P, NT, S], scope=mix)
        causal = const("causal").rearrange("p (t k) -> p t k", t=NT)

        with ExitStack() as scope:
            qk = heads(proj, 0, 9, 64)
            ix = heads(proj, O_IQ, 9, 64)
            sq = sb("sq", [P, NT * 9, 64], scope=scope)
            tmp = sb("tmp", [P, 2, 9, 32], scope=scope)
            qkT = hT[0:64, :, :].rearrange("p k n -> p (k n)")[:, 0:9 * S].rearrange("p (h s) -> p h s", h=9)
            ixT = sb("ixT", [64, 9, S], scope=scope)
            pT = sb("pT", [P, 2, 1024], scope=scope)
            rel = sb("rel", [P, 2, 512], scope=scope)
            score = hT[:, :, :].rearrange("p k n -> p (k n)")[:, 9 * S:11 * S].rearrange("p (t k) -> p t k", t=NT)
            top8 = sb("top8", [P, NT, 8], scope=scope)
            bias = attn_bias
            hnorm = HeadNorm("dsa")
            qk_ready, ix_ready = sem("qk_ready"), sem("ix_ready")
            scored = sem("scored")
            to_qkT = Transpose("qkT", lambda n, t: qk[:, t, n, :], 9, 64, lambda g, m: qkT[:, g:g + m, :])
            to_ixT = Transpose("ixT", lambda n, t: ix[:, t, n, :], 9, 64, lambda g, m: ixT[:, g:g + m, :])
            att = Attention("dsa", DSA_H, lambda h: qkT[:, h, :], lambda h: qkT[:, 8, :],
                            lambda h, kt: proj[:, kt, 576:640], S, HD ** -0.5, lambda p: outA[:, p, :], (probs, (pT[:, 0, :], pT[:, 1, :]), negmax, sums),
                            bias=lambda t: bias[:, t, :])
            pairs = [(t, h) for t in range(NT) for h in range(0, DSA_H, 2)]
            block = scope.enter_context(nc.Block())

            @block.tensor
            def _(pe):
                pe.wait_ge(ix_ready, 1)
                to_ixT.tensor(pe)
                to_ixT.wait_all(pe)
                for t, h in pairs:
                    b = banks.open(("rel", t, h), ACTE)
                    if b.emptied:
                        pe.wait_ge(*b.emptied)
                    for j in range(2):
                        i = pe.matmul(b.ap[:, j * S:(j + 1) * S], ixT[:, h + j, t * P:(t + 1) * P], ixT[:, 8, :],
                                      start=True, stop=True)
                    i.then_inc(bank_full, 1)
                pe.wait_ge(qk_ready, 1)
                to_qkT.tensor(pe)
                to_qkT.wait_all(pe)
                att.tensor(pe)

            @block.gpsimd
            def _(pool):
                hnorm.pool(pool, 9, 64)

            @block.scalar
            def _(act):
                to_ixT.evacuate(act, ACTE)
                for n, (t, h) in enumerate(pairs):
                    b = banks["rel", t, h]
                    act.wait_ge(bank_full, b.full)
                    if n >= 2:
                        act.wait_ge(scored, n - 1)
                    act.activation(rel[:, n % 2, :], b.ap[:, :], ACT.Relu).then_inc(emptied[ACTE], 1)
                to_qkT.evacuate(act, ACTE)
                att.scalar(act)

            @block.vector
            def _(dve):
                link = chain(dve, dve_step)
                rope(dve, link, ix, ix, tmp, 9, 32, 64, 0, cos(32), sin(32))
                dve.sem_inc(ix_ready, 1)
                hnorm.vector_sum(dve, link, qk, sq[:, :, :], 9, 64)
                to_ixT.evacuate(dve, DVE)
                hnorm.vector_scale(dve, link, qk, qk, [(0, 8, gain("dsa_q_norm_g")), (8, 9, gain("dsa_k_norm_g"))], 9, 64)
                rope(dve, link, qk, qk, tmp, 9, 32, 64, 0, cos(32), sin(32))
                dve.sem_inc(qk_ready, 1)
                for n, (t, h) in enumerate(pairs):
                    b = banks["rel", t, h]
                    dve.wait_ge(emptied[ACTE], b.done)
                    for j in range(2):
                        w_h = proj[:, t, O_IW + h + j:O_IW + h + j + 1]
                        r = rel[:, n % 2, j * S:(j + 1) * S]
                        if h + j == 0:
                            link(dve.tensor_scalar(score[:, t, :], r, w_h, None, ALU.mult))
                        elif j == 0:
                            link(dve.scalar_tensor_tensor(score[:, t, :], r, w_h, score[:, t, :], ALU.mult, ALU.add))
                        else:
                            dve.scalar_tensor_tensor(score[:, t, :], r, w_h, score[:, t, :],
                                                     ALU.mult, ALU.add).then_inc(scored, 1)
                            dve.wait_ge(scored, n + 1)
                link(dve.tensor_scalar(score[:, :, :], score[:, :, :], float(64 ** -0.5 * 8 ** -0.5), None, ALU.mult))
                link(dve.tensor_tensor(score[:, :, :], score[:, :, :], causal, ALU.mult))
                link(dve.tensor_scalar(bias[:, :, :], causal, 1.0, -NEG, ALU.subtract, ALU.mult))
                link(dve.tensor_tensor(score[:, :, :], score[:, :, :], bias[:, :, :], ALU.add))
                for r in range(TOPK // 8):
                    for t in range(NT):
                        i = dve.max(top8[:, t, :], score[:, t, :])
                    link(i)
                    for t in range(NT):
                        i = dve.match_replace(score[:, t, :], top8[:, t, :], score[:, t, :], TAKEN)
                    link(i)
                link(dve.scalar_tensor_tensor(bias[:, :, :].rearrange("p t k -> p (t k)"),
                                              score[:, :, :].rearrange("p t k -> p (t k)"), TAKEN,
                                              const("causal"), ALU.is_equal, ALU.mult))
                link(dve.tensor_scalar(bias[:, :, :], bias[:, :, :], 1.0, BIG, ALU.subtract, ALU.mult))
                to_qkT.evacuate(dve, DVE)
                att.vector(dve, link)

            @block.sync
            def _(sp):
                load_weights(sp)

        with ExitStack() as scope:
            cn = sb("cn", [P, NT, 384], scope=scope)
            cT = sb("cT", [P, 3, S], scope=scope)
            mqk = sb("mqk", [P, NT, 16 * MLA_QK], scope=scope)
            kvb = sb("kvb", [P, NT, 1024], scope=scope)
            mqkT = hT[0:MLA_QK, :, :].rearrange("p k n -> p (k n)").rearrange("p (h s) -> p h s", h=16)
            msq = hT[:, :, :].rearrange("p k n -> p (k n)")[:, 0:NT * 16 * MLA_QK].rearrange("p (h d) -> p h d", d=MLA_QK)
            tmp = proj[:, 0, 0:512].rearrange("p (a h d) -> p a h d", a=2, h=16)
            cbias = attn_bias
            mh = mqk[:, :, :].rearrange("p t (h d) -> p t h d", d=MLA_QK)
            kvh = kvb[:, :, :].rearrange("p t (h d) -> p t h d", d=128)
            c_squared, c_rooted, c_normed, heads_ready = sem("c_squared"), sem("c_rooted"), sem("c_normed"), sem("heads_ready")
            hnorm = HeadNorm("mla")
            cgain = lambda n: vcols[:, VCOL["mla_cq_norm_g"] + n:VCOL["mla_cq_norm_g"] + n + 1]
            to_cT = Transpose("cT", lambda n, t: cn[:, t, n * P:(n + 1) * P], 3, P, lambda g, m: cT[:, g:g + m, :], gain=cgain)
            to_T = Transpose("mqkT", lambda n, t: mh[:, t, n, :], 16, MLA_QK, lambda g, m: mqkT[:, g:g + m, :])
            att = Attention("mla", MLA_H, lambda h: mqkT[:, h, :], lambda h: mqkT[:, 8 + h, :],
                            lambda h, kt: kvb[:, kt, h * 128 + 64:h * 128 + 128], S, MLA_QK ** -0.5, lambda p: outB[:, p, :],
                            (probs, (proj[:, 0, 0:1024], proj[:, 1, 0:1024]), negmax, sums),
                            bias=lambda t: cbias[:, t, :])
            block = scope.enter_context(nc.Block())

            @block.tensor
            def _(pe):
                pe.wait_ge(c_normed, 1)
                to_cT.tensor(pe)
                to_cT.wait_all(pe)
                piece = ring["mla"]
                pe.wait_ge(piece.sem, piece.full)
                uq, ukv = view(piece, 0, 2, 768), view(piece, 1536, 1, 1024)
                for t in range(NT):
                    tt = slice(t * P, (t + 1) * P)
                    for n in range(2):
                        b, _ = gemm(pe, ("uq", t, n), lambda k: cT[:, k, tt], 2, t,
                                    lambda k: uq[:, k, n * 384:(n + 1) * 384], 384, ACTE)
                    for n in range(2):
                        b, _ = gemm(pe, ("ukv", t, n), lambda k: cT[:, 2, tt], 1, t,
                                    lambda k: ukv[:, 0, n * 512:(n + 1) * 512], 512, DVE)
                piece.freed = (bank_full, b.full)
                pe.wait_ge(heads_ready, 1)
                to_T.tensor(pe)
                to_T.wait_all(pe)
                att.tensor(pe)

            @block.gpsimd
            def _(pool):
                pool.wait_ge(c_squared, 4)
                root(pool, 0, 2, MLA_QR)
                root(pool, 2, 2, MLA_KVR, c_rooted)
                hnorm.pool(pool, 16, MLA_QK)

            @block.scalar
            def _(act):
                for t in range(NT):
                    act.activation(cn[:, t, 0:256], proj[:, t, O_CQ:O_CKV], ACT.Square,
                                   accum_out=eps_rows[:, t:t + 1]).then_inc(c_squared, 1)
                    act.activation(cn[:, t, 256:384], proj[:, t, O_CKV:O_KPE], ACT.Square,
                                   accum_out=eps_rows[:, 2 + t:3 + t]).then_inc(c_squared, 1)
                to_cT.evacuate(act, ACTE)
                for t in range(NT):
                    for n in range(2):
                        copy_out(act, ACTE, ("uq", t, n), mqk[:, t, n * 384:(n + 1) * 384], 384)
                to_T.evacuate(act, ACTE)
                att.scalar(act)

            @block.vector
            def _(dve):
                link = chain(dve, dve_step)
                link(dve.tensor_scalar(cbias[:, :, :], causal, 1.0, BIG, ALU.subtract, ALU.mult))
                dve.wait_ge(c_rooted, 1)
                for t in range(NT):
                    dve.tensor_scalar(cn[:, t, 0:256], proj[:, t, O_CQ:O_CKV], rstd[:, t:t + 1],
                                      MLA_QR ** 0.5, ALU.mult, ALU.mult)
                    i = dve.tensor_scalar(cn[:, t, 256:384], proj[:, t, O_CKV:O_KPE], rstd[:, 2 + t:3 + t],
                                          float(MLA_KVR) ** 0.5, ALU.mult, ALU.mult)
                i.then_inc(c_normed, 1)
                to_cT.evacuate(dve, DVE)
                for t in range(NT):
                    for n in range(2):
                        copy_out(dve, DVE, ("ukv", t, n), kvb[:, t, n * 512:(n + 1) * 512], 512)
                b = banks["ukv", NT - 1, 1]
                dve.wait_ge(emptied[DVE], b.done)
                for t in range(NT):
                    dve.tensor_copy(mh[:, t, 8:16, 0:64], kvh[:, t, :, 0:64])
                    i = dve.tensor_copy(mh[:, t, 8:16, 64:96],
                                        proj[:, t, O_KPE:O_GD].unsqueeze(1).broadcast_to([P, 8, 32]))
                link(i)
                b = banks["uq", NT - 1, 1]
                dve.wait_ge(emptied[ACTE], b.done)
                hnorm.vector_sum(dve, link, mh, msq, 16, MLA_QK)
                hnorm.vector_scale(dve, link, mh, mh, [(0, 8, gain("mla_q_norm_g")), (8, 16, gain("mla_k_norm_g"))], 16, MLA_QK)
                rope(dve, link, mh, mh, tmp, 16, 16, MLA_QK, 64, cos(16), sin(16))
                dve.sem_inc(heads_ready, 1)
                to_T.evacuate(dve, DVE)
                att.vector(dve, link)

            @block.sync
            def _(sp):
                load_weights(sp)

        with ExitStack() as scope:
            mT = hT[:, :, S:2 * S]
            merged = sb("merged", [P, NT, D], scope=scope)
            part = sb("part", [P, 2, 512], scope=scope)
            gates_ready, merged_ready = sem("gates_ready"), sem("merged_ready")
            both = (outA, outB)
            to_mT = Transpose("mT", lambda n, t: merged[:, t, n * P:(n + 1) * P], 8, P, lambda g, m: mT[:, g:g + m, :])
            block = scope.enter_context(nc.Block())

            @block.tensor
            def _(pe):
                pa, pb = ring["br_dsa"], ring["br_mla"]
                pe.wait_ge(pa.sem, pa.full)
                pe.wait_ge(pb.sem, pb.full)
                for t in range(NT):
                    for n in range(2):
                        for m, piece in enumerate((pa, pb)):
                            wv = view(piece, 0, 4, D)
                            b, _ = gemm(pe, ("br", t, n, m), lambda k: both[m][:, k, t * P:(t + 1) * P], 4, t,
                                        lambda k: wv[:, k, n * 512:(n + 1) * 512], 512, DVE)
                            piece.freed = (bank_full, b.full)
                pe.wait_ge(merged_ready, 4)
                to_mT.tensor(pe)
                to_mT.wait_all(pe)
                w0, w1 = ring["w_out", 0], ring["w_out", 1]
                pe.wait_ge(w0.sem, w0.full)
                pe.wait_ge(w1.sem, w1.full)
                wv = (view(w0, 0, 4, D), view(w1, 0, 4, D))
                for t in range(NT):
                    for n in range(2):
                        b, _ = gemm(pe, ("mixed", t, n), lambda k: mT[:, k, t * P:(t + 1) * P], 8, t,
                                    lambda k: wv[k // 4][:, k % 4, n * 512:(n + 1) * 512], 512, DVE)
                w0.freed = w1.freed = (bank_full, b.full)

            @block.scalar
            def _(act):
                act.activation(proj[:, :, O_GD:N_IN], proj[:, :, O_GD:N_IN], ACT.Sigmoid).then_inc(gates_ready, 1)
                to_mT.evacuate(act, ACTE)

            @block.vector
            def _(dve):
                link = chain(dve, dve_step)
                dve.wait_ge(gates_ready, 1)
                for t in range(NT):
                    for n in range(2):
                        c = slice(n * 512, (n + 1) * 512)
                        b = banks["br", t, n, 0]
                        dve.wait_ge(bank_full, b.full)
                        dve.tensor_tensor(merged[:, t, c], b.ap[:, :], proj[:, t, O_GD + n * 512:O_GD + (n + 1) * 512],
                                          ALU.mult).then_inc(emptied[DVE], 1)
                        b = banks["br", t, n, 1]
                        dve.wait_ge(bank_full, b.full)
                        dve.tensor_tensor(part[:, n, :], b.ap[:, :], proj[:, t, O_GM + n * 512:O_GM + (n + 1) * 512],
                                          ALU.mult).then_inc(emptied[DVE], 1)
                        dve.wait_ge(emptied[DVE], b.done)
                        dve.tensor_tensor(merged[:, t, c], merged[:, t, c], part[:, n, :], ALU.add).then_inc(merged_ready, 1)
                to_mT.evacuate(dve, DVE)
                for t in range(NT):
                    for n in range(2):
                        c = slice(n * 512, (n + 1) * 512)
                        b = banks["mixed", t, n]
                        dve.wait_ge(bank_full, b.full)
                        dve.tensor_tensor(X[:, t, c], X[:, t, c], b.ap[:, :], ALU.add).then_inc(emptied[DVE], 1)

            @block.sync
            def _(sp):
                load_weights(sp)
        mix.close()

        with ExitStack() as scope:
            M = sb("M", [P, NT, D], scope=scope)
            xn = sb("xn2", [P, 4, D], scope=scope)
            cq = sb("cqk", [P, NT, 8 * 64], scope=scope)
            cv = sb("cv", [P, NT, 256], scope=scope)
            csq = sb("csq", [P, NT * 8, 64], scope=scope)
            cqT = sb("cqT", [64, 8, S], scope=scope)
            coT = sb("coT", [P, 2, S], scope=scope)
            pT2 = sb("pT2", [P, 2, 1024], scope=scope)
            bufs = (sb("probs2", [P, 4, 512], scope=scope), (pT2[:, 0, :], pT2[:, 1, :]),
                    sb("negmax2", [P, 32], scope=scope), sb("sums2", [P, 32], scope=scope))
            mem_loaded = sem("mem_loaded")
            mheads_ready = sem("mheads_ready")
            gx, gm = VCOL["mem_x_norm_g"], VCOL["mem_norm_g"]
            norm = NormT("n2", [X[:, t, :] for t in range(NT)] + [M[:, t, :] for t in range(NT)], xn, hT,
                         lambda k: [(0, S, vcols[:, gx + k:gx + k + 1], None), (S, 2 * S, vcols[:, gm + k:gm + k + 1], None)])
            ch = cq[:, :, :].rearrange("p t (h d) -> p t h d", d=64)
            hnorm = HeadNorm("mem")
            to_T = Transpose("cqT", lambda n, t: ch[:, t, n, :], 8, 64, lambda g, m: cqT[:, g:g + m, :])
            att = Attention("mem", MEM_H, lambda h: cqT[:, h, :], lambda h: cqT[:, 4 + h, :],
                            lambda h, kt: cv[:, kt, h * 64:(h + 1) * 64], S, 64 ** -0.5, lambda p: coT[:, p, :], bufs)
            block = scope.enter_context(nc.Block())

            @block.tensor
            def _(pe):
                norm.tensor(pe)
                for k in range(KD):
                    norm.wait_chunk(pe, k)
                pq, pkv, po = ring["mem_q"], ring["mem_kv"], ring["mem_o"]
                pe.wait_ge(pq.sem, pq.full)
                wq, wkv, wo = view(pq, 0, KD, 256), view(pkv, 0, KD, 512), view(po, 0, 2, D)
                for t in range(NT):
                    b, _ = gemm(pe, ("mq", t), lambda k: hT[:, k, t * P:(t + 1) * P], KD, t, lambda k: wq[:, k, :], 256, ACTE)
                pq.freed = (bank_full, b.full)
                pe.wait_ge(pkv.sem, pkv.full)
                for t in range(NT):
                    b, _ = gemm(pe, ("mkv", t), lambda k: hT[:, k, S + t * P:S + (t + 1) * P], KD, t,
                                lambda k: wkv[:, k, :], 512, DVE)
                pkv.freed = (bank_full, b.full)
                pe.wait_ge(mheads_ready, 1)
                to_T.tensor(pe)
                to_T.wait_all(pe)
                att.tensor(pe)
                pe.wait_ge(emptied[DVE], banks["mem", "pv", MEM_H // 2 - 1].done)
                pe.wait_ge(po.sem, po.full)
                for t in range(NT):
                    for n in range(2):
                        b, _ = gemm(pe, ("memo", t, n), lambda k: coT[:, k, t * P:(t + 1) * P], 2, t,
                                    lambda k: wo[:, k, n * 512:(n + 1) * 512], 512, DVE)
                po.freed = (bank_full, b.full)

            @block.gpsimd
            def _(pool):
                norm.pool(pool)
                hnorm.pool(pool, 8, 64)

            @block.scalar
            def _(act):
                act.dma_start(M[:, :, :], A["mem"].rearrange("b (t p) d -> p (b t) d", p=P)).then_inc(mem_loaded, 16)
                act.wait_ge(mem_loaded, 16)
                norm.scalar_squares(act)
                norm.evacuate(act, ACTE)
                for t in range(NT):
                    copy_out(act, ACTE, ("mq", t), cq[:, t, 0:256], 256)
                to_T.evacuate(act, ACTE)
                att.scalar(act)

            @block.vector
            def _(dve):
                link = chain(dve, dve_step)
                norm.vector_scale(dve)
                norm.evacuate(dve, DVE)
                for t in range(NT):
                    b = banks["mkv", t]
                    dve.wait_ge(bank_full, b.full)
                    dve.tensor_copy(cq[:, t, 256:512], b.ap[:, 0:256])
                    dve.tensor_copy(cv[:, t, :], b.ap[:, 256:512]).then_inc(emptied[DVE], 1)
                b = banks["mkv", NT - 1]
                dve.wait_ge(emptied[DVE], b.done)
                dve.wait_ge(emptied[ACTE], banks["mq", NT - 1].done)
                hnorm.vector_sum(dve, link, ch, csq[:, :, :], 8, 64)
                hnorm.vector_scale(dve, link, ch, ch, [(0, 4, gain("mem_q_norm_g")), (4, 8, gain("mem_k_norm_g"))], 8, 64)
                dve.sem_inc(mheads_ready, 1)
                to_T.evacuate(dve, DVE)
                att.vector(dve, link)
                for t in range(NT):
                    for n in range(2):
                        c = slice(n * 512, (n + 1) * 512)
                        b = banks["memo", t, n]
                        dve.wait_ge(bank_full, b.full)
                        dve.tensor_tensor(X[:, t, c], X[:, t, c], b.ap[:, :], ALU.add).then_inc(emptied[DVE], 1)

            @block.sync
            def _(sp):
                load_weights(sp)


        with ExitStack() as scope:
            xn = sb("xn3", [P, NT, D], scope=scope)
            wr = sb("wr", [P, KD, 20], scope=scope)
            lg = sb("lg", [P, NT, 20], scope=scope)
            R = {k: sb("r_" + k, [P, NT, 16], scope=scope) for k in ("aff", "score", "w", "one", "both", "m", "d")}
            comb = sb("comb", [P, NT, 16], scope=scope)
            combT = sb("combT", [16, S], scope=scope)
            cb = sb("cb", [P, N_EXP, S], scope=scope)
            gated = sb("gated", [P, 2, 512], scope=scope)
            actT = sb("actT", [P, 2, 512], scope=scope)
            norm = NormT("n3", [X[:, t, :] for t in range(NT)], xn, hT, plain_gain("moe_norm_g"))
            to_combT = Transpose("combT", lambda n, t: comb[:, t, :], 1, 16, lambda g, m: combT[:, :].unsqueeze(1), by=(DVE,))
            wr_loaded, sub_ready, exp_ready, comb_ready = (sem(x) for x in ("wr_loaded", "sub_ready", "exp_ready", "comb_ready"))
            gu_full, silued, act_ready, down_done = (sem(x) for x in ("gu_full", "silued", "act_ready", "down_done"))
            gated_step = sem("gated_step")
            Y = [psum[i][:, :] for i in range(4)]
            GU = [[psum[4][:, :], psum[5][:, :]], [psum[6][:, :], psum[7][:, :]]]
            prep = scope.enter_context(ExitStack())
            block = prep.enter_context(nc.Block())

            @block.tensor
            def _(pe):
                norm.tensor(pe)
                pe.wait_ge(wr_loaded, 32)
                for t in range(NT):
                    b = banks.open(("router", t), DVE)
                    if b.emptied:
                        pe.wait_ge(*b.emptied)
                    for k in range(KD):
                        norm.wait_chunk(pe, k)
                        i = pe.matmul(b.ap[:, 0:20], hT[:, k, t * P:(t + 1) * P], wr[:, k, :], start=(k == 0), stop=(k == KD - 1))
                    i.then_inc(bank_full, 1)
                pe.wait_ge(comb_ready, 1)
                to_combT.tensor(pe)
                to_combT.wait_all(pe)
                for e in range(0, N_EXP, 2):
                    b = banks.open(("cb", e), (DVE, ACTE)[e // 2 % 2])
                    if b.emptied:
                        pe.wait_ge(*b.emptied)
                    for j in range(2):
                        i = pe.matmul(b.ap[:, j * S:(j + 1) * S], consts[0:16, e + j:e + j + 1].broadcast_to([16, P]),
                                      combT[:, :], start=True, stop=True)
                    i.then_inc(bank_full, 1)

            @block.gpsimd
            def _(pool):
                norm.pool(pool)

            @block.scalar
            def _(act):
                norm.scalar_squares(act)
                norm.evacuate(act, ACTE)
                act.wait_ge(sub_ready, 1)
                act.activation(R["m"][:, :, 0:4], R["m"][:, :, 0:4], ACT.Exp).then_inc(exp_ready, 1)
                act.activation(R["aff"][:, :, :], lg[:, :, 4:20], ACT.Sigmoid).then_inc(exp_ready, 1)
                for e in range(0, N_EXP, 2):
                    copy_out(act, ACTE, ("cb", e), cb[:, e:e + 2, :].rearrange("p e t -> p (e t)"), 512)

            @block.vector
            def _(dve):
                link = chain(dve, dve_step)
                norm.vector_scale(dve)
                norm.evacuate(dve, DVE)
                for t in range(NT):
                    copy_out(dve, DVE, ("router", t), lg[:, t, :], 20)
                dve.wait_ge(emptied[DVE], banks["router", NT - 1].done)
                v = {k: a[:, :, :] for k, a in R.items()}
                grp = v["m"][:, :, 0:4]
                top = v["d"][:, :, 0:1]

                def first_largest(dst, val, n):
                    link(dve.tensor_reduce(top, val, AX.X, ALU.max))
                    link(dve.tensor_tensor(dst, val, top.broadcast_to([P, NT, n]), ALU.is_equal))
                    down = const("down16")[:, 16 - n:16].unsqueeze(1).broadcast_to([P, NT, n])
                    link(dve.tensor_tensor(dst, dst, down, ALU.mult))
                    link(dve.tensor_reduce(v["d"][:, :, 1:2], dst, AX.X, ALU.max))
                    link(dve.tensor_tensor(dst, dst, v["d"][:, :, 1:2].broadcast_to([P, NT, n]), ALU.is_equal))

                link(dve.tensor_reduce(top, lg[:, :, 0:4], AX.X, ALU.max))
                link(dve.tensor_tensor(grp, lg[:, :, 0:4], top.broadcast_to([P, NT, 4]), ALU.subtract))
                dve.sem_inc(sub_ready, 1)
                dve.wait_ge(exp_ready, 2)
                link(dve.tensor_reduce(top, grp, AX.X, ALU.add))
                link(dve.reciprocal(top, top))
                link(dve.tensor_tensor(grp, grp, top.broadcast_to([P, NT, 4]), ALU.mult))
                pick = v["w"][:, :, 0:4]
                first_largest(pick, grp, 4)
                link(dve.tensor_copy(v["d"][:, :, 2:3], top))
                g16 = v["one"].rearrange("p t (g e) -> p t g e", g=4)
                link(dve.tensor_copy(g16, pick.unsqueeze(3).broadcast_to([P, NT, 4, 4])))
                bias16 = gain("moe_expert_bias").unsqueeze(1).broadcast_to([P, NT, 16])
                link(dve.tensor_tensor(v["score"], v["aff"], bias16, ALU.add))
                link(dve.tensor_tensor(v["score"], v["score"], v["one"], ALU.mult))
                link(dve.tensor_scalar(v["one"], v["one"], 1.0, BIG, ALU.subtract, ALU.mult))
                link(dve.tensor_tensor(v["score"], v["score"], v["one"], ALU.add))
                first_largest(v["both"], v["score"], 16)
                link(dve.tensor_scalar(v["one"], v["both"], -10 * BIG, None, ALU.mult))
                link(dve.tensor_tensor(v["score"], v["score"], v["one"], ALU.add))
                first_largest(v["w"], v["score"], 16)
                link(dve.tensor_tensor(v["both"], v["both"], v["w"], ALU.add))
                link(dve.tensor_tensor(v["aff"], v["aff"], v["both"], ALU.mult))
                link(dve.tensor_reduce(top, v["aff"], AX.X, ALU.add))
                link(dve.reciprocal(top, top))
                link(dve.tensor_tensor(top, top, v["d"][:, :, 2:3], ALU.mult))
                link(dve.tensor_tensor(comb[:, :, :], v["aff"], top.broadcast_to([P, NT, 16]), ALU.mult))
                dve.sem_inc(comb_ready, 1)
                to_combT.evacuate(dve, DVE)
                for e in range(0, N_EXP, 2):
                    copy_out(dve, DVE, ("cb", e), cb[:, e:e + 2, :].rearrange("p e t -> p (e t)"), 512)

            @block.sync
            def _(sp):
                for c, name, n in ((0, "moe_w_group", 4), (4, "moe_w_expert", 16)):
                    sp.dma_start(wr[:, :, c:c + n], A[name].rearrange("a (k p) n -> p (a k) n", p=P),
                                 allow_slow_non_contiguous=True).then_inc(wr_loaded, 16)
                load_weights(sp)
            prep.close()

            block = scope.enter_context(nc.Block())

            @block.tensor
            def _(pe):
                pe.sem_inc(down_done, 2)
                for t in range(NT):
                    for n in range(2):
                        pe.matmul(Y[2 * t + n], ident, X[:, t, n * 512:(n + 1) * 512], start=True, stop=False,
                                  skip_group_check=True)

                def gate_up(i, j):
                    e = 4 * i + j
                    slot = MOE1[(0, 1, 3, 4)[j]][0]
                    piece = ring["moe1", (0, 1, 3, 4)[j]]
                    pe.wait_ge(piece.sem, piece.full + 32 * i)
                    pe.wait_ge(act_ready, e + 1)
                    for m in range(2):
                        wv = view(piece, 2048 * m, KD, D_EXP)
                        for f in range(2):
                            for k in range(KD):
                                ins = pe.matmul(GU[j % 2][m][:, f * S:(f + 1) * S], wv[:, k, f * P:(f + 1) * P],
                                                hT[:, k, 0:S], start=(k == 0), stop=(k == KD - 1),
                                                skip_group_check=True)
                        ins.then_inc(gu_full, 1)

                def down(i, j):
                    e = 4 * i + j
                    piece = ring["moe1", (2, 2, 5, 5)[j]]
                    if j % 2 == 0:
                        pe.wait_ge(piece.sem, piece.full + 32 * i)
                    pe.wait_ge(act_ready, e + 3)
                    wv = view(piece, 2048 * (j % 2), 2, D)
                    for t in range(NT):
                        for n in range(2):
                            for f in range(2):
                                ins = pe.matmul(Y[2 * t + n], actT[:, j % 2, f * S + t * P:f * S + (t + 1) * P],
                                                wv[:, f, n * 512:(n + 1) * 512], start=False, stop=False,
                                                skip_group_check=True)
                    ins.then_inc(down_done, 1)

                with pe.Fori(0, MOE1_TURNS) as i:
                    gate_up(i, 0)
                    for j in range(1, 4):
                        gate_up(i, j)
                        down(i, j - 1)
                    down(i, 3)

            @block.scalar
            def _(act):
                with act.Fori(0, MOE1_TURNS) as i:
                    for j in range(4):
                        e = 4 * i + j
                        act.wait_ge(gu_full, 2 * e + 1)
                        act.wait_ge(act_ready, e + 1)
                        act.activation(gated[:, j % 2, :], GU[j % 2][0], ACT.Silu).then_inc(silued, 1)

            @block.vector
            def _(dve):
                dve.sem_inc(act_ready, 2)
                with dve.Fori(0, MOE1_TURNS) as i:
                    for j in range(4):
                        e = 4 * i + j
                        dve.wait_ge(silued, e + 1)
                        dve.wait_ge(gu_full, 2 * e + 2)
                        g = gated[:, j % 2, :]
                        dve.tensor_tensor(g, g, GU[j % 2][1], ALU.mult).then_inc(gated_step, 1)
                        dve.wait_ge(gated_step, e + 1)
                        dve.wait_ge(down_done, e + 1)
                        dve.tensor_tensor(actT[:, j % 2, :].rearrange("p (f s) -> p f s", f=2),
                                          g.rearrange("p (f s) -> p f s", f=2),
                                          cb[:, e, :].unsqueeze(1).broadcast_to([P, 2, S]), ALU.mult).then_inc(act_ready, 1)
                dve.wait_ge(down_done, N_EXP + 2)
                for t in range(NT):
                    for n in range(2):
                        dve.tensor_copy(X[:, t, n * 512:(n + 1) * 512], Y[2 * t + n])

            @block.sync
            def _(sp):
                with sp.Fori(1, MOE1_TURNS) as i:
                    for j in range(6):
                        slot, e0 = MOE1[j]
                        piece = ring["moe1", j]
                        if j % 3 < 2:
                            e = 4 * i + e0
                            sp.wait_ge(gu_full, 2 * e - 6)
                            sp.dma_start(view(piece, 0, KD, D_EXP), gate_v[:, e]).then_inc(piece.sem, 16)
                            sp.dma_start(view(piece, 2048, KD, D_EXP), up_v[:, e]).then_inc(piece.sem, 16)
                        else:
                            sp.wait_ge(down_done, 4 * i + e0)
                            for h in range(2):
                                sp.dma_start(view(piece, 2048 * h, 2, D), down_v[:, 4 * i + e0 + h]).then_inc(piece.sem, 16)
                for j in range(6):
                    slot, e0 = MOE1[j]
                    e = N_EXP - 4 + e0
                    ring["moe1", j].freed = (gu_full, 2 * e + 2) if j % 3 < 2 else (down_done, e + 4)
                load_weights(sp)

        ncol = sb("ncol", [P, 2, 2, 2, KD])
        with ExitStack() as scope:
            mod = sb("mod", [P, 2, 3, 512], scope=scope)
            scT = sb("scT", [P, KD, 32], scope=scope)
            adab = sb("adab", [P, 2, 3, 512], scope=scope)
            sc_zeroed, sc_ready, adab_loaded, adab_zeroed = (sem(x) for x in ("sc_zeroed", "sc_ready", "adab_loaded", "adab_zeroed"))
            ada_full, ada_emptied = sem("ada_full"), sem("ada_emptied")
            block = scope.enter_context(nc.Block())

            @block.tensor
            def _(pe):
                pe.wait_ge(sc_ready, 2)
                with pe.Fori(0, 2) as i:
                    for q in range(3):
                        for j in range(4):
                            c = 4 * q + j
                            piece = ring["ada", c]
                            pe.wait_ge(piece.sem, piece.full + 32 * i)
                        pe.wait_ge(ada_emptied, 3 * i + q + 1)
                        for k in range(KD):
                            for j in range(4):
                                wv = view(ring["ada", 4 * q + j], 0, KD, 512)
                                ins = pe.matmul(psum[q][32 * j:32 * j + 32, :], scT[:, k, :], wv[:, k, :], start=(k == 0),
                                                stop=(k == KD - 1), tile_position=(0, 32 * j), skip_group_check=True)
                        ins.then_inc(ada_full, 1)
                pe.wait_ge(ada_emptied, 9)
                for l in range(2):
                    for q in range(3):
                        b = banks.open(("modT", l, q), DVE)
                        if b.emptied:
                            pe.wait_ge(*b.emptied)
                        for j in range(4):
                            ins = pe.transpose(b.ap[:, j * P:(j + 1) * P], mod[:, l, q, j * P:(j + 1) * P], ident)
                        ins.then_inc(bank_full, 1)

            @block.scalar
            def _(act):
                act.wait_ge(sc_zeroed, 1)
                for s_, name in enumerate(("c_2", "c_ctx_2")):
                    act.activation(scT[:, :, s_], vcols[:, VCOL[name]:VCOL[name] + KD], ACT.Silu).then_inc(sc_ready, 1)

            @block.vector
            def _(dve):
                link = chain(dve, dve_step)
                dve.memset(adab[:, :, :, :], 0.0).then_inc(adab_zeroed, 1)
                dve.memset(scT[:, :, :], 0.0).then_inc(sc_zeroed, 1)
                dve.sem_inc(ada_emptied, 3)
                dve.wait_ge(adab_loaded, 16 * 24)
                with dve.Fori(0, 2) as i:
                    for q in range(3):
                        dve.wait_ge(ada_full, 3 * i + q + 1)
                        dve.tensor_tensor(mod[:, i, q, :], psum[q][:, :], adab[:, i, q, :], ALU.add).then_inc(ada_emptied, 1)
                for l in range(2):
                    for q in range(3):
                        b = banks["modT", l, q]
                        dve.wait_ge(bank_full, b.full)
                        for s_ in range(2):
                            ins = dve.tensor_copy(modcol[:, l, 4 * q:4 * q + 4, :, s_].rearrange("p j b -> p b j"),
                                                  b.ap[:, :].rearrange("p (b j r) -> p b j r", b=4, j=4)[:, :, :, s_])
                        ins.then_inc(emptied[DVE], 1)
                dve.wait_ge(emptied[DVE], banks["modT", 1, 2].done)
                for l in range(2):
                    for n, (name, v) in enumerate((("norm1_w_2", 1), ("norm2_w_2", 4))):
                        c = VCOL[name] + 8 * l
                        for s_ in range(2):
                            dve.scalar_tensor_tensor(ncol[:, l, n, s_, :].rearrange("p (a b) -> p a b", a=2),
                                                     modcol[:, l, 2 * v:2 * v + 2, :, s_], 1.0,
                                                     vcols[:, c:c + 8].rearrange("p (a b) -> p a b", a=2), ALU.add, ALU.mult)

            @block.sync
            def _(sp):
                sp.wait_ge(adab_zeroed, 1)
                for l in range(2):
                    for c in range(12):
                        q, j = c // 4, c % 4
                        sp.dma_start(adab[32 * j:32 * j + 2, l, q, :],
                                     A["ada_b_2"][l, c * 512:(c + 1) * 512].partition_broadcast(2)).then_inc(adab_loaded, 16)
                for c in range(24):
                    ring["ada", c].freed = (ada_full, c // 4 + 1)
                load_weights(sp)

        gate_full = sem("gate_full")
        TT = 2 * NT
        streams = [C[:, t, :] for t in range(NT)] + [X[:, t, :] for t in range(NT)]

        def mod_segments(l, n):
            def segs(k):
                v = 3 * n
                bias = lambda s_: modcol[:, l, 2 * v + k // 4, k % 4, s_:s_ + 1]
                return [(0, S, ncol[:, l, n, 1, k:k + 1], bias(1)), (S, 2 * S, ncol[:, l, n, 0, k:k + 1], bias(0))]
            return segs

        def gate_banks(pe, tag, l, v, s_, by):
            for n in range(2):
                b = banks.open((tag, s_, n), by)
                if b.emptied:
                    pe.wait_ge(*b.emptied)
                for j in range(4):
                    i = pe.matmul(b.ap[:, j * P:(j + 1) * P],
                                  modcol[:, l, 2 * v + n, j, s_:s_ + 1].broadcast_to([P, P]), ident,
                                  start=True, stop=True)
                i.then_inc(bank_full, 1)

        acum_dram = nc.dram_tensor("acum_rows", (64, TT * P), F32, kind="Internal").ap()
        with ExitStack() as ssd:
            Yt = sb("Yt", [P, TT, D_INNER], scope=ssd)
            scratch = slots[:, 3:6, :].rearrange("p s n -> p (s n)")
            pos = [0]

            def carve(n):
                pos[0] += n
                return scratch[:, pos[0] - n:pos[0]]

            padded = carve(4 * 2 * 260).rearrange("p (c s n) -> p c s n", c=4, s=2)
            conv = carve(4 * 512).rearrange("p (c n) -> p c n", c=4)
            tok = carve(TT * 384).rearrange("p (t n) -> p t n", t=TT)
            xdt = carve(2 * TT * GW).rearrange("p (d t n) -> p d t n", d=2, t=TT)
            dt, acs, wst, ea, dec = (carve(TT * 64).rearrange("p (t n) -> p t n", t=TT) for _ in range(5))
            xst = sb("xst", [P, 2, TT, GW], scope=ssd)
            rowsB = sb("rowsB", [P, 2, HPG, TT * P], scope=ssd)
            with ExitStack() as scope:
                u, dtmp, lnu = (rowsB[:, 0, i, 0:TT * 64].rearrange("p (t n) -> p t n", t=TT) for i in range(3))
                ab = rowsB[:, 1, 0, 0:TT * 64].rearrange("p (t n) -> p t n", t=TT)
                negA = rowsB[:, 1, 1, 0:64]
                aT = rowsB[0:64, 1, 2, :]
                xn = Yt[:, 0:2, :].rearrange("p t (a d) -> p (t a) d", a=2)
                norm = NormT("s1", streams, xn, hT, mod_segments(0, 0))
                ctx_loaded, sp_step, a_ready, aT_stored = (sem(x) for x in ("ctx_loaded", "sp_step", "a_ready", "aT_stored"))
                acum_ready = sem("acum_ready")
                block = scope.enter_context(nc.Block())

                @block.tensor
                def _(pe):
                    norm.tensor(pe)
                    for k in range(KD):
                        norm.wait_chunk(pe, k)
                    piece = ring["dt"]
                    pe.wait_ge(piece.sem, piece.full)
                    wv = view(piece, 0, KD, 64)
                    b = banks.open("dt", DVE)
                    pe.wait_ge(*b.emptied)
                    for t in range(TT):
                        for k in range(KD):
                            i = pe.matmul(b.ap[:, t * 64:(t + 1) * 64], hT[:, k, t * P:(t + 1) * P], wv[:, k, :],
                                          start=(k == 0), stop=(k == KD - 1))
                    i.then_inc(bank_full, 1)
                    piece.freed = (bank_full, b.full)
                    pe.wait_ge(a_ready, 1)
                    b = banks.open("acum", DVE)
                    pe.wait_ge(*b.emptied)
                    for t in range(TT):
                        for d in range(2):
                            c = slice(d * 32, (d + 1) * 32)
                            i = pe.matmul(b.ap[:, t * 64 + d * 32:t * 64 + d * 32 + 32], const(("upto", "from")[d]),
                                          ab[:, t, c], start=True, stop=True)
                    i.then_inc(bank_full, 1)
                    b = banks.open("last", DVE)
                    pe.wait_ge(*b.emptied)
                    pe.matmul(b.ap[:, 0:TT * 64], const("ones"), ab[:, :, :].rearrange("p t n -> p (t n)"),
                              start=True, stop=True).then_inc(bank_full, 1)
                    pe.wait_ge(emptied[DVE], banks["acum"].done)
                    b = banks.open("acumT", DVE)
                    pe.wait_ge(*b.emptied)
                    for t in range(TT):
                        i = pe.transpose(b.ap[0:64, t * P:(t + 1) * P], acs[:, t, :], ident)
                    i.then_inc(bank_full, 1)

                @block.gpsimd
                def _(pool):
                    norm.pool(pool)

                @block.scalar
                def _(act):
                    act.dma_start(C[:, :, :], A["ctx_2"].rearrange("b (t p) d -> p (b t) d", p=P)).then_inc(ctx_loaded, 16)
                    act.wait_ge(ctx_loaded, 16)
                    norm.scalar_squares(act)
                    norm.evacuate(act, ACTE)
                    act.activation(negA, gain("ssd_A_log_2"), ACT.Exp).then_inc(sp_step, 1)
                    act.wait_ge(sp_step, 2)
                    act.activation(u, u, ACT.Exp).then_inc(sp_step, 1)
                    act.wait_ge(sp_step, 4)
                    act.activation(lnu, dtmp, ACT.Ln).then_inc(sp_step, 1)
                    act.wait_ge(acum_ready, 1)
                    act.activation(wst, wst, ACT.Exp).then_inc(acum_ready, 1)
                    act.activation(ea, acs, ACT.Exp)
                    act.activation(dec, dec, ACT.Exp)

                @block.vector
                def _(dve):
                    link = chain(dve, dve_step)
                    norm.vector_scale(dve)
                    norm.evacuate(dve, DVE)
                    b = banks["dt"]
                    dve.wait_ge(bank_full, b.full)
                    bias = gain("ssd_dt_bias_2").unsqueeze(1).broadcast_to([P, TT, 64])
                    dve.tensor_tensor(dt, b.ap[:, 0:TT * 64].rearrange("p (t n) -> p t n", t=TT), bias,
                                      ALU.add).then_inc(emptied[DVE], 1)
                    dve.wait_ge(emptied[DVE], b.done)
                    dve.wait_ge(sp_step, 1)
                    link(dve.scalar_tensor_tensor(u, dt, -1.0, dt, ALU.mult, ALU.min))
                    dve.sem_inc(sp_step, 1)
                    dve.wait_ge(sp_step, 3)
                    link(dve.tensor_scalar(dtmp, u, 1.0, None, ALU.add))
                    dve.sem_inc(sp_step, 1)
                    dve.wait_ge(sp_step, 5)
                    link(dve.tensor_scalar(dtmp, dtmp, 1.0, None, ALU.subtract))
                    link(dve.tensor_tensor(lnu, lnu, u, ALU.mult))
                    link(dve.tensor_scalar(ab, dtmp, 0.0, None, ALU.is_equal))
                    link(dve.tensor_tensor(u, u, ab, ALU.mult))
                    link(dve.tensor_scalar(dtmp, dtmp, 1e-30, None, ALU.max))
                    link(dve.reciprocal(dtmp, dtmp))
                    link(dve.tensor_tensor(lnu, lnu, dtmp, ALU.mult))
                    link(dve.tensor_tensor(lnu, lnu, u, ALU.add))
                    link(dve.tensor_scalar(dt, dt, 0.0, None, ALU.max))
                    link(dve.tensor_tensor(dt, dt, lnu, ALU.add))
                    link(dve.tensor_tensor(ab, dt, negA.unsqueeze(1).broadcast_to([P, TT, 64]), ALU.mult))
                    link(dve.tensor_scalar(ab, ab, -1.0, None, ALU.mult))
                    dve.sem_inc(a_ready, 1)
                    flat_ = lambda ap: ap.rearrange("p t n -> p (t n)")
                    b = banks["acum"]
                    dve.wait_ge(bank_full, b.full)
                    dve.tensor_copy(flat_(acs), b.ap[:, 0:TT * 64]).then_inc(emptied[DVE], 1)
                    dve.wait_ge(emptied[DVE], b.done)
                    b = banks["last"]
                    dve.wait_ge(bank_full, b.full)
                    link(dve.tensor_tensor(flat_(wst), b.ap[:, 0:TT * 64], flat_(acs), ALU.subtract))
                    dve.tensor_copy(flat_(dec), b.ap[:, 0:TT * 64]).then_inc(emptied[DVE], 1)
                    dve.wait_ge(emptied[DVE], b.done)
                    dve.sem_inc(acum_ready, 1)
                    b = banks["acumT"]
                    dve.wait_ge(bank_full, b.full)
                    dve.tensor_copy(aT, b.ap[0:64, :]).then_inc(emptied[DVE], 1)
                    dve.wait_ge(acum_ready, 2)
                    link(dve.tensor_tensor(flat_(wst), flat_(wst), flat_(dt), ALU.mult))
                    dve.memset(padded, 0.0)

                @block.sync
                def _(sp):
                    load_weights(sp)
                    sp.wait_ge(emptied[DVE], banks["acumT"].done)
                    sp.dma_start(acum_dram, aT).then_inc(aT_stored, 16)
                    sp.wait_ge(aT_stored, 16)

            with ExitStack() as scope:
                hp = sb("hp", [P, 2, TT, GW], scope=scope)
                off = carve(2 * GW).rearrange("p (d n) -> p d n", d=2)
                rows_loaded = sem("rows_loaded")
                conv_done, silu_done, conv_step = sem("conv_done"), sem("silu_done"), sem("conv_step")
                exps_in, exps_out, m_ready, prod_ready, hp_ready, y_done = (
                    sem(x) for x in ("exps_in", "exps_out", "m_ready", "prod_ready", "hp_ready", "y_done"))
                cbm = carve(2 * TT * P).rearrange("p (d n) -> p d n", d=2)
                CH = lambda g: (2 * g, 2 * g + 1, 16 + g, 24 + g)
                block = scope.enter_context(nc.Block())

                def tap(j, c):
                    at = (1 * P + j * 32 + c) if j < 4 else 2 * P + c
                    return vcols[:, at:at + 1]

                ORDER_B = {0: 1, 3: 0, 2: 3}
                ORDER_F = {1: 0, 2: 1, 3: 2}

                @block.tensor
                def _(pe):
                    def project(g, cs):
                        piece = ring["grp", g]
                        pe.wait_ge(piece.sem, piece.full)
                        for c in cs:
                            b = banks.open(("ch", g, c), ACTE)
                            pe.wait_ge(*b.emptied)
                            wv = view(piece, 0, KD, 256)[:, :, c * P:(c + 1) * P] if c < 2 else \
                                view(piece, 2048 + 1024 * (c - 2), KD, P)
                            for k in range(KD):
                                i = pe.matmul(b.ap[:, :], wv[:, k, :], hT[:, k, :], start=(k == 0), stop=(k == KD - 1))
                            i.then_inc(bank_full, 1)
                        piece.freed = (bank_full, b.full)

                    def to_tokens(g):
                        pe.wait_ge(silu_done, g + 1)
                        b = banks.open(("cbs", g), DVE)
                        pe.wait_ge(*b.emptied)
                        for t in range(TT):
                            tt = slice(t * P, (t + 1) * P)
                            i = pe.matmul(b.ap[:, tt], conv[:, 2, tt], conv[:, 3, tt], start=True, stop=True)
                        i.then_inc(bank_full, 1)
                        for t in range(TT):
                            b = banks.open(("tok", g, t), ACTE)
                            pe.wait_ge(*b.emptied)
                            for c in range(3):
                                i = pe.transpose(b.ap[:, c * P:(c + 1) * P], conv[:, c, t * P:(t + 1) * P], ident)
                            i.then_inc(bank_full, 1)

                    def states(g):
                        pe.wait_ge(prod_ready, g + 1)
                        for n in range(3):
                            b = banks.open(("st", g, n), DVE)
                            pe.wait_ge(*b.emptied)
                            for d in range(2):
                                t = (ORDER_F[n + 1], ORDER_B[(0, 3, 2)[n]])[d]
                                i = pe.matmul(b.ap[:, d * GW:(d + 1) * GW], tok[:, t, 256:384], xst[:, d, t, :],
                                              start=True, stop=True)
                            i.then_inc(bank_full, 1)

                    def outputs(g):
                        for t in range(TT):
                            b = banks.open(("off", g, t), DVE)
                            pe.wait_ge(*b.emptied)
                            if t == 0:
                                pe.wait_ge(hp_ready, g + 1)
                            for d in range(2):
                                if t in (ORDER_F, ORDER_B)[d]:
                                    i = pe.matmul(b.ap[:, d * GW:(d + 1) * GW], conv[:, 3, t * P:(t + 1) * P],
                                                  hp[:, d, t, :], start=True, stop=True)
                            i.then_inc(bank_full, 1)
                            b = banks.open(("diag", g, t), DVE)
                            pe.wait_ge(*b.emptied)
                            if t == 0:
                                pe.wait_ge(m_ready, g + 1)
                            for h in range(HPG):
                                for d in range(2):
                                    i = pe.matmul(b.ap[:, h * 64:(h + 1) * 64], rowsB[:, d, h, t * P:(t + 1) * P],
                                                  xdt[:, d, t, h * 64:(h + 1) * 64], start=(d == 0), stop=(d == 1))
                            i.then_inc(bank_full, 1)

                    project(0, range(4))
                    for g in range(SSD_G):
                        more = g + 1 < SSD_G
                        if more:
                            project(g + 1, (0, 1))
                        to_tokens(g)
                        if more:
                            project(g + 1, (2,))
                        states(g)
                        if more:
                            project(g + 1, (3,))
                        outputs(g)

                @block.scalar
                def _(act):
                    def take(g, cs):
                        for c in cs:
                            b = banks["ch", g, c]
                            act.wait_ge(bank_full, b.full)
                            act.activation(padded[:, c, :, 2:2 + S], b.ap[:, :].rearrange("p (s n) -> p s n", s=2),
                                           ACT.Copy).then_inc(emptied[ACTE], 1)

                    take(0, range(4))
                    for g in range(SSD_G):
                        more = g + 1 < SSD_G
                        for c in range(4):
                            act.wait_ge(conv_done, 4 * g + c + 1)
                            col = 2 * P + 32 + CH(g)[c]
                            i = act.activation(conv[:, c, :], conv[:, c, :], ACT.Silu, bias=vcols[:, col:col + 1])
                        i.then_inc(silu_done, 1)
                        if more:
                            take(g + 1, (0, 1))
                        for t in range(TT):
                            copy_out(act, ACTE, ("tok", g, t), tok[:, t, :], 384)
                        if more:
                            take(g + 1, (2,))
                        for d in range(2):
                            act.wait_ge(exps_in, 2 * g + d + 1)
                            r = rowsB[:, d, :, :].rearrange("p h n -> p (h n)")
                            act.activation(r, r, ACT.Exp).then_inc(exps_out, 1)
                        if more:
                            take(g + 1, (3,))

                @block.vector
                def _(dve):
                    link = chain(dve, dve_step)
                    heads4 = lambda ap: ap.rearrange("p (h d) -> p h d", h=HPG)
                    for g in range(SSD_G):
                        hs = slice(g * HPG, (g + 1) * HPG)
                        for c in range(4):
                            b = banks["ch", g, c]
                            dve.wait_ge(emptied[ACTE], b.done)
                            o = conv[:, c, :].rearrange("p (s n) -> p s n", s=2)
                            link(dve.tensor_scalar(o, padded[:, c, :, 0:S], tap(0, CH(g)[c]), None, ALU.mult))
                            for j in range(1, CONV_W):
                                i = dve.scalar_tensor_tensor(o, padded[:, c, :, j:j + S], tap(j, CH(g)[c]), o,
                                                             ALU.mult, ALU.add)
                                if j < CONV_W - 1:
                                    link(i)
                            i.then_inc(conv_done, 1)
                        dve.wait_ge(rows_loaded, 32 * (g + 1))
                        for d in range(2):
                            r = rowsB[:, d, :, :].rearrange("p h (t n) -> p h t n", t=TT)
                            a_s = acs[:, :, d * 32 + g * HPG:d * 32 + (g + 1) * HPG].rearrange("p t h -> p h t")
                            link(dve.tensor_tensor(r, r, a_s.unsqueeze(3).broadcast_to([P, HPG, TT, P]), ALU.subtract))
                            r = rowsB[:, d, :, :].rearrange("p h n -> p (h n)")
                            dve.tensor_scalar(r, r, 0.0, None, ALU.min).then_inc(exps_in, 1)
                        b = banks["cbs", g]
                        dve.wait_ge(bank_full, b.full)
                        for d in range(2):
                            mask = const(("upto", "from")[d]).unsqueeze(1).broadcast_to([P, TT, P])
                            i = dve.tensor_tensor(cbm[:, d, :].rearrange("p (t n) -> p t n", t=TT),
                                                  b.ap[:, :].rearrange("p (t n) -> p t n", t=TT), mask, ALU.mult)
                        i.then_inc(emptied[DVE], 1)
                        for t in range(TT):
                            dve.wait_ge(emptied[ACTE], banks["tok", g, t].done)
                        xs = tok[:, :, 0:GW].rearrange("p t (h d) -> p t h d", h=HPG)
                        for d in range(2):
                            hd = slice(d * 32 + g * HPG, d * 32 + (g + 1) * HPG)
                            for dst, f in ((xst, wst), (xdt, dt)):
                                i = dve.tensor_tensor(dst[:, d, :, :].rearrange("p t (h d) -> p t h d", h=HPG), xs,
                                                      f[:, :, hd].unsqueeze(3).broadcast_to([P, TT, HPG, 64]), ALU.mult)
                        i.then_inc(prod_ready, 1)
                        dve.wait_ge(emptied[DVE], banks["cbs", g].done)
                        for d in range(2):
                            dve.wait_ge(exps_out, 2 * g + d + 1)
                            r = rowsB[:, d, :, :]
                            i = dve.tensor_tensor(r, r, cbm[:, d, :].unsqueeze(1).broadcast_to([P, HPG, TT * P]), ALU.mult)
                        i.then_inc(m_ready, 1)
                        for n in range(3):
                            b = banks["st", g, n]
                            dve.wait_ge(bank_full, b.full)
                            for d in range(2):
                                t = (n + 1, (0, 3, 2)[n])[d]
                                if n == 0:
                                    i = dve.tensor_copy(hp[:, d, t, :], b.ap[:, d * GW:(d + 1) * GW])
                                else:
                                    before = (n, (0, 3, 2)[n - 1])[d]
                                    chunk = (n, (1, 0, 3)[n])[d]
                                    dd = dec[:, chunk, d * 32 + g * HPG:d * 32 + (g + 1) * HPG]
                                    link(dve.tensor_tensor(heads4(hp[:, d, t, :]), heads4(hp[:, d, before, :]),
                                                           dd.unsqueeze(2).broadcast_to([P, HPG, 64]), ALU.mult))
                                    i = dve.tensor_tensor(hp[:, d, t, :], hp[:, d, t, :], b.ap[:, d * GW:(d + 1) * GW], ALU.add)
                            i.then_inc(emptied[DVE], 1)
                            dve.wait_ge(emptied[DVE], b.done)
                        dve.sem_inc(hp_ready, 1)
                        for t in range(TT):
                            y = Yt[:, t, g * GW:(g + 1) * GW]
                            Db = gain("ssd_D_2")[:, hs].unsqueeze(2).broadcast_to([P, HPG, 64])
                            link(dve.tensor_tensor(heads4(y), heads4(tok[:, t, 0:GW]), Db, ALU.mult))
                            b = banks["off", g, t]
                            dve.wait_ge(bank_full, b.full)
                            ds = [d for d in range(2) if t in (ORDER_F, ORDER_B)[d]]
                            for d in ds:
                                e = ea[:, t, d * 32 + g * HPG:d * 32 + (g + 1) * HPG].unsqueeze(2).broadcast_to([P, HPG, 64])
                                i = dve.tensor_tensor(heads4(off[:, d, :]), heads4(b.ap[:, d * GW:(d + 1) * GW]), e, ALU.mult)
                            i.then_inc(emptied[DVE], 1)
                            dve.wait_ge(emptied[DVE], b.done)
                            for d in ds:
                                link(dve.tensor_tensor(y, y, off[:, d, :], ALU.add))
                            b = banks["diag", g, t]
                            dve.wait_ge(bank_full, b.full)
                            dve.tensor_tensor(y, y, b.ap[:, 0:GW], ALU.add).then_inc(emptied[DVE], 1)
                        dve.wait_ge(emptied[DVE], b.done)

                @block.gpsimd
                def _(pool):
                    for g in range(SSD_G):
                        if g:
                            pool.wait_ge(bank_full, banks["diag", g - 1, TT - 1].full)
                        for d in range(2):
                            src = acum_dram[d * 32 + g * HPG:d * 32 + (g + 1) * HPG, :].rearrange("h n -> (h n)")
                            pool.dma_start(rowsB[:, d, :, :].rearrange("p h n -> p (h n)"),
                                           src.partition_broadcast(P)).then_inc(rows_loaded, 16)

                @block.sync
                def _(sp):
                    load_weights(sp)

            with ExitStack() as scope:
                sz = sb("sz", [P, 2, 512], scope=scope)
                g1 = rowsB[:, :, :, :].rearrange("p d h n -> p (d h n)")[:, 0:2048].rearrange("p (s n) -> p s n", s=2)
                part = rowsB[:, :, :, :].rearrange("p d h n -> p (d h n)")[:, 2048:4096].rearrange("p (s n) -> p s n", s=4)
                yT = scratch[:, 0:16 * 512].rearrange("p (k n) -> p k n", k=16)
                z_silued, z_used, y_squared, y_rooted = (sem(x) for x in ("z_silued", "z_used", "y_squared", "y_rooted"))
                gate_done = sem("gate1_done")
                ng = VCOL["ssd_norm_w_2"]
                to_yT = Transpose("yT", lambda n, t: Yt[:, t, n * P:(n + 1) * P], 16, P, lambda g, m: yT[:, g:g + m, :],
                                  gain=lambda n: vcols[:, ng + n:ng + n + 1], tiles=TT)
                block = scope.enter_context(nc.Block())

                @block.tensor
                def _(pe):
                    gate_banks(pe, "g1", 0, 2, 0, ACTE)
                    gate_banks(pe, "g1", 0, 2, 1, ACTE)
                    for n in range(4):
                        piece = ring["z", n]
                        pe.wait_ge(piece.sem, piece.full)
                        wv = view(piece, 0, KD, 512)
                        for t in range(TT):
                            b, _ = gemm(pe, ("z", n, t), lambda k: hT[:, k, t * P:(t + 1) * P], KD, t,
                                        lambda k: wv[:, k, :], 512, ACTE)
                        piece.freed = (bank_full, b.full)
                    pe.wait_ge(z_used, 16)
                    to_yT.tensor(pe)
                    to_yT.wait_all(pe)
                    outs = [(t, n, banks.open(("so", t, n), DVE)) for t in range(TT) for n in range(2)]
                    for q in range(4):
                        piece = ring["ssd_out", q]
                        pe.wait_ge(piece.sem, piece.full)
                        wv = view(piece, 0, 4, D)
                        for t, n, b in outs:
                            if q == 0:
                                pe.wait_ge(*b.emptied)
                            for k in range(4):
                                i = pe.matmul(b.ap[:, :], yT[:, 4 * q + k, t * P:(t + 1) * P], wv[:, k, n * 512:(n + 1) * 512],
                                              start=(q == 0 and k == 0), stop=(q == 3 and k == 3), skip_group_check=True)
                            if q == 3:
                                i.then_inc(bank_full, 1)
                            elif (t, n) == (TT - 1, 1):
                                i.then_inc(gate_full, 1)
                        piece.freed = (gate_full, q + 1) if q < 3 else (bank_full, b.full)
                    scratch_use.freed = (bank_full, b.full)

                @block.gpsimd
                def _(pool):
                    pool.wait_ge(y_squared, TT)
                    root(pool, 0, TT, D_INNER, y_rooted)

                @block.scalar
                def _(act):
                    for s_ in range(2):
                        for n in range(2):
                            copy_out(act, ACTE, ("g1", s_, n), g1[:, s_, n * 512:(n + 1) * 512], 512)
                    for n in range(4):
                        for t in range(TT):
                            i = 4 * n + t
                            b = banks["z", n, t]
                            act.wait_ge(bank_full, b.full)
                            if i >= 2:
                                act.wait_ge(z_used, i - 1)
                            act.activation(sz[:, i % 2, :], b.ap[:, :], ACT.Silu).then_inc(emptied[ACTE], 1)
                    act.wait_ge(z_used, 16)
                    for t in range(TT):
                        junk = 8192 + D_INNER * (t % 2)
                        if t >= 2:
                            act.wait_ge(y_squared, t - 1)
                        act.activation(scratch[:, junk:junk + D_INNER], Yt[:, t, :], ACT.Square,
                                       accum_out=eps_rows[:, t:t + 1]).then_inc(y_squared, 1)
                    to_yT.evacuate(act, ACTE)

                @block.vector
                def _(dve):
                    link = chain(dve, dve_step)
                    for n in range(4):
                        for t in range(TT):
                            i = 4 * n + t
                            dve.wait_ge(emptied[ACTE], banks["z", n, t].done)
                            y = Yt[:, t, n * 512:(n + 1) * 512]
                            dve.tensor_tensor(y, y, sz[:, i % 2, :], ALU.mult).then_inc(z_used, 1)
                    to_yT.evacuate(dve, DVE)
                    dve.wait_ge(y_rooted, 1)
                    link(dve.tensor_scalar(rstd[:, 0:TT], rstd[:, 0:TT], float(D_INNER) ** 0.5, None, ALU.mult))
                    dve.wait_ge(emptied[ACTE], banks["g1", 1, 1].done)
                    for t in range(TT):
                        for n in range(2):
                            b = banks["so", t, n]
                            c = slice(n * 512, (n + 1) * 512)
                            dve.wait_ge(bank_full, b.full)
                            p_ = part[:, (2 * t + n) % 4, :]
                            dve.scalar_tensor_tensor(p_, b.ap[:, :], rstd[:, t:t + 1], g1[:, 1 - t // 2, c],
                                                     ALU.mult, ALU.mult).then_inc(emptied[DVE], 1)
                            dve.wait_ge(emptied[DVE], b.done)
                            dve.tensor_tensor(streams[t][:, c], streams[t][:, c], p_, ALU.add)

                @block.sync
                def _(sp):
                    load_weights(sp)

        def expert_choice(l):
            sid = (1, 0) if l == 0 else (0,)
            NJ = len(sid)
            res = [streams[2 * NT - NJ * NT + j * NT:][:NT] for j in range(NJ)]
            T = NJ * NT
            tag = f"e{l}"
            with ExitStack() as scope:
                xgT = sb("xgT" + tag, [P, N_EXP, KD, 2 * CAP], scope=scope)
                G = sb("G" + tag, [P, NJ, 4, S], scope=scope)
                shared = sb("xn" + tag, [P, 4, D], scope=scope)
                xn = shared[:, 0:T, :]
                with ExitStack() as route:
                    wr = routers[:, l]
                    lg = sb("lg" + tag, [P, T, N_EXP], scope=route)
                    aff = sb("aff" + tag, [P, NT, NJ * N_EXP], scope=route)
                    red = sb("red" + tag, [P, T], scope=route)
                    sv = sb("sv" + tag, [P, NT, NJ * N_EXP], scope=route)
                    R = NJ * N_EXP
                    affT = sb("affT" + tag, [R, S], scope=route)
                    ones = sb("ones" + tag, [R, S], scope=route)
                    top8 = sb("top8" + tag, [R, 8], scope=route)
                    hflat = hT[:, :, :].rearrange("p k n -> p (k n)")
                    onehot = hflat[:, 0:2048].rearrange("p (t j n) -> p t j n", t=NT, j=2)
                    gated = hflat[:, 2048:4096].rearrange("p (t j n) -> p t j n", t=NT, j=2)
                    if l == 0:
                        segs = mod_segments(0, 1)
                    else:
                        segs = lambda k: [(0, S, ncol[:, 1, 1, 0, k:k + 1], modcol[:, 1, 6 + k // 4, k % 4, 0:1])]
                    norm = NormT(tag, [r for rs in res for r in rs], xn, hT, segs)
                    sub_ready, exp_ready, aff_ready, sv_ready, onehot_ready = (
                        sem(x + tag) for x in ("sub_ready_", "exp_ready_", "aff_ready_", "sv_ready_", "onehot_ready_"))
                    block = route.enter_context(nc.Block())

                    @block.tensor
                    def _(pe):
                        norm.tensor(pe)
                        for k in range(KD):
                            norm.wait_chunk(pe, k)
                        pe.wait_ge(routers_loaded, 32)
                        b = banks.open((tag, "router"), DVE)
                        pe.wait_ge(*b.emptied)
                        for t in range(T):
                            for k in range(KD):
                                i = pe.matmul(b.ap[:, t * 16:(t + 1) * 16], hT[:, k, t * P:(t + 1) * P], wr[:, k, :],
                                              start=(k == 0), stop=(k == KD - 1))
                        i.then_inc(bank_full, 1)
                        pe.wait_ge(aff_ready, 1)
                        b = banks.open((tag, "affT"), DVE)
                        pe.wait_ge(*b.emptied)
                        for t in range(NT):
                            i = pe.transpose(b.ap[0:R, t * P:(t + 1) * P], aff[:, t, :], ident)
                        i.then_inc(bank_full, 1)
                        pe.wait_ge(sv_ready, 1)
                        b = banks.open((tag, "sv"), DVE)
                        pe.wait_ge(*b.emptied)
                        for t in range(NT):
                            i = pe.transpose(b.ap[:, t * R:(t + 1) * R], affT[:, t * P:(t + 1) * P], consts[0:R, 0:R])
                        i.then_inc(bank_full, 1)
                        pe.wait_ge(onehot_ready, 1)
                        for j in range(NJ):
                            for k in range(KD):
                                b = banks.open((tag, "xg", j, k), (DVE, ACTE)[k % 2])
                                pe.wait_ge(*b.emptied)
                                for t in range(NT):
                                    i = pe.matmul(b.ap[:, :], xn[:, j * NT + t, k * P:(k + 1) * P], onehot[:, t, j, :],
                                                  start=(t == 0), stop=(t == NT - 1))
                                i.then_inc(bank_full, 1)
                            for n in range(2):
                                b = banks.open((tag, "G", j, n), (DVE, ACTE)[n])
                                pe.wait_ge(*b.emptied)
                                for m in range(2):
                                    for t in range(NT):
                                        c = (2 * n + m) * P
                                        i = pe.transpose(b.ap[:, (2 * m + t) * P:(2 * m + t + 1) * P],
                                                         gated[:, t, j, c:c + P], ident)
                                i.then_inc(bank_full, 1)

                    @block.gpsimd
                    def _(pool):
                        norm.pool(pool)

                    def take(eng, by):
                        for j in range(NJ):
                            for k in range(KD):
                                b = banks[tag, "xg", j, k]
                                if b.by != by:
                                    continue
                                eng.wait_ge(bank_full, b.full)
                                g, bias = ncol[:, l, 1, sid[j], k:k + 1], modcol[:, l, 6 + k // 4, k % 4, sid[j]:sid[j] + 1]
                                dst = xgT[:, :, k, j * CAP:(j + 1) * CAP]
                                src = b.ap[:, :].rearrange("p (e c) -> p e c", c=CAP)
                                if by == DVE:
                                    i = eng.tensor_scalar(dst, src, g, bias, ALU.mult, ALU.add)
                                else:
                                    i = eng.activation(dst, src, ACT.Identity, scale=g, bias=bias)
                                i.then_inc(emptied[by], 1)
                            for n in range(2):
                                copy_out(eng, by, (tag, "G", j, n), G[:, j, 2 * n:2 * n + 2, :].rearrange("p m t -> p (m t)"), 512)

                    @block.scalar
                    def _(act):
                        norm.scalar_squares(act)
                        norm.evacuate(act, ACTE)
                        act.wait_ge(sub_ready, 1)
                        act.activation(lg[:, :, :], lg[:, :, :], ACT.Exp).then_inc(exp_ready, 1)
                        take(act, ACTE)

                    @block.vector
                    def _(dve):
                        link = chain(dve, dve_step)
                        if NJ == 1:
                            dve.memset(xgT[:, :, :, CAP:2 * CAP], 0.0)
                        dve.memset(ones[:, :], 1.0)
                        norm.vector_scale(dve)
                        norm.evacuate(dve, DVE)
                        b = banks[tag, "router"]
                        dve.wait_ge(bank_full, b.full)
                        lgt = b.ap[:, 0:T * 16].rearrange("p (t e) -> p t e", e=16)
                        link(dve.tensor_reduce(red[:, :], lgt, AX.X, ALU.max))
                        rb = red[:, :].unsqueeze(2).broadcast_to([P, T, 16])
                        dve.tensor_tensor(lg[:, :, :], lgt, rb, ALU.subtract).then_inc(emptied[DVE], 1)
                        dve.wait_ge(emptied[DVE], b.done)
                        dve.sem_inc(sub_ready, 1)
                        dve.wait_ge(exp_ready, 1)
                        link(dve.tensor_reduce(red[:, :], lg[:, :, :], AX.X, ALU.add))
                        link(dve.reciprocal(red[:, :], red[:, :]))
                        for j in range(NJ):
                            i = dve.tensor_tensor(aff[:, :, j * 16:(j + 1) * 16], lg[:, j * NT:(j + 1) * NT, :],
                                                  red[:, j * NT:(j + 1) * NT].unsqueeze(2).broadcast_to([P, NT, 16]), ALU.mult)
                        link(i)
                        dve.sem_inc(aff_ready, 1)
                        b = banks[tag, "affT"]
                        dve.wait_ge(bank_full, b.full)
                        dve.tensor_copy(affT[:, :], b.ap[0:R, 0:S]).then_inc(emptied[DVE], 1)
                        dve.wait_ge(emptied[DVE], b.done)
                        for r in range(CAP // 8):
                            link(dve.max(top8[:, :], affT[:, :]))
                            link(dve.match_replace(affT[:, :], top8[:, :], affT[:, :], TAKEN))
                        link(dve.tensor_scalar(affT[:, :], affT[:, :], TAKEN, None, ALU.is_equal))
                        link(dve.tensor_tensor_scan(ones[:, :], ones[:, :], affT[:, :], 0.0, ALU.mult, ALU.add))
                        link(dve.tensor_tensor(affT[:, :], affT[:, :], ones[:, :], ALU.mult))
                        link(dve.tensor_scalar(affT[:, :], affT[:, :], 1.0, None, ALU.subtract))
                        dve.sem_inc(sv_ready, 1)
                        b = banks[tag, "sv"]
                        dve.wait_ge(bank_full, b.full)
                        dve.tensor_copy(sv[:, :, :].rearrange("p t r -> p (t r)"), b.ap[:, 0:NT * R]).then_inc(emptied[DVE], 1)
                        dve.wait_ge(emptied[DVE], b.done)
                        for t in range(NT):
                            for j in range(NJ):
                                o = onehot[:, t, j, :].rearrange("p (e c) -> p e c", c=CAP)
                                place = const("slot").unsqueeze(1).broadcast_to([P, 16, CAP])
                                mine = sv[:, t, j * 16:(j + 1) * 16].unsqueeze(2).broadcast_to([P, 16, CAP])
                                link(dve.tensor_tensor(o, place, mine, ALU.is_equal))
                                link(dve.tensor_tensor(gated[:, t, j, :].rearrange("p (e c) -> p e c", c=CAP), o,
                                                       aff[:, t, j * 16:(j + 1) * 16].unsqueeze(2).broadcast_to([P, 16, CAP]),
                                                       ALU.mult))
                        dve.sem_inc(onehot_ready, 1)
                        take(dve, DVE)

                    @block.sync
                    def _(sp):
                        load_weights(sp)

                hflat = hT[:, :, :].rearrange("p k n -> p (k n)")
                xg = hflat[:, 0:512].rearrange("p (k c) -> p k c", k=KD)
                sg, acts, aT, Gs, g2 = (hflat[:, 512 * n:512 * (n + 1)] for n in (1, 2, 3, 4, 5))
                sflat = shared[:, 2:4, :].rearrange("p t d -> p (t d)")
                ye = [hflat[:, 3072:3584], hflat[:, 3584:4096], sflat[:, 0:512], sflat[:, 512:1024]]
                if NJ == 2:
                    Gs = Gs.rearrange("p (j t) -> p j t", j=2)
                else:
                    Gs = Gs[:, 0:S].unsqueeze(1)
                aTv = aT.rearrange("p (b c) -> p b c", b=4)
                Y2 = shared[:, 0:NJ, :]
                names = ("xg_ready_", "half_used_", "h1_full_", "h3_full_", "silued_", "a_ready_", "tr_full_", "aT_ready_",
                         "y_full_", "ye_ready_", "gs_ready_", "sc_full_", "sc_added_", "g2_full_", "g2_ready_")
                (xg_ready, half_used, h1_full, h3_full, silued, a_ready, tr_full, aT_ready, y_full, ye_ready,
                 gs_ready, sc_full, sc_added, g2_full, g2_ready) = (sem(n + tag) for n in names)
                moved = [sem(f"y2_moved{j}_{tag}") for j in range(4)]
                PIECES = [ring["moe2", l, j] for j in range(6)]
                SC = 4 * NJ
                TURNS = N_EXP // 4
                block = scope.enter_context(nc.Block())

                @block.tensor
                def _(pe):
                    for n in range(2):
                        for s_ in range(2):
                            row = 64 * n + 32 * s_
                            for j in range(4):
                                col = modcol[:, l, 10 + n, j, sid[s_ % NJ]:sid[s_ % NJ] + 1]
                                i = pe.matmul(psum[7][row:row + 32, j * P:(j + 1) * P], col.broadcast_to([P, 32]), ident,
                                              start=True, stop=True, tile_position=(0, row), skip_group_check=True)
                    i.then_inc(g2_full, 1)

                    def halves(bank, lhsT, first, e, done):
                        for h in range(2):
                            piece = PIECES[first + h]
                            pe.wait_ge(piece.sem, piece.full + 16 * e)
                            wv = view(piece, 0, 4, D)
                            for k in range(4):
                                for n in range(2):
                                    i = pe.matmul(bank[64 * n:64 * n + 64, :], lhsT(4 * h + k), wv[:, k, n * 512:(n + 1) * 512],
                                                  start=(h == 0 and k == 0), stop=(h == 1 and k == 3),
                                                  tile_position=(0, 64 * n), skip_group_check=True)
                            i.then_inc(half_used if h == 0 else done, 1)

                    def expert(e, first):
                        pe.wait_ge(xg_ready, e + 1)
                        if not first:
                            pe.wait_ge(a_ready, e)
                        halves(psum[0], lambda k: xg[:, k, :], 0, e, h1_full)
                        halves(psum[1], lambda k: xg[:, k, :], 2, e, h3_full)
                        pe.wait_ge(a_ready, e + 1)
                        if not first:
                            pe.wait_ge(aT_ready, e)
                        for b in range(4):
                            i = pe.transpose(psum[2][:, b * P:(b + 1) * P], acts[:, b * P:(b + 1) * P], ident)
                        i.then_inc(tr_full, 1)
                        pe.wait_ge(aT_ready, e + 1)
                        if not first:
                            pe.wait_ge(ye_ready, e)
                        halves(psum[3], lambda k: aTv[:, k % 4, 64 * (k // 4):64 * (k // 4) + 64], 4, e, y_full)

                    def scatter(turn, first):
                        for j in range(4):
                            pe.wait_ge(moved[j], 32 * NJ * (turn + 1))
                        pe.wait_ge(gs_ready, turn + 1)
                        for q in range(SC):
                            j, t, n = q // 4, q // 2 % 2, q % 2
                            if q >= 4 or not first:
                                pe.wait_ge(sc_added, SC * turn + q - 3)
                            pe.matmul(psum[4 + q % 4][:, :], Gs[:, j, t * P:(t + 1) * P], Y2[:, j, n * 512:(n + 1) * 512],
                                      start=True, stop=True, skip_group_check=True).then_inc(sc_full, 1)

                    for e in range(4):
                        expert(e, e == 0)
                    pe.wait_ge(g2_ready, 1)
                    expert(4, False)
                    expert(5, False)
                    scatter(0, True)
                    with pe.Fori(1, TURNS - 1) as turn:
                        for j in range(2, 6):
                            expert(4 * turn + j, False)
                        scatter(turn, False)
                    expert(N_EXP - 2, False)
                    expert(N_EXP - 1, False)
                    scatter(TURNS - 1, False)

                @block.scalar
                def _(act):
                    def gather(e):
                        act.activation(xg, xgT[:, e, :, :], ACT.Copy).then_inc(xg_ready, 1)

                    def silu(e):
                        act.wait_ge(h1_full, e + 1)
                        act.activation(sg, psum[0][:, :], ACT.Silu).then_inc(silued, 1)

                    def transposed(e):
                        act.wait_ge(tr_full, e + 1)
                        act.activation(aT, psum[2][:, :], ACT.Copy).then_inc(aT_ready, 1)

                    def move(e, j):
                        act.wait_ge(ye_ready, e + 1)
                        for s_ in range(NJ):
                            for n in range(2):
                                act.dma_start(Y2[32 * j:32 * j + 32, s_, n * 512:(n + 1) * 512],
                                              ye[j][64 * n + 32 * s_:64 * n + 32 * s_ + 32, :]).then_inc(moved[j], 16)

                    def gates(turn):
                        act.activation(Gs, G[:, :, turn, :], ACT.Copy).then_inc(gs_ready, 1)

                    def second_half(turn, first):
                        gather(4 * turn + 2)
                        silu(4 * turn + 2)
                        if not first:
                            act.wait_ge(sc_full, SC * turn)
                        move(4 * turn, 0)
                        move(4 * turn + 1, 1)
                        transposed(4 * turn + 2)
                        gates(turn)
                        gather(4 * turn + 3)
                        silu(4 * turn + 3)
                        move(4 * turn + 2, 2)
                        transposed(4 * turn + 3)

                    def next_half(turn):
                        gather(4 * turn + 4)
                        silu(4 * turn + 4)
                        move(4 * turn + 3, 3)
                        transposed(4 * turn + 4)
                        gather(4 * turn + 5)
                        silu(4 * turn + 5)
                        transposed(4 * turn + 5)

                    for e in range(2):
                        gather(e)
                        if e == 0:
                            act.wait_ge(g2_full, 1)
                            act.activation(g2, psum[7][:, :], ACT.Copy).then_inc(g2_ready, 1)
                        silu(e)
                        transposed(e)
                    second_half(0, True)
                    next_half(0)
                    with act.Fori(1, TURNS - 1) as turn:
                        second_half(turn, False)
                        next_half(turn)
                    second_half(TURNS - 1, False)
                    move(N_EXP - 1, 3)

                @block.vector
                def _(dve):
                    dve.wait_ge(g2_ready, 1)

                    def expert(e, j, turn):
                        dve.wait_ge(silued, e + 1)
                        dve.wait_ge(h3_full, e + 1)
                        dve.tensor_tensor(acts, sg, psum[1][:, :], ALU.mult).then_inc(a_ready, 1)
                        dve.wait_ge(y_full, e + 1)
                        if turn is not None:
                            dve.wait_ge(moved[j], 32 * NJ * turn)
                        dve.tensor_tensor(ye[j], psum[3][:, :], g2, ALU.mult).then_inc(ye_ready, 1)

                    def add(turn, first):
                        if not first:
                            dve.wait_ge(sc_added, SC * turn)
                        for q in range(SC):
                            j, t, n = q // 4, q // 2 % 2, q % 2
                            c = slice(n * 512, (n + 1) * 512)
                            dve.wait_ge(sc_full, SC * turn + q + 1)
                            dve.tensor_tensor(res[j][t][:, c], res[j][t][:, c], psum[4 + q % 4][:, :], ALU.add).then_inc(sc_added, 1)

                    for e in range(4):
                        expert(e, e, None)
                    expert(4, 0, 1)
                    expert(5, 1, 1)
                    add(0, True)
                    with dve.Fori(1, TURNS - 1) as turn:
                        for j in range(2, 6):
                            expert(4 * turn + j, j % 4, turn + j // 4)
                        add(turn, False)
                    expert(N_EXP - 2, 2, TURNS - 1)
                    expert(N_EXP - 1, 3, TURNS - 1)
                    add(TURNS - 1, False)

                @block.sync
                def _(sp):
                    with sp.Fori(1, N_EXP) as e:
                        for j in range(6):
                            if j % 2 == 0:
                                sp.wait_ge(half_used, 3 * e - 2 + j // 2)
                            else:
                                sp.wait_ge((h1_full, h3_full, y_full)[j // 2], e)
                            src = w_v[j // 2][:, l * N_EXP + e, 4 * (j % 2):4 * (j % 2) + 4]
                            sp.dma_start(view(PIECES[j], 0, 4, D), src).then_inc(PIECES[j].sem, 16)
                    for j in range(6):
                        PIECES[j].freed = (half_used, 3 * N_EXP - 2 + j // 2) if j % 2 == 0 else ((h1_full, h3_full, y_full)[j // 2], N_EXP)
                    load_weights(sp)

        expert_choice(0)

        with ExitStack() as scope:
            shared = sb("xn5", [P, 4, D], scope=scope)
            q = sb("q5", [P, NT, QH * 64], scope=scope)
            kk = sb("k5", [P, TT, KVH * 64], scope=scope)
            vv = sb("v5", [P, TT, KVH * 64], scope=scope)
            kT = sb("kT5", [64, KVH, TT * P], scope=scope)
            g1 = sb("g15", [P, D], scope=scope)
            part = sb("part5", [P, 2, 512], scope=scope)
            pT5 = sb("pT5", [P, 2048], scope=scope)
            bufs = (sb("probs5", [P, 4, 512], scope=scope), (pT5, hT[:, :, :].rearrange("p k n -> p (k n)")[:, 2048:4096]),
                    sb("negmax5", [P, 32], scope=scope), sb("sums5", [P, 32], scope=scope))
            qT = shared[0:64, :, :].rearrange("p t d -> p (t d)").rearrange("p (h n) -> p h n", h=QH)
            hflat = hT[:, :, :].rearrange("p k n -> p (k n)")
            sq = hflat[:, 0:2048].rearrange("p (h d) -> p h d", d=64)
            tmp = hflat[:, 2048:3072].rearrange("p (a h d) -> p a h d", a=2, h=16)
            oT = hflat[:, 0:2048].rearrange("p (k n) -> p k n", k=8)
            norm = NormT("n5", streams, shared, hT, mod_segments(1, 0))
            qh = q[:, :, :].rearrange("p t (h d) -> p t h d", d=64)
            kh = kk[:, :, :].rearrange("p t (h d) -> p t h d", d=64)
            qn, kn = HeadNorm("q5"), HeadNorm("k5")
            cos2 = const("cos2d").rearrange("p (t d) -> p t d", t=NT)
            sin2 = const("sin2d").rearrange("p (t d) -> p t d", t=NT)
            q_ready, k_ready = sem("q5_ready"), sem("k5_ready")
            to_qT = Transpose("qT5", lambda n, t: qh[:, t, n, :], QH, 64, lambda g, m: qT[:, g:g + m, :])
            to_kT = Transpose("kT5", lambda n, t: kh[:, t, n, :], KVH, 64, lambda g, m: kT[:, g:g + m, :], tiles=TT)
            att = Attention("att5", QH, lambda h: qT[:, h, :], lambda h: kT[:, h // QPK, :],
                            lambda h, kt: vv[:, kt, (h // QPK) * 64:(h // QPK + 1) * 64], TT * P, HD ** -0.5, lambda p: oT[:, p, :], bufs)
            block = scope.enter_context(nc.Block())

            @block.tensor
            def _(pe):
                gate_banks(pe, "g15", 1, 2, 0, ACTE)
                norm.tensor(pe)
                for k in range(KD):
                    norm.wait_chunk(pe, k)
                for n in range(2):
                    piece = ring["qkv", n]
                    pe.wait_ge(piece.sem, piece.full)
                    wv = view(piece, 0, KD, 512)
                    for t in range(NT):
                        b, _ = gemm(pe, ("q5", n, t), lambda k: hT[:, k, S + t * P:S + (t + 1) * P], KD, t,
                                    lambda k: wv[:, k, :], 512, ACTE)
                    piece.freed = (bank_full, b.full)
                piece = ring["qkv", 2]
                pe.wait_ge(piece.sem, piece.full)
                wv = view(piece, 0, KD, 512)
                for t in range(TT):
                    b, _ = gemm(pe, ("kv5", t), lambda k: hT[:, k, t * P:(t + 1) * P], KD, t, lambda k: wv[:, k, :], 512, DVE)
                piece.freed = (bank_full, b.full)
                pe.wait_ge(q_ready, 1)
                to_qT.tensor(pe)
                pe.wait_ge(k_ready, 1)
                to_kT.tensor(pe)
                to_qT.wait_all(pe)
                to_kT.wait_all(pe)
                att.tensor(pe)
                pe.wait_ge(emptied[DVE], banks["att5", "pv", QH // 2 - 1].done)
                w0, w1 = ring["attn_out", 0], ring["attn_out", 1]
                pe.wait_ge(w0.sem, w0.full)
                pe.wait_ge(w1.sem, w1.full)
                wv2 = (view(w0, 0, 4, D), view(w1, 0, 4, D))
                for t in range(NT):
                    for n in range(2):
                        b, _ = gemm(pe, ("ao5", t, n), lambda k: oT[:, k, t * P:(t + 1) * P], KD, t,
                                    lambda k: wv2[k // 4][:, k % 4, n * 512:(n + 1) * 512], 512, DVE)
                w0.freed = w1.freed = (bank_full, b.full)

            @block.gpsimd
            def _(pool):
                norm.pool(pool)
                qn.pool(pool, QH, 64)
                kn.pool(pool, KVH, 64, T=TT)

            @block.scalar
            def _(act):
                norm.scalar_squares(act)
                for n in range(2):
                    copy_out(act, ACTE, ("g15", 0, n), g1[:, n * 512:(n + 1) * 512], 512)
                norm.evacuate(act, ACTE)
                for n in range(2):
                    for t in range(NT):
                        copy_out(act, ACTE, ("q5", n, t), q[:, t, n * 512:(n + 1) * 512], 512)
                to_qT.evacuate(act, ACTE)
                to_kT.evacuate(act, ACTE)
                att.scalar(act)

            @block.vector
            def _(dve):
                link = chain(dve, dve_step)
                norm.vector_scale(dve)
                norm.evacuate(dve, DVE)
                for t in range(TT):
                    b = banks["kv5", t]
                    dve.wait_ge(bank_full, b.full)
                    dve.tensor_copy(kk[:, t, :], b.ap[:, 0:256])
                    dve.tensor_copy(vv[:, t, :], b.ap[:, 256:512]).then_inc(emptied[DVE], 1)
                dve.wait_ge(emptied[ACTE], banks["q5", 1, NT - 1].done)
                dve.wait_ge(emptied[DVE], banks["kv5", TT - 1].done)
                qn.vector_sum(dve, link, qh, sq, QH, 64)
                qn.vector_scale(dve, link, qh, qh, [(0, QH, gain("attn_q_norm_w_2"))], QH, 64)
                rope(dve, link, qh, qh, tmp, QH, 32, 64, 0, cos2, sin2)
                dve.sem_inc(q_ready, 1)
                kn.vector_sum(dve, link, kh, sq[:, 0:16, :], KVH, 64, T=TT)
                kn.vector_scale(dve, link, kh, kh, [(0, KVH, gain("attn_k_norm_w_2"))], KVH, 64, T=TT)
                rope(dve, link, kh[:, NT:TT], kh[:, NT:TT], tmp, KVH, 32, 64, 0, cos2, sin2)
                dve.sem_inc(k_ready, 1)
                to_qT.evacuate(dve, DVE)
                to_kT.evacuate(dve, DVE)
                att.vector(dve, link)
                dve.wait_ge(emptied[ACTE], banks["g15", 0, 1].done)
                for t in range(NT):
                    for n in range(2):
                        c = slice(n * 512, (n + 1) * 512)
                        b = banks["ao5", t, n]
                        dve.wait_ge(bank_full, b.full)
                        dve.tensor_tensor(part[:, n, :], b.ap[:, :], g1[:, c], ALU.mult).then_inc(emptied[DVE], 1)
                        dve.wait_ge(emptied[DVE], b.done)
                        link(dve.tensor_tensor(X[:, t, c], X[:, t, c], part[:, n, :], ALU.add))

            @block.sync
            def _(sp):
                load_weights(sp)

        expert_choice(1)

        with ExitStack() as scope:
            fin = sb("fin", [P, D], scope=scope)
            y = sb("y_out", [P, NT, D], scope=scope)
            fin_loaded, f_squared, f_rooted, f_done, out_stored = (sem(x) for x in ("fin_loaded", "f_squared", "f_rooted", "f_done", "out_stored"))
            block = scope.enter_context(nc.Block())

            @block.scalar
            def _(act):
                for t in range(NT):
                    act.activation(y[:, t, :], X[:, t, :], ACT.Square, accum_out=eps_rows[:, t:t + 1]).then_inc(f_squared, 1)

            @block.gpsimd
            def _(pool):
                pool.wait_ge(f_squared, NT)
                root(pool, 0, NT, D, f_rooted)

            @block.vector
            def _(dve):
                link = chain(dve, dve_step)
                dve.wait_ge(f_rooted, 1)
                link(dve.tensor_scalar(rstd[:, 0:NT], rstd[:, 0:NT], float(D) ** 0.5, None, ALU.mult))
                dve.wait_ge(fin_loaded, 16)
                for t in range(NT):
                    dve.scalar_tensor_tensor(y[:, t, :], X[:, t, :], rstd[:, t:t + 1], fin[:, :],
                                             ALU.mult, ALU.mult).then_inc(f_done, 1)

            @block.sync
            def _(sp):
                sp.dma_start(fin[:, :], A["final_norm_w_2"].partition_broadcast(P)).then_inc(fin_loaded, 16)
                for t in range(NT):
                    sp.wait_ge(f_done, t + 1)
                    sp.dma_start(out["out"][0, t * P:(t + 1) * P, :], y[:, t, :]).then_inc(out_stored, 16)
                sp.wait_ge(out_stored, 16 * NT)



_CONST_TABLE = constant_table()
NAMES = ["x", "mem", "positions", "attn_norm_g", "w_in", "dsa_q_norm_g", "dsa_k_norm_g", "mla_cq_norm_g",
         "mla_ckv_norm_g", "mla_w_uq", "mla_w_ukv", "mla_q_norm_g", "mla_k_norm_g", "w_branch_dsa",
         "w_branch_mla", "w_out", "mem_x_norm_g", "mem_norm_g", "mem_w_q", "mem_w_kv", "mem_q_norm_g",
         "mem_k_norm_g", "mem_w_o", "moe_norm_g", "moe_w_group", "moe_w_expert", "moe_expert_bias",
         "moe_w_gate", "moe_w_up", "moe_w_down", "c_2", "ctx_2", "c_ctx_2", "ada_w_2", "ada_b_2",
         "norm1_w_2", "norm2_w_2", "ssd_in_w_2", "ssd_conv_w_2", "ssd_conv_b_2", "ssd_dt_bias_2",
         "ssd_A_log_2", "ssd_D_2", "ssd_norm_w_2", "ssd_out_w_2", "attn_qkv_w_2", "attn_q_norm_w_2",
         "attn_k_norm_w_2", "attn_out_w_2", "moe_router_w_2", "moe_w1_2", "moe_w3_2", "moe_w2_2",
         "final_norm_w_2"]


def kernel(**inputs):
    import concourse.bacc as bacc
    from concourse.bass_utils import run_bass_kernel_spmd

    nc = bacc.Bacc("TRN2", target_bir_lowering=False, num_devices=1)
    arrays = {"consts": _CONST_TABLE}
    for name in NAMES:
        arrays[name] = np.ascontiguousarray(inputs[name])
    A = {n: nc.dram_tensor("in_" + n, a.shape, mybir.dt.from_np(a.dtype), kind="ExternalInput").ap()
         for n, a in arrays.items()}
    out = {"out": nc.dram_tensor("out_x", (1, S, D), F32, kind="ExternalOutput").ap()}
    build(nc, A, out)
    r = run_bass_kernel_spmd(nc, [{"in_" + n: a for n, a in arrays.items()}], core_ids=[0])
    return r.results[0]["out_x"]
```

```python
import numpy as np
import concourse.bass as bass
from concourse import mybir
from contextlib import ExitStack

F32 = mybir.dt.float32
I32 = mybir.dt.int32
F32R = mybir.dt.float32r
ALU = mybir.AluOpType
ACT = mybir.ActivationFunctionType
AX = mybir.AxisListType

P = 128
D = 1024
KD = D // P
S = 256
NT = S // P
EPS = 1e-6
DSA_H, HD = 8, 64
MLA_H, MLA_QK, MLA_NOPE, MLA_ROPE, MLA_V = 8, 96, 64, 32, 64
MLA_QR, MLA_KVR = 256, 128
MEM_H = 4
N_IN = 3688
O_IQ, O_IW, O_CQ, O_CKV, O_KPE, O_GD, O_GM = 640, 1216, 1224, 1480, 1608, 1640, 2664
TOPK = 64
N_EXP, GROUPS, D_EXP = 16, 4, 256
NEG = -3.0e38
TAKEN = -3.3e38
BIG = 1.0e30

D_INNER, SSD_G, HPG, SSD_HD, D_STATE = 2048, 8, 4, 64, 128
SSD_H = SSD_G * HPG
GW = HPG * SSD_HD
CONV_W = 5
SSD_IN = 6208
O_XS, O_B, O_C, O_DT = 2048, 4096, 5120, 6144
QH, KVH, QPK = 16, 4, 4
CAP = 32

SLOTS, SLOT = 6, 4096

CONSTS = {}


def constant_table():
    p = np.arange(P)
    parts = {
        "ident": np.eye(P),
        "upto": p[:, None] <= p[None, :],
        "from": p[:, None] >= p[None, :],
        "ones": np.ones((P, P)),
        "causal": np.stack([(np.arange(S)[None, :] <= (p + t * P)[:, None]) for t in range(NT)], 1),
        "inv_freq": np.broadcast_to(np.concatenate([
            np.float32(10000.0) ** (-np.arange(32, dtype=np.float32) / np.float32(32)),
            np.float32(10000.0) ** (-np.arange(16, dtype=np.float32) / np.float32(16))]), (P, 48)),
        "down16": np.broadcast_to(np.arange(16, 0, -1), (P, 16)),
        "slot": np.broadcast_to(np.arange(CAP), (P, CAP)),
    }
    f = np.float32(10000.0) ** (-np.arange(0, 32, 2, dtype=np.float32) / np.float32(32))
    tok = p[:, None] + np.arange(NT)[None, :] * P
    ang = np.concatenate([(tok // 64)[..., None].astype(np.float32) * f,
                          (tok % 64)[..., None].astype(np.float32) * f], -1)
    parts["cos2d"], parts["sin2d"] = np.cos(ang), np.sin(ang)
    at, cols = 0, []
    for name, a in parts.items():
        a = np.asarray(a, np.float32).reshape(P, -1)
        CONSTS[name] = (at, at + a.shape[1])
        at += a.shape[1]
        cols.append(a)
    return np.ascontiguousarray(np.concatenate(cols, 1))


VECTORS = [
    (0, 0, "attn_norm_g", 8), (0, 8, "mem_x_norm_g", 8), (0, 16, "mem_norm_g", 8), (0, 24, "moe_norm_g", 8),
    (0, 32, "norm1_w_2", 16), (0, 48, "norm2_w_2", 16), (0, 64, "ssd_norm_w_2", 16),
    (0, 80, "mla_cq_norm_g", 2), (0, 82, "mla_ckv_norm_g", 1), (0, 83, "c_2", 8), (0, 91, "c_ctx_2", 8),
    (1, 0, "ssd_conv_w_2", 128), (2, 0, "ssd_conv_w_2", 32), (2, 32, "ssd_conv_b_2", 32),
    (3, 0, "ada_b_2", 96)]
VCOL = {name: tile * P + row for tile, row, name, _ in VECTORS if not (name == "ssd_conv_w_2" and tile == 2)}

DVE, ACTE = "dve", "act"


class Bank:

    def __init__(self, ap, full, by, done, emptied):
        self.ap, self.full, self.by, self.done, self.emptied = ap, full, by, done, emptied


class Banks:

    def __init__(self, psum, emptied):
        self.psum, self.sem = psum, emptied
        self.order, self.names, self.count = [], {}, {k: 0 for k in emptied}

    def open(self, name, by):
        n = len(self.order)
        self.count[by] += 1
        before = None
        if n >= 8:
            b = self.order[n - 8]
            before = (self.sem[b.by], b.done)
        bank = Bank(self.psum[n % 8], n + 1, by, self.count[by], before)
        self.order.append(bank)
        assert name not in self.names, name
        self.names[name] = bank
        return bank

    def __getitem__(self, name):
        return self.names[name]


class Piece:

    def __init__(self, ap, sem, full, before):
        self.ap, self.sem, self.full = ap, sem, full
        self.before = before
        self.freed = None


class Ring:

    def __init__(self, slots, loaded):
        self.slots, self.loaded = slots, loaded
        self.total = [0] * SLOTS
        self.last = [None] * SLOTS
        self.pieces = {}

    def add(self, name, slot, dmas=1):
        self.total[slot] += 16 * dmas
        piece = Piece(self.slots[:, slot, :], self.loaded[slot], self.total[slot], self.last[slot])
        self.pieces[name] = self.last[slot] = piece
        return piece

    def __getitem__(self, name):
        return self.pieces[name]


def build(nc, A, out):
    ctx = ExitStack()
    sem_names = set()

    def sem(name):
        assert name not in sem_names, name
        sem_names.add(name)
        return ctx.enter_context(nc.semaphore(name))

    def sb(name, shape, dt=F32, scope=None):
        return (scope or ctx).enter_context(nc.sbuf_tensor(name, shape, dt))

    def flat(name):
        a = A[name]
        return a.rearrange("a b -> (a b)") if len(a.shape) == 2 else a.rearrange("a b c -> (a b c)") if len(a.shape) == 3 else a

    with ctx:
        slots_base = (nc.sbuf_base + 31) // 32 * 32
        slots = sb("slots", [P, SLOTS, SLOT])
        slots_r = nc.alloc_sbuf_tensor_at("slots_r", [P, SLOTS, SLOT], F32R, offset=slots_base)
        X = sb("X", [P, NT, D])
        C = sb("C", [P, NT, D])
        consts = sb("consts", [P, CONSTS["sin2d"][1]])
        vcols = sb("vcols", [P, 4 * P])
        modcol = sb("modcol", [P, 2, 12, 4, 2])
        eps_rows = sb("eps_rows", [P, 64])
        rstd = sb("rstd", [P, 64])
        minus_half = sb("minus_half", [P, 64])
        ncol = sb("ncol", [P, 2, 2, 2, KD])
        scT = sb("scT", [P, KD, 32])
        routers = sb("routers", [P, 2, KD, N_EXP])
        psum = [ctx.enter_context(nc.psum_tensor(f"bank{i}", [P, 512], F32)) for i in range(8)]

        def const(name):
            a, b = CONSTS[name]
            return consts[:, a:b]

        ident = const("ident")

        bank_full = sem("bank_full")
        emptied = {DVE: sem("emptied_by_dve"), ACTE: sem("emptied_by_act")}
        banks = Banks(psum, emptied)
        slot_loaded = [sem(f"slot_loaded{i}") for i in range(SLOTS)]
        ring = Ring(slots, slot_loaded)
        stored = sem("stored")
        routers_loaded = sem("routers_loaded")
        dve_step, act_step, pool_step = sem("dve_step"), sem("act_step"), sem("pool_step")
        steps = {}

        def chain(eng, own):
            def link(ins):
                steps[own.name] = steps.get(own.name, 0) + 1
                ins.then_inc(own, 1)
                eng.wait_ge(own, steps[own.name])
            return link

        def w(name, k, n, c0, c1, k0=0, k1=None):
            return A[name].rearrange("(k p) n -> p k n", p=P)[:, k0:k1 or k, c0:c1]

        stream = []

        def weights(name, parts, among=SLOTS):
            slot = 0 if not stream else (stream[-1][2] + 1) % among
            piece = ring.add(name, slot, len(parts))
            stream.append((piece, parts, slot))

        def view(piece, at, k, n):
            return piece.ap[:, at:at + k * n].rearrange("p (k n) -> p k n", n=n)

        w_in = A["w_in"].rearrange("a r c -> (a r) c").rearrange("(k p) n -> p k n", p=P)
        def rows(name):
            return A[name].rearrange("a r c -> (a r) c").rearrange("(k p) n -> p k n", p=P)
        CI = N_IN // 8
        for n in range(8):
            weights(("in", n), [(0, KD, CI, w_in[:, :, n * CI:(n + 1) * CI])])
        ada_v = A["ada_w_2"].rearrange("l (k p) (c n) -> p l c k n", p=P, n=512)
        ADA = 3
        ada_at = [0]

        def ada_weights():
            for c in range(ada_at[0], ada_at[0] + ADA):
                weights(("ada", c), [(0, KD, 512, ada_v[:, c // 12, c % 12])])
            ada_at[0] += ADA

        ada_weights()
        ada_weights()
        ada_weights()
        weights("mla", [(0, 2, 768, rows("mla_w_uq")), (1536, 1, 1024, rows("mla_w_ukv"))])
        ada_weights()
        weights("br_dsa", [(0, 4, D, rows("w_branch_dsa"))])
        weights("br_mla", [(0, 4, D, rows("w_branch_mla"))])
        for h in range(2):
            weights(("w_out", h), [(0, 4, D, rows("w_out")[:, 4 * h:4 * h + 4, :])])
        ada_weights()
        weights("mem_q", [(0, KD, 256, rows("mem_w_q"))])
        weights("mem_kv", [(0, KD, 512, rows("mem_w_kv"))])
        ada_weights()
        weights("mem_o", [(0, 2, D, rows("mem_w_o"))])
        ada_weights()
        ada_weights()
        gate_v = A["moe_w_gate"].rearrange("a e (k p) n -> p (a e) k n", p=P)
        up_v = A["moe_w_up"].rearrange("a e (k p) n -> p (a e) k n", p=P)
        down_v = A["moe_w_down"].rearrange("a e (k p) n -> p (a e) k n", p=P)
        weights(("moe1", 0), [(0, KD, D_EXP, gate_v[:, 0]), (2048, KD, D_EXP, up_v[:, 0])], among=3)
        weights(("moe1", 1), [(0, KD, D_EXP, gate_v[:, 1]), (2048, KD, D_EXP, up_v[:, 1])], among=3)
        weights(("moe1", 2), [(2048 * i, 2, D, down_v[:, i]) for i in range(2)], among=3)
        MOE1_SLOTS = [stream[-3 + j][2] for j in range(3)]
        scratch_use = Piece(None, None, 0, None)
        for slot in range(3, SLOTS):
            ring.last[slot] = scratch_use
        ssd_v = rows("ssd_in_w_2")
        weights("dt", [(0, KD, 64, ssd_v[:, :, O_DT:])], among=3)
        for g in range(SSD_G):
            weights(("grp", g), [(0, KD, 256, ssd_v[:, :, O_XS + g * 256:O_XS + (g + 1) * 256]),
                                 (2048, KD, 128, ssd_v[:, :, O_B + g * 128:O_B + (g + 1) * 128]),
                                 (3072, KD, 128, ssd_v[:, :, O_C + g * 128:O_C + (g + 1) * 128])], among=3)
        for n in range(4):
            weights(("z", n), [(0, KD, 512, ssd_v[:, :, n * 512:(n + 1) * 512])], among=3)
        for n in range(4):
            weights(("ssd_out", n), [(0, 4, D, rows("ssd_out_w_2")[:, 4 * n:4 * n + 4, :])], among=3)
        w_v = [A[f"moe_w{m}_2"].rearrange("l e (k p) n -> p (l e) k n", p=P) for m in (1, 3, 2)]

        def moe2_weights(l):
            for j in range(6):
                weights(("moe2", l, j), [(0, 4, D, w_v[j // 2][:, l * N_EXP, 4 * (j % 2):4 * (j % 2) + 4])])
            for j in range(6):
                ring.total[stream[-1 - j][2]] += 16 * (N_EXP - 1)

        moe2_weights(0)
        for n in (2, 0, 1):
            weights(("qkv", n), [(0, KD, 512, rows("attn_qkv_w_2")[:, :, n * 512:(n + 1) * 512])])
        for n in range(2):
            weights(("attn_out", n), [(0, 4, D, rows("attn_out_w_2")[:, 4 * n:4 * n + 4, :])])
        moe2_weights(1)
        issued = [0]

        def load_weights(sp, upto=1000):
            while issued[0] < min(upto, len(stream)):
                piece, parts, _ = stream[issued[0]]
                if piece.before is not None:
                    if piece.before.freed is None:
                        return
                    sp.wait_ge(*piece.before.freed)
                for at, k, n, src in parts:
                    sp.dma_start(view(piece, at, k, n), src).then_inc(piece.sem, 16)
                issued[0] += 1

        def root(pool, at, n, width, done=None):
            link = chain(pool, pool_step)
            c = slice(at, at + n)
            link(pool.tensor_scalar(rstd[:, c], eps_rows[:, c], float(width * EPS), None, ALU.add))
            i = pool.tensor_tensor(rstd[:, c], rstd[:, c], minus_half[:, 0:n], ALU.pow)
            if done is not None:
                i.then_inc(done, 1)

        ld = {k: sem("ld_" + k) for k in ("consts", "vec", "x", "misc", "pos")}
        vrow_zeroed = sem("vrow_zeroed")
        trig_ready = sem("trig_ready")
        cs = sb("cs", [P, 2, NT, 48])
        MISC = ["dsa_q_norm_g", "dsa_k_norm_g", "mla_q_norm_g", "mla_k_norm_g", "mem_q_norm_g", "mem_k_norm_g",
                "moe_expert_bias", "attn_q_norm_w_2", "attn_k_norm_w_2", "ssd_D_2", "ssd_dt_bias_2", "ssd_A_log_2"]
        GAIN, at = {}, 0
        for name in MISC:
            n = int(np.prod(A[name].shape))
            GAIN[name] = (at, at + n)
            at += n
        gains = sb("gains", [P, at])

        def gain(name):
            a, b = GAIN[name]
            return gains[:, a:b]

        with ExitStack() as scope:
            vrows = sb("vrows", [P, 4, P], scope=scope)
            pos_i = sb("pos_i", [P, NT], I32, scope)
            pos_f = sb("pos_f", [P, NT], scope=scope)
            ang = sb("ang", [P, NT, 48], scope=scope)
            turns = sb("turns", [P, NT, 48], scope=scope)
            half_sin = sb("half_sin", [P, NT, 48], scope=scope)
            block = scope.enter_context(nc.Block())

            @block.sync
            def _(sp):
                sp.dma_start(X[:, :, :], A["x"].rearrange("b (t p) d -> p (b t) d", p=P)).then_inc(ld["x"], 16)
                sp.dma_start(consts[:, :], A["consts"]).then_inc(ld["consts"], 16)
                sp.dma_start(pos_i[:, :], A["positions"].rearrange("b (t p) -> p (b t)", p=P),
                             allow_slow_non_contiguous=True).then_inc(ld["pos"], 16)
                load_weights(sp, 2)
                sp.wait_ge(vrow_zeroed, 1)
                for tile, row, name, n in VECTORS:
                    src = flat(name).rearrange("(r c) -> r c", c=P)
                    if name == "ssd_conv_w_2" and tile == 2:
                        src = src[P:, :]
                    sp.dma_start(vrows[row:row + n, tile, :], src[0:n, :]).then_inc(ld["vec"], 16)
                for name in MISC:
                    a, b = GAIN[name]
                    sp.dma_start(gains[:, a:b], flat(name).partition_broadcast(P)).then_inc(ld["misc"], 16)
                load_weights(sp)
                sp.wait_ge(ld["misc"], 16 * len(MISC))
                sp.wait_ge(ld["x"], 16)

            @block.gpsimd
            def _(pool):
                pool.memset(minus_half[:, :], -0.5)
                pool.memset(scT[:, :, :], 0.0)

            @block.tensor
            def _(pe):
                pe.wait_ge(ld["consts"], 16)
                pe.wait_ge(ld["vec"], 16 * len(VECTORS))
                b = banks.open("vec", DVE)
                for t in range(4):
                    ins = pe.transpose(b.ap[:, t * P:(t + 1) * P], vrows[:, t, :], ident)
                ins.then_inc(bank_full, 1)

            @block.vector
            def _(dve):
                link = chain(dve, dve_step)
                dve.memset(vrows[:, :, :], 0.0).then_inc(vrow_zeroed, 1)
                dve.wait_ge(ld["pos"], 16)
                dve.wait_ge(ld["consts"], 16)
                link(dve.tensor_copy(pos_f[:, :], pos_i[:, :]))
                for t in range(NT):
                    i = dve.tensor_scalar(ang[:, t, :], const("inv_freq"), pos_f[:, t:t + 1], None, ALU.mult)
                link(i)
                link(dve.tensor_scalar(turns[:, :, :], ang[:, :, :], float(1 / (2 * np.pi)), 12582912.0,
                                       ALU.mult, ALU.add))
                link(dve.tensor_scalar(turns[:, :, :], turns[:, :, :], 12582912.0, None, ALU.subtract))
                first = 6.28125
                second = float(np.round((2 * np.pi - first) * 2**20) / 2**20)
                for part in (first, second, float(np.float32(2 * np.pi - first - second))):
                    link(dve.scalar_tensor_tensor(ang[:, :, :], turns[:, :, :], -part, ang[:, :, :],
                                                  ALU.mult, ALU.add))
                link(dve.tensor_scalar(ang[:, :, :], ang[:, :, :], 3.1415925, -3.1415925, ALU.min, ALU.max))
                link(dve.tensor_scalar(turns[:, :, :], ang[:, :, :], 0.5, None, ALU.mult))
                dve.tensor_copy(cs[:, 1, :, :], ang[:, :, :]).then_inc(trig_ready, 1)
                b = banks["vec"]
                dve.wait_ge(bank_full, b.full)
                dve.tensor_copy(vcols[:, :], b.ap[:, :]).then_inc(emptied[b.by], 1)
                dve.wait_ge(trig_ready, 3)
                link(dve.tensor_tensor(half_sin[:, :, :], half_sin[:, :, :], half_sin[:, :, :], ALU.mult))
                dve.tensor_scalar(cs[:, 0, :, :], half_sin[:, :, :], -2.0, 1.0, ALU.mult, ALU.add).then_inc(trig_ready, 1)

            @block.scalar
            def _(act):
                act.wait_ge(trig_ready, 1)
                act.activation(cs[:, 1, :, :], ang[:, :, :], ACT.Sin).then_inc(trig_ready, 1)
                act.activation(half_sin[:, :, :], turns[:, :, :], ACT.Sin).then_inc(trig_ready, 1)

        def cos(rope):
            return cs[:, 0, :, 0:32] if rope == 32 else cs[:, 0, :, 32:48]

        def sin(rope):
            return cs[:, 1, :, 0:32] if rope == 32 else cs[:, 1, :, 32:48]

        normed, squared, rooted = sem("normed"), sem("squared"), sem("rooted")
        heads_summed, heads_rooted = sem("heads_summed"), sem("heads_rooted")
        counted = {"streams": 0, "norms": 0, "head_norms": 0, "ada": 0}

        class NormT:

            def __init__(self, tag, srcs, xn, hT, gain_col, bias_col=None):
                self.tag, self.srcs, self.xn, self.hT = tag, srcs, xn, hT
                self.gain_col, self.bias_col = gain_col, bias_col
                self.T = len(srcs)
                self.before, self.nth = counted["streams"], counted["norms"] + 1
                counted["streams"] += self.T
                counted["norms"] += 1

            def scalar_squares(self, act):
                for t, src in enumerate(self.srcs):
                    act.activation(self.xn[:, t, :], src, ACT.Square,
                                   accum_out=eps_rows[:, t:t + 1]).then_inc(squared, 1)

            def pool(self, pool):
                pool.wait_ge(squared, self.before + self.T)
                root(pool, 0, self.T, D, rooted)

            def vector_scale(self, dve):
                dve.wait_ge(rooted, self.nth)
                for t, src in enumerate(self.srcs):
                    dve.tensor_scalar(self.xn[:, t, :], src, rstd[:, t:t + 1], float(D) ** 0.5,
                                      ALU.mult, ALU.mult).then_inc(normed, 1)

            def per_bank(self):
                return 4 // self.T

            def tensor(self, pe):
                pe.wait_ge(normed, self.before + self.T)
                m = self.per_bank()
                for n in range(KD // m):
                    b = banks.open((self.tag, n), (DVE, ACTE)[n % 2])
                    if b.emptied:
                        pe.wait_ge(*b.emptied)
                    for j in range(m):
                        for t in range(self.T):
                            k = n * m + j
                            i = pe.transpose(b.ap[:, (j * self.T + t) * P:(j * self.T + t + 1) * P],
                                             self.xn[:, t, k * P:(k + 1) * P], ident)
                    i.then_inc(bank_full, 1)

            def evacuate(self, eng, by):
                m = self.per_bank()
                W = self.T * P
                for n in range(KD // m):
                    b = banks[self.tag, n]
                    if b.by != by:
                        continue
                    eng.wait_ge(bank_full, b.full)
                    for j in range(m):
                        k = n * m + j
                        src = b.ap[:, j * W:(j + 1) * W]
                        segs = self.gain_col(k)
                        for a, z, g, bias in segs:
                            if by == DVE:
                                if bias is None:
                                    i = eng.tensor_scalar(self.hT[:, k, a:z], src[:, a:z], g, None, ALU.mult)
                                else:
                                    i = eng.tensor_scalar(self.hT[:, k, a:z], src[:, a:z], g, bias, ALU.mult, ALU.add)
                            else:
                                i = eng.activation(self.hT[:, k, a:z], src[:, a:z], ACT.Identity, scale=g,
                                                   **({} if bias is None else {"bias": bias}))
                    i.then_inc(emptied[by], 1)

            def wait_chunk(self, pe, k):
                b = banks[self.tag, k // self.per_bank()]
                pe.wait_ge(emptied[b.by], b.done)

        def split_high(dve, high, x):
            return dve.tensor_copy(high, x)

        def split_low(dve, low, x, high):
            return dve.tensor_tensor(low, x, high.bitcast(F32), ALU.subtract)

        def matmul_split(pe, out, lhsT, rhs, start, stop):
            pe.matmul(out, lhsT[0], rhs[1], start=start, stop=False, skip_group_check=True)
            pe.matmul(out, lhsT[0], rhs[0], start=False, stop=False, skip_group_check=True)
            return pe.matmul(out, lhsT[1], rhs[0], start=False, stop=stop, skip_group_check=True)

        def plain_gain(name, first=0, W=S):
            c = VCOL[name] + first
            return lambda k: [(0, W, vcols[:, c + k:c + k + 1], None)]

        class Transpose:

            def __init__(self, tag, src, n, width, dst, gain=None, by=(DVE, ACTE), tiles=NT):
                self.tag, self.src, self.n, self.width, self.dst, self.gain, self.by = tag, src, n, width, dst, gain, by
                self.T = tiles
                self.per = 4 // tiles

            def groups(self):
                return [(g, range(g, min(g + self.per, self.n))) for g in range(0, self.n, self.per)]

            def tensor(self, pe):
                for q, (g, blocks) in enumerate(self.groups()):
                    b = banks.open((self.tag, g), self.by[q % len(self.by)])
                    if b.emptied:
                        pe.wait_ge(*b.emptied)
                    for j, n in enumerate(blocks):
                        for t in range(self.T):
                            i = pe.transpose(b.ap[0:self.width, (j * self.T + t) * P:(j * self.T + t + 1) * P],
                                             self.src(n, t), ident)
                    i.then_inc(bank_full, 1)

            def evacuate(self, eng, by):
                W = self.T * P
                for g, blocks in self.groups():
                    b = banks[self.tag, g]
                    if b.by != by:
                        continue
                    eng.wait_ge(bank_full, b.full)
                    m = len(blocks)
                    if self.gain is None:
                        src = b.ap[0:self.width, 0:m * W].rearrange("p (m w) -> p m w", m=m)
                        if by == DVE:
                            i = eng.tensor_copy(self.dst(g, m), src)
                        else:
                            i = eng.activation(self.dst(g, m), src, ACT.Copy)
                    else:
                        for j, n in enumerate(blocks):
                            src = b.ap[0:self.width, j * W:(j + 1) * W].rearrange("p (m w) -> p m w", m=1)
                            if by == DVE:
                                i = eng.tensor_scalar(self.dst(n, 1), src, self.gain(n), None, ALU.mult)
                            else:
                                i = eng.activation(self.dst(n, 1), src, ACT.Identity, scale=self.gain(n))
                    i.then_inc(emptied[by], 1)

            def wait_all(self, pe):
                for g, _ in self.groups()[-len(self.by):]:
                    b = banks[self.tag, g]
                    pe.wait_ge(emptied[b.by], b.done)

        def gemm(pe, tag, lhsT, K, T, rhs, width, by, wait_k=None, first=None, last=None):
            b = banks.open(tag, by)
            if b.emptied:
                pe.wait_ge(*b.emptied)
            for k in range(K):
                i = pe.matmul(b.ap[:, 0:width], lhsT(k), rhs(k), start=(k == 0), stop=(k == K - 1))
            i.then_inc(bank_full, 1)
            return b, i

        def copy_out(eng, by, tag, dst, width):
            b = banks[tag]
            if b.by != by:
                return
            eng.wait_ge(bank_full, b.full)
            if by == DVE:
                i = eng.tensor_copy(dst, b.ap[:, 0:width])
            else:
                i = eng.activation(dst, b.ap[:, 0:width], ACT.Copy)
            i.then_inc(emptied[by], 1)

        def rope(dve, link, dst, src, tmp, H, half, width, off, c, s):
            for t in range(NT):
                x1 = src[:, t, :, off:off + half]
                x2 = src[:, t, :, off + half:off + 2 * half]
                y1 = dst[:, t, :, off:off + half]
                y2 = dst[:, t, :, off + half:off + 2 * half]
                cb = c[:, t, :].unsqueeze(1).broadcast_to([P, H, half])
                sbb = s[:, t, :].unsqueeze(1).broadcast_to([P, H, half])
                dve.tensor_tensor(tmp[:, 0, 0:H, 0:half], x1, sbb, ALU.mult)
                dve.tensor_tensor(tmp[:, 1, 0:H, 0:half], x2, sbb, ALU.mult)
                dve.tensor_tensor(y1, x1, cb, ALU.mult)
                link(dve.tensor_tensor(y2, x2, cb, ALU.mult))
                dve.tensor_tensor(y1, y1, tmp[:, 1, 0:H, 0:half], ALU.subtract)
                link(dve.tensor_tensor(y2, y2, tmp[:, 0, 0:H, 0:half], ALU.add))

        class HeadNorm:

            def __init__(self, tag):
                counted["head_norms"] += 1
                self.nth = counted["head_norms"]

            def vector_sum(self, dve, link, src, sq, H, width, T=NT):
                n = T * H
                link(dve.tensor_tensor(sq, src, src, ALU.mult))
                dve.tensor_reduce(eps_rows[:, 0:n], sq, AX.X, ALU.add).then_inc(heads_summed, 1)

            def pool(self, pool, H, width, T=NT):
                n = T * H
                pool.wait_ge(heads_summed, self.nth)
                root(pool, 0, n, width, heads_rooted)

            def vector_scale(self, dve, link, dst, src, gains_of, H, width, T=NT):
                dve.wait_ge(heads_rooted, self.nth)
                n = T * H
                link(dve.tensor_scalar(rstd[:, 0:n], rstd[:, 0:n], float(width) ** 0.5, None, ALU.mult))
                for t in range(T):
                    r = rstd[:, t * H:(t + 1) * H].unsqueeze(2).broadcast_to([P, H, width])
                    i = dve.tensor_tensor(dst[:, t, :, :], src[:, t, :, :], r, ALU.mult)
                link(i)
                for t in range(T):
                    for a, z, g in gains_of:
                        gb = g.unsqueeze(1).broadcast_to([P, z - a, width])
                        i = dve.tensor_tensor(dst[:, t, a:z, :], dst[:, t, a:z, :], gb, ALU.mult)
                link(i)

        class Attention:
            RING, LAG = 4, 3

            def __init__(self, tag, heads, qT, kT, v, keys, scale, outT, bufs, bias=None):
                self.tag, self.heads, self.qT, self.kT, self.v, self.keys = tag, heads, qT, kT, v, keys
                self.scale, self.outT, self.bias = scale, outT, bias
                self.KT = keys // P
                self.hp = 512 // keys
                self.items = [(t, h) for h in range(0, heads, self.hp) for t in range(NT)]
                self.per_pair = 2 * NT // self.hp
                self.probs, self.pT, self.negmax, self.sums = bufs
                self.max_ready, self.scaled = sem("max_ready_" + tag), sem("scaled_" + tag)
                self.exped = sem("exped_" + tag) if bias is not None else None

            def wait_exped(self, eng, n):
                if self.bias is None:
                    eng.wait_ge(emptied[ACTE], banks[self.tag, "qk", n].done)
                else:
                    eng.wait_ge(self.exped, n + 1)

            def wait_transposed(self, eng, n):
                eng.wait_ge(bank_full, banks[self.tag, "pT", n].full)

            def pair_done(self, m):
                return m // self.per_pair if m >= 0 and m % self.per_pair == self.per_pair - 1 else None

            def tensor(self, pe):
                N, LAG = len(self.items), self.LAG
                for i in range(N + LAG + 1):
                    if i < N:
                        t, h = self.items[i]
                        b = banks.open((self.tag, "qk", i), ACTE if self.bias is None else DVE)
                        if b.emptied:
                            pe.wait_ge(*b.emptied)
                        for j in range(self.hp):
                            ins = pe.matmul(b.ap[:, j * self.keys:(j + 1) * self.keys],
                                            self.qT(h + j)[:, t * P:(t + 1) * P], self.kT(h + j),
                                            start=True, stop=True)
                        ins.then_inc(bank_full, 1)
                    n = i - LAG
                    if 0 <= n < N:
                        b = banks.open((self.tag, "pT", n), ACTE)
                        if b.emptied:
                            pe.wait_ge(*b.emptied)
                        pe.wait_ge(self.scaled, n + 1)
                        for c in range(0, 512, P):
                            ins = pe.transpose(b.ap[:, c:c + P], self.probs[:, n % self.RING, c:c + P], ident)
                        ins.then_inc(bank_full, 1)
                    p = self.pair_done(n - 1)
                    if p is not None:
                        o = banks.open((self.tag, "pv", p), DVE)
                        if o.emptied:
                            pe.wait_ge(*o.emptied)
                        pe.wait_ge(emptied[ACTE], banks[self.tag, "pT", n - 1].done)
                        for kt in range(self.KT):
                            for j in range(2):
                                c = (j * self.KT + kt) * S
                                ins = pe.matmul(o.ap[64 * j:64 * j + 64, 0:S], self.v(2 * p + j, kt),
                                                self.pT[p % 2][:, c:c + S], start=(kt == 0), stop=(kt == self.KT - 1),
                                                tile_position=(0, 64 * j), skip_group_check=True)
                        ins.then_inc(bank_full, 1)

            def vector(self, dve, link):
                N, LAG = len(self.items), self.LAG
                hp, K = self.hp, self.keys
                for i in range(N + LAG + 1):
                    if i < N:
                        t, h = self.items[i]
                        b = banks[self.tag, "qk", i]
                        dve.wait_ge(bank_full, b.full)
                        L = b.ap[:, 0:hp * K].rearrange("p (h k) -> p h k", h=hp)
                        mx = self.negmax[:, i * hp:(i + 1) * hp]
                        if self.bias is None:
                            link(dve.tensor_reduce(mx, L, AX.X, ALU.max))
                            dve.tensor_scalar(mx, mx, -self.scale, None, ALU.mult).then_inc(self.max_ready, 1)
                        else:
                            if i >= self.RING:
                                self.wait_transposed(dve, i - self.RING)
                            B = self.probs[:, i % self.RING, :].rearrange("p (h k) -> p h k", h=hp)
                            bb = self.bias(t).unsqueeze(1).broadcast_to([P, hp, K])
                            dve.scalar_tensor_tensor(B, L, self.scale, bb, ALU.mult, ALU.add).then_inc(emptied[DVE], 1)
                            dve.wait_ge(emptied[DVE], b.done)
                            dve.tensor_reduce(mx, B, AX.X, ALU.max, negate=True).then_inc(self.max_ready, 1)
                    n = i - 1
                    if 0 <= n < N:
                        self.wait_exped(dve, n)
                        s = self.sums[:, n * hp:(n + 1) * hp]
                        link(dve.reciprocal(s, s))
                        for j in range(hp):
                            B = self.probs[:, n % self.RING, j * K:(j + 1) * K]
                            ins = dve.tensor_scalar(B, B, s[:, j:j + 1], None, ALU.mult)
                        ins.then_inc(self.scaled, 1)
                    p = self.pair_done(i - LAG - 1)
                    if p is not None:
                        o = banks[self.tag, "pv", p]
                        dve.wait_ge(bank_full, o.full)
                        dve.tensor_copy(self.outT(p), o.ap[:, 0:S]).then_inc(emptied[DVE], 1)

            def scalar(self, act):
                N = len(self.items)
                hp, K = self.hp, self.keys
                for i in range(N + self.LAG):
                    if i < N:
                        b = banks[self.tag, "qk", i]
                        act.wait_ge(self.max_ready, i + 1)
                        if self.bias is None and i >= self.RING:
                            self.wait_transposed(act, i - self.RING)
                        for j in range(hp):
                            c = i * hp + j
                            B = self.probs[:, i % self.RING, j * K:(j + 1) * K]
                            if self.bias is None:
                                ins = act.activation(B, b.ap[:, j * K:(j + 1) * K], ACT.Exp, scale=self.scale,
                                                     bias=self.negmax[:, c:c + 1], accum_out=self.sums[:, c:c + 1])
                                if j == hp - 1:
                                    ins.then_inc(emptied[ACTE], 1)
                            else:
                                ins = act.activation(B, B, ACT.Exp, bias=self.negmax[:, c:c + 1],
                                                     accum_out=self.sums[:, c:c + 1])
                                if j == hp - 1:
                                    ins.then_inc(self.exped, 1)
                    n = i - self.LAG
                    if n >= 0:
                        t, h = self.items[n]
                        p = n // self.per_pair
                        b = banks[self.tag, "pT", n]
                        act.wait_ge(bank_full, b.full)
                        if p >= 2:
                            act.wait_ge(bank_full, banks[self.tag, "pv", p - 2].full)
                        j = h % 2
                        dst = self.pT[p % 2].rearrange("p (c q) -> p c q", q=S)[:, j * self.KT:(j + hp) * self.KT, t * P:(t + 1) * P]
                        act.activation(dst, b.ap[:, :].rearrange("p (c q) -> p c q", q=P), ACT.Copy).then_inc(emptied[ACTE], 1)

        class Ada:

            def __init__(self, buf):
                self.buf = buf
                self.pieces = range(counted["ada"], counted["ada"] + ADA)
                counted["ada"] += ADA

            def tensor(self, pe):
                def back(c):
                    a = banks["ada", c]
                    b = banks.open(("adaT", c), DVE)
                    if b.emptied:
                        pe.wait_ge(*b.emptied)
                    pe.wait_ge(emptied[ACTE], a.done)
                    for m in range(4):
                        i = pe.transpose(b.ap[:, m * P:(m + 1) * P], self.buf[:, c % 2, m * P:(m + 1) * P], ident)
                    i.then_inc(bank_full, 1)

                for c in self.pieces:
                    piece = ring["ada", c]
                    pe.wait_ge(piece.sem, piece.full)
                    b = banks.open(("ada", c), ACTE)
                    if b.emptied:
                        pe.wait_ge(*b.emptied)
                    wv = view(piece, 0, KD, 512)
                    for kk in range(2):
                        for j in range(4):
                            i = pe.matmul(b.ap[32 * j:32 * j + 32, :], scT[:, 2 * j + kk, :], wv[:, 2 * j + kk, :],
                                          start=(kk == 0), stop=(kk == 1), tile_position=(0, 32 * j), skip_group_check=True)
                    i.then_inc(bank_full, 1)
                    piece.freed = (bank_full, b.full)
                    if c > self.pieces[0]:
                        back(c - 1)
                back(self.pieces[-1])

            def scalar(self, act):
                for c in self.pieces:
                    b = banks["ada", c]
                    act.wait_ge(bank_full, b.full)
                    if c >= self.pieces[0] + 2:
                        act.wait_ge(bank_full, banks["adaT", c - 2].full)
                    act.activation(self.buf[:, c % 2, :], b.ap[:, :], ACT.Copy).then_inc(emptied[ACTE], 1)

            def vector(self, dve):
                for c in self.pieces:
                    b = banks["adaT", c]
                    dve.wait_ge(bank_full, b.full)
                    dve.tensor_reduce(modcol[:, c // 12, c % 12, :, :],
                                      b.ap[:, :].rearrange("p (b j r) -> p b r j", b=4, j=4)[:, :, 0:2, :],
                                      AX.X, ALU.add).then_inc(emptied[DVE], 1)

        hT_base = (nc.sbuf_base + 31) // 32 * 32
        hT = sb("hT", [P, KD, 2 * S])
        hT_r = nc.alloc_sbuf_tensor_at("hT_r", [P, KD, 2 * S], F32R, offset=hT_base)
        mix = ExitStack()
        proj = sb("proj", [P, NT, N_IN], scope=mix)
        with ExitStack() as scope:
            xn = sb("xn", [P, NT, D], scope=scope)
            norm = NormT("n1", [X[:, t, :] for t in range(NT)], xn, hT, plain_gain("attn_norm_g"))
            block = scope.enter_context(nc.Block())

            @block.tensor
            def _(pe):
                norm.tensor(pe)
                for n in range(8):
                    piece = ring["in", n]
                    pe.wait_ge(piece.sem, piece.full)
                    wv = view(piece, 0, KD, CI)
                    for t in range(NT):
                        b = banks.open(("proj", n, t), (DVE, ACTE)[t])
                        if b.emptied:
                            pe.wait_ge(*b.emptied)
                        for k in range(KD):
                            if n == 0 and t == 0:
                                norm.wait_chunk(pe, k)
                            i = pe.matmul(b.ap[:, 0:CI], hT[:, k, t * P:(t + 1) * P], wv[:, k, :],
                                          start=(k == 0), stop=(k == KD - 1))
                        i.then_inc(bank_full, 1)
                    piece.freed = (bank_full, b.full)

            @block.sync
            def _(sp):
                for l in range(2):
                    sp.dma_start(routers[:, l], A["moe_router_w_2"][l].rearrange("(k p) n -> p k n", p=P)).then_inc(routers_loaded, 16)
                load_weights(sp)

            @block.gpsimd
            def _(pool):
                norm.pool(pool)

            @block.vector
            def _(dve):
                norm.vector_scale(dve)
                norm.evacuate(dve, DVE)
                for n in range(8):
                    copy_out(dve, DVE, ("proj", n, 0), proj[:, 0, n * CI:(n + 1) * CI], CI)

            @block.scalar
            def _(act):
                norm.scalar_squares(act)
                for s_, name in enumerate(("c_2", "c_ctx_2")):
                    act.activation(scT[:, :, s_], vcols[:, VCOL[name]:VCOL[name] + KD], ACT.Silu)
                norm.evacuate(act, ACTE)
                for n in range(8):
                    copy_out(act, ACTE, ("proj", n, 1), proj[:, 1, n * CI:(n + 1) * CI], CI)

        def heads(buf, off, H, width):
            return buf[:, :, off:off + H * width].rearrange("p t (h d) -> p t h d", d=width)

        spare = C[:, :, :].rearrange("p t d -> p (t d)")
        probs = spare.rearrange("p (n k) -> p n k", n=4)
        negmax, sums = sb("negmax", [P, 32], scope=mix), sb("sums", [P, 32], scope=mix)
        outA = sb("outA", [P, 4, S], scope=mix)
        outB = sb("outB", [P, 4, S], scope=mix)
        attn_bias = sb("attn_bias", [P, NT, S], scope=mix)
        causal = const("causal").rearrange("p (t k) -> p t k", t=NT)

        with ExitStack() as scope:
            qk = heads(proj, 0, 9, 64)
            ix = heads(proj, O_IQ, 9, 64)
            sq = sb("sq", [P, NT * 9, 64], scope=scope)
            tmp = sb("tmp", [P, 2, 9, 32], scope=scope)
            qkT = hT[0:64, :, :].rearrange("p k n -> p (k n)")[:, 0:9 * S].rearrange("p (h s) -> p h s", h=9)
            ixT = sb("ixT", [64, 9, S], scope=scope)
            pT = sb("pT", [P, 2, 1024], scope=scope)
            rel = hT[:, :, :].rearrange("p k n -> p (k n)")[:, 11 * S:15 * S].rearrange("p (a n) -> p a n", a=2)
            score = hT[:, :, :].rearrange("p k n -> p (k n)")[:, 9 * S:11 * S].rearrange("p (t k) -> p t k", t=NT)
            top8 = sb("top8", [P, NT, 8], scope=scope)
            bias = attn_bias
            hnorm = HeadNorm("dsa")
            qk_ready, ix_ready = sem("qk_ready"), sem("ix_ready")
            scored = sem("scored")
            to_qkT = Transpose("qkT", lambda n, t: qk[:, t, n, :], 9, 64, lambda g, m: qkT[:, g:g + m, :])
            to_ixT = Transpose("ixT", lambda n, t: ix[:, t, n, :], 9, 64, lambda g, m: ixT[:, g:g + m, :])
            att = Attention("dsa", DSA_H, lambda h: qkT[:, h, :], lambda h: qkT[:, 8, :],
                            lambda h, kt: proj[:, kt, 576:640], S, HD ** -0.5, lambda p: outA[:, p, :], (probs, (pT[:, 0, :], pT[:, 1, :]), negmax, sums),
                            bias=lambda t: bias[:, t, :])
            pairs = [(t, h) for t in range(NT) for h in range(0, DSA_H, 2)]
            ada_buf = outB[:, :, :].rearrange("p k n -> p (k n)").rearrange("p (a n) -> p a n", a=2)
            ada0, ada1 = Ada(ada_buf), Ada(ada_buf)
            block = scope.enter_context(nc.Block())

            @block.tensor
            def _(pe):
                ada0.tensor(pe)
                pe.wait_ge(ix_ready, 1)
                to_ixT.tensor(pe)
                to_ixT.wait_all(pe)
                for t, h in pairs:
                    b = banks.open(("rel", t, h), ACTE)
                    if b.emptied:
                        pe.wait_ge(*b.emptied)
                    for j in range(2):
                        i = pe.matmul(b.ap[:, j * S:(j + 1) * S], ixT[:, h + j, t * P:(t + 1) * P], ixT[:, 8, :],
                                      start=True, stop=True)
                    i.then_inc(bank_full, 1)
                ada1.tensor(pe)
                pe.wait_ge(qk_ready, 1)
                to_qkT.tensor(pe)
                to_qkT.wait_all(pe)
                att.tensor(pe)

            @block.gpsimd
            def _(pool):
                hnorm.pool(pool, 9, 64)

            @block.scalar
            def _(act):
                ada0.scalar(act)
                to_ixT.evacuate(act, ACTE)
                for n, (t, h) in enumerate(pairs):
                    b = banks["rel", t, h]
                    act.wait_ge(bank_full, b.full)
                    if n >= 2:
                        act.wait_ge(scored, n - 1)
                    act.activation(rel[:, n % 2, :], b.ap[:, :], ACT.Relu).then_inc(emptied[ACTE], 1)
                ada1.scalar(act)
                to_qkT.evacuate(act, ACTE)
                att.scalar(act)

            @block.vector
            def _(dve):
                link = chain(dve, dve_step)
                rope(dve, link, ix, ix, tmp, 9, 32, 64, 0, cos(32), sin(32))
                dve.sem_inc(ix_ready, 1)
                hnorm.vector_sum(dve, link, qk, sq[:, :, :], 9, 64)
                ada0.vector(dve)
                to_ixT.evacuate(dve, DVE)
                hnorm.vector_scale(dve, link, qk, qk, [(0, 8, gain("dsa_q_norm_g")), (8, 9, gain("dsa_k_norm_g"))], 9, 64)
                rope(dve, link, qk, qk, tmp, 9, 32, 64, 0, cos(32), sin(32))
                dve.sem_inc(qk_ready, 1)
                for n, (t, h) in enumerate(pairs):
                    b = banks["rel", t, h]
                    dve.wait_ge(emptied[ACTE], b.done)
                    for j in range(2):
                        w_h = proj[:, t, O_IW + h + j:O_IW + h + j + 1]
                        r = rel[:, n % 2, j * S:(j + 1) * S]
                        if h + j == 0:
                            link(dve.tensor_scalar(score[:, t, :], r, w_h, None, ALU.mult))
                        elif j == 0:
                            link(dve.scalar_tensor_tensor(score[:, t, :], r, w_h, score[:, t, :], ALU.mult, ALU.add))
                        else:
                            dve.scalar_tensor_tensor(score[:, t, :], r, w_h, score[:, t, :],
                                                     ALU.mult, ALU.add).then_inc(scored, 1)
                            dve.wait_ge(scored, n + 1)
                link(dve.tensor_scalar(score[:, :, :], score[:, :, :], float(64 ** -0.5 * 8 ** -0.5), None, ALU.mult))
                link(dve.tensor_tensor(score[:, :, :], score[:, :, :], causal, ALU.mult))
                link(dve.tensor_scalar(bias[:, :, :], causal, 1.0, -NEG, ALU.subtract, ALU.mult))
                link(dve.tensor_tensor(score[:, :, :], score[:, :, :], bias[:, :, :], ALU.add))
                for r in range(TOPK // 8):
                    for t in range(NT):
                        i = dve.max(top8[:, t, :], score[:, t, :])
                    link(i)
                    for t in range(NT):
                        i = dve.match_replace(score[:, t, :], top8[:, t, :], score[:, t, :], TAKEN)
                    link(i)
                link(dve.scalar_tensor_tensor(bias[:, :, :].rearrange("p t k -> p (t k)"),
                                              score[:, :, :].rearrange("p t k -> p (t k)"), TAKEN,
                                              const("causal"), ALU.is_equal, ALU.mult))
                link(dve.tensor_scalar(bias[:, :, :], bias[:, :, :], 1.0, BIG, ALU.subtract, ALU.mult))
                ada1.vector(dve)
                to_qkT.evacuate(dve, DVE)
                att.vector(dve, link)

            @block.sync
            def _(sp):
                load_weights(sp)

        with ExitStack() as scope:
            cn = sb("cn", [P, NT, 384], scope=scope)
            cT = sb("cT", [P, 3, S], scope=scope)
            mqk = sb("mqk", [P, NT, 16 * MLA_QK], scope=scope)
            kvb = sb("kvb", [P, NT, 1024], scope=scope)
            mqkT = hT[0:MLA_QK, :, :].rearrange("p k n -> p (k n)").rearrange("p (h s) -> p h s", h=16)
            msq = hT[:, :, :].rearrange("p k n -> p (k n)")[:, 0:NT * 16 * MLA_QK].rearrange("p (h d) -> p h d", d=MLA_QK)
            tmp = proj[:, 0, 0:512].rearrange("p (a h d) -> p a h d", a=2, h=16)
            cbias = attn_bias
            mh = mqk[:, :, :].rearrange("p t (h d) -> p t h d", d=MLA_QK)
            kvh = kvb[:, :, :].rearrange("p t (h d) -> p t h d", d=128)
            c_squared, c_rooted, c_normed, heads_ready = sem("c_squared"), sem("c_rooted"), sem("c_normed"), sem("heads_ready")
            hnorm = HeadNorm("mla")
            cgain = lambda n: vcols[:, VCOL["mla_cq_norm_g"] + n:VCOL["mla_cq_norm_g"] + n + 1]
            to_cT = Transpose("cT", lambda n, t: cn[:, t, n * P:(n + 1) * P], 3, P, lambda g, m: cT[:, g:g + m, :], gain=cgain)
            to_T = Transpose("mqkT", lambda n, t: mh[:, t, n, :], 16, MLA_QK, lambda g, m: mqkT[:, g:g + m, :])
            att = Attention("mla", MLA_H, lambda h: mqkT[:, h, :], lambda h: mqkT[:, 8 + h, :],
                            lambda h, kt: kvb[:, kt, h * 128 + 64:h * 128 + 128], S, MLA_QK ** -0.5, lambda p: outB[:, p, :],
                            (probs, (proj[:, 0, 0:1024], proj[:, 1, 0:1024]), negmax, sums),
                            bias=lambda t: cbias[:, t, :])
            ada0, ada1 = Ada(ada_buf), Ada(ada_buf)
            block = scope.enter_context(nc.Block())

            @block.tensor
            def _(pe):
                ada0.tensor(pe)
                pe.wait_ge(c_normed, 1)
                to_cT.tensor(pe)
                to_cT.wait_all(pe)
                piece = ring["mla"]
                pe.wait_ge(piece.sem, piece.full)
                uq, ukv = view(piece, 0, 2, 768), view(piece, 1536, 1, 1024)
                for t in range(NT):
                    tt = slice(t * P, (t + 1) * P)
                    for n in range(2):
                        b, _ = gemm(pe, ("uq", t, n), lambda k: cT[:, k, tt], 2, t,
                                    lambda k: uq[:, k, n * 384:(n + 1) * 384], 384, ACTE)
                    for n in range(2):
                        b, _ = gemm(pe, ("ukv", t, n), lambda k: cT[:, 2, tt], 1, t,
                                    lambda k: ukv[:, 0, n * 512:(n + 1) * 512], 512, DVE)
                piece.freed = (bank_full, b.full)
                ada1.tensor(pe)
                pe.wait_ge(heads_ready, 1)
                to_T.tensor(pe)
                to_T.wait_all(pe)
                att.tensor(pe)

            @block.gpsimd
            def _(pool):
                pool.wait_ge(c_squared, 4)
                root(pool, 0, 2, MLA_QR)
                root(pool, 2, 2, MLA_KVR, c_rooted)
                hnorm.pool(pool, 16, MLA_QK)

            @block.scalar
            def _(act):
                for t in range(NT):
                    act.activation(cn[:, t, 0:256], proj[:, t, O_CQ:O_CKV], ACT.Square,
                                   accum_out=eps_rows[:, t:t + 1]).then_inc(c_squared, 1)
                    act.activation(cn[:, t, 256:384], proj[:, t, O_CKV:O_KPE], ACT.Square,
                                   accum_out=eps_rows[:, 2 + t:3 + t]).then_inc(c_squared, 1)
                ada0.scalar(act)
                to_cT.evacuate(act, ACTE)
                for t in range(NT):
                    for n in range(2):
                        copy_out(act, ACTE, ("uq", t, n), mqk[:, t, n * 384:(n + 1) * 384], 384)
                ada1.scalar(act)
                to_T.evacuate(act, ACTE)
                att.scalar(act)

            @block.vector
            def _(dve):
                link = chain(dve, dve_step)
                link(dve.tensor_scalar(cbias[:, :, :], causal, 1.0, BIG, ALU.subtract, ALU.mult))
                dve.wait_ge(c_rooted, 1)
                for t in range(NT):
                    dve.tensor_scalar(cn[:, t, 0:256], proj[:, t, O_CQ:O_CKV], rstd[:, t:t + 1],
                                      MLA_QR ** 0.5, ALU.mult, ALU.mult)
                    i = dve.tensor_scalar(cn[:, t, 256:384], proj[:, t, O_CKV:O_KPE], rstd[:, 2 + t:3 + t],
                                          float(MLA_KVR) ** 0.5, ALU.mult, ALU.mult)
                i.then_inc(c_normed, 1)
                ada0.vector(dve)
                to_cT.evacuate(dve, DVE)
                for t in range(NT):
                    for n in range(2):
                        copy_out(dve, DVE, ("ukv", t, n), kvb[:, t, n * 512:(n + 1) * 512], 512)
                b = banks["ukv", NT - 1, 1]
                dve.wait_ge(emptied[DVE], b.done)
                for t in range(NT):
                    dve.tensor_copy(mh[:, t, 8:16, 0:64], kvh[:, t, :, 0:64])
                    i = dve.tensor_copy(mh[:, t, 8:16, 64:96],
                                        proj[:, t, O_KPE:O_GD].unsqueeze(1).broadcast_to([P, 8, 32]))
                link(i)
                b = banks["uq", NT - 1, 1]
                dve.wait_ge(emptied[ACTE], b.done)
                hnorm.vector_sum(dve, link, mh, msq, 16, MLA_QK)
                hnorm.vector_scale(dve, link, mh, mh, [(0, 8, gain("mla_q_norm_g")), (8, 16, gain("mla_k_norm_g"))], 16, MLA_QK)
                rope(dve, link, mh, mh, tmp, 16, 16, MLA_QK, 64, cos(16), sin(16))
                dve.sem_inc(heads_ready, 1)
                ada1.vector(dve)
                to_T.evacuate(dve, DVE)
                att.vector(dve, link)

            @block.sync
            def _(sp):
                load_weights(sp)

        with ExitStack() as scope:
            mT = hT[:, :, S:2 * S]
            merged = sb("merged", [P, NT, D], scope=scope)
            part = sb("part", [P, 2, 512], scope=scope)
            gates_ready, merged_ready, mem_loaded = sem("gates_ready"), sem("merged_ready"), sem("mem_loaded")
            both = (outA, outB)
            to_mT = Transpose("mT", lambda n, t: merged[:, t, n * P:(n + 1) * P], 8, P, lambda g, m: mT[:, g:g + m, :])
            block = scope.enter_context(nc.Block())

            @block.tensor
            def _(pe):
                pa, pb = ring["br_dsa"], ring["br_mla"]
                pe.wait_ge(pa.sem, pa.full)
                pe.wait_ge(pb.sem, pb.full)
                for t in range(NT):
                    for n in range(2):
                        for m, piece in enumerate((pa, pb)):
                            wv = view(piece, 0, 4, D)
                            b, _ = gemm(pe, ("br", t, n, m), lambda k: both[m][:, k, t * P:(t + 1) * P], 4, t,
                                        lambda k: wv[:, k, n * 512:(n + 1) * 512], 512, DVE)
                            piece.freed = (bank_full, b.full)
                pe.wait_ge(merged_ready, 4)
                to_mT.tensor(pe)
                to_mT.wait_all(pe)
                w0, w1 = ring["w_out", 0], ring["w_out", 1]
                pe.wait_ge(w0.sem, w0.full)
                pe.wait_ge(w1.sem, w1.full)
                wv = (view(w0, 0, 4, D), view(w1, 0, 4, D))
                for t in range(NT):
                    for n in range(2):
                        b, _ = gemm(pe, ("mixed", t, n), lambda k: mT[:, k, t * P:(t + 1) * P], 8, t,
                                    lambda k: wv[k // 4][:, k % 4, n * 512:(n + 1) * 512], 512, DVE)
                w0.freed = w1.freed = (bank_full, b.full)

            @block.scalar
            def _(act):
                act.dma_start(C[:, :, :], A["mem"].rearrange("b (t p) d -> p (b t) d", p=P)).then_inc(mem_loaded, 16)
                act.activation(proj[:, :, O_GD:N_IN], proj[:, :, O_GD:N_IN], ACT.Sigmoid).then_inc(gates_ready, 1)
                to_mT.evacuate(act, ACTE)

            @block.vector
            def _(dve):
                link = chain(dve, dve_step)
                dve.wait_ge(gates_ready, 1)
                for t in range(NT):
                    for n in range(2):
                        c = slice(n * 512, (n + 1) * 512)
                        b = banks["br", t, n, 0]
                        dve.wait_ge(bank_full, b.full)
                        dve.tensor_tensor(merged[:, t, c], b.ap[:, :], proj[:, t, O_GD + n * 512:O_GD + (n + 1) * 512],
                                          ALU.mult).then_inc(emptied[DVE], 1)
                        b = banks["br", t, n, 1]
                        dve.wait_ge(bank_full, b.full)
                        dve.tensor_tensor(part[:, n, :], b.ap[:, :], proj[:, t, O_GM + n * 512:O_GM + (n + 1) * 512],
                                          ALU.mult).then_inc(emptied[DVE], 1)
                        dve.wait_ge(emptied[DVE], b.done)
                        dve.tensor_tensor(merged[:, t, c], merged[:, t, c], part[:, n, :], ALU.add).then_inc(merged_ready, 1)
                to_mT.evacuate(dve, DVE)
                for t in range(NT):
                    for n in range(2):
                        c = slice(n * 512, (n + 1) * 512)
                        b = banks["mixed", t, n]
                        dve.wait_ge(bank_full, b.full)
                        dve.tensor_tensor(X[:, t, c], X[:, t, c], b.ap[:, :], ALU.add).then_inc(emptied[DVE], 1)

            @block.sync
            def _(sp):
                load_weights(sp)
        mix.close()

        with ExitStack() as scope:
            M = C
            xn = sb("xn2", [P, 4, D], scope=scope)
            cq = sb("cqk", [P, NT, 8 * 64], scope=scope)
            cv = sb("cv", [P, NT, 256], scope=scope)
            csq = sb("csq", [P, NT * 8, 64], scope=scope)
            cqT = sb("cqT", [64, 8, S], scope=scope)
            coT = sb("coT", [P, 2, S], scope=scope)
            pT2 = sb("pT2", [P, 2, 1024], scope=scope)
            bufs = (sb("probs2", [P, 4, 512], scope=scope), (pT2[:, 0, :], pT2[:, 1, :]),
                    sb("negmax2", [P, 32], scope=scope), sb("sums2", [P, 32], scope=scope))
            ada_buf = sb("ada_buf2", [P, 2, 512], scope=scope)
            ada0, ada1 = Ada(ada_buf), Ada(ada_buf)
            mheads_ready = sem("mheads_ready")
            gx, gm = VCOL["mem_x_norm_g"], VCOL["mem_norm_g"]
            norm = NormT("n2", [X[:, t, :] for t in range(NT)] + [M[:, t, :] for t in range(NT)], xn, hT,
                         lambda k: [(0, S, vcols[:, gx + k:gx + k + 1], None), (S, 2 * S, vcols[:, gm + k:gm + k + 1], None)])
            ch = cq[:, :, :].rearrange("p t (h d) -> p t h d", d=64)
            hnorm = HeadNorm("mem")
            to_T = Transpose("cqT", lambda n, t: ch[:, t, n, :], 8, 64, lambda g, m: cqT[:, g:g + m, :])
            att = Attention("mem", MEM_H, lambda h: cqT[:, h, :], lambda h: cqT[:, 4 + h, :],
                            lambda h, kt: cv[:, kt, h * 64:(h + 1) * 64], S, 64 ** -0.5, lambda p: coT[:, p, :], bufs)
            block = scope.enter_context(nc.Block())

            @block.tensor
            def _(pe):
                ada0.tensor(pe)
                norm.tensor(pe)
                for k in range(KD):
                    norm.wait_chunk(pe, k)
                pq, pkv, po = ring["mem_q"], ring["mem_kv"], ring["mem_o"]
                pe.wait_ge(pq.sem, pq.full)
                wq, wkv, wo = view(pq, 0, KD, 256), view(pkv, 0, KD, 512), view(po, 0, 2, D)
                for t in range(NT):
                    b, _ = gemm(pe, ("mq", t), lambda k: hT[:, k, t * P:(t + 1) * P], KD, t, lambda k: wq[:, k, :], 256, ACTE)
                pq.freed = (bank_full, b.full)
                pe.wait_ge(pkv.sem, pkv.full)
                for t in range(NT):
                    b, _ = gemm(pe, ("mkv", t), lambda k: hT[:, k, S + t * P:S + (t + 1) * P], KD, t,
                                lambda k: wkv[:, k, :], 512, DVE)
                pkv.freed = (bank_full, b.full)
                ada1.tensor(pe)
                pe.wait_ge(mheads_ready, 1)
                to_T.tensor(pe)
                to_T.wait_all(pe)
                att.tensor(pe)
                pe.wait_ge(emptied[DVE], banks["mem", "pv", MEM_H // 2 - 1].done)
                pe.wait_ge(po.sem, po.full)
                for t in range(NT):
                    for n in range(2):
                        b, _ = gemm(pe, ("memo", t, n), lambda k: coT[:, k, t * P:(t + 1) * P], 2, t,
                                    lambda k: wo[:, k, n * 512:(n + 1) * 512], 512, DVE)
                po.freed = (bank_full, b.full)

            @block.gpsimd
            def _(pool):
                norm.pool(pool)
                hnorm.pool(pool, 8, 64)

            @block.scalar
            def _(act):
                act.wait_ge(mem_loaded, 16)
                norm.scalar_squares(act)
                ada0.scalar(act)
                norm.evacuate(act, ACTE)
                for t in range(NT):
                    copy_out(act, ACTE, ("mq", t), cq[:, t, 0:256], 256)
                ada1.scalar(act)
                to_T.evacuate(act, ACTE)
                att.scalar(act)

            @block.vector
            def _(dve):
                link = chain(dve, dve_step)
                norm.vector_scale(dve)
                ada0.vector(dve)
                norm.evacuate(dve, DVE)
                for t in range(NT):
                    b = banks["mkv", t]
                    dve.wait_ge(bank_full, b.full)
                    dve.tensor_copy(cq[:, t, 256:512], b.ap[:, 0:256])
                    dve.tensor_copy(cv[:, t, :], b.ap[:, 256:512]).then_inc(emptied[DVE], 1)
                b = banks["mkv", NT - 1]
                dve.wait_ge(emptied[DVE], b.done)
                dve.wait_ge(emptied[ACTE], banks["mq", NT - 1].done)
                hnorm.vector_sum(dve, link, ch, csq[:, :, :], 8, 64)
                hnorm.vector_scale(dve, link, ch, ch, [(0, 4, gain("mem_q_norm_g")), (4, 8, gain("mem_k_norm_g"))], 8, 64)
                dve.sem_inc(mheads_ready, 1)
                ada1.vector(dve)
                to_T.evacuate(dve, DVE)
                att.vector(dve, link)
                for t in range(NT):
                    for n in range(2):
                        c = slice(n * 512, (n + 1) * 512)
                        b = banks["memo", t, n]
                        dve.wait_ge(bank_full, b.full)
                        dve.tensor_tensor(X[:, t, c], X[:, t, c], b.ap[:, :], ALU.add).then_inc(emptied[DVE], 1)

            @block.sync
            def _(sp):
                load_weights(sp)


        with ExitStack() as scope:
            xn = sb("xn3", [P, NT, D], scope=scope)
            wr = sb("wr", [P, KD, 20], scope=scope)
            lg = sb("lg", [P, NT, 20], scope=scope)
            R = {k: sb("r_" + k, [P, NT, 16], scope=scope) for k in ("aff", "score", "w", "one", "both", "m", "d")}
            comb = sb("comb", [P, NT, 16], scope=scope)
            combT = sb("combT", [16, S], scope=scope)
            cb = sb("cb", [P, N_EXP, S], scope=scope)
            gated = sb("gated", [P, 2, 512], scope=scope)
            actT = sb("actT", [P, 2, 2, 512], F32R, scope)
            norm = NormT("n3", [X[:, t, :] for t in range(NT)], xn, hT, plain_gain("moe_norm_g"))
            to_combT = Transpose("combT", lambda n, t: comb[:, t, :], 1, 16, lambda g, m: combT[:, :].unsqueeze(1), by=(DVE,))
            wr_loaded, sub_ready, exp_ready, comb_ready = (sem(x) for x in ("wr_loaded", "sub_ready", "exp_ready", "comb_ready"))
            gu_full, silued, act_ready, down_done = (sem(x) for x in ("gu_full", "silued", "act_ready", "down_done"))
            gated_step = sem("gated_step")
            gu_split, down_split = sem("gu_split"), sem("down_split")
            gu_loaded = [sem(f"gu_loaded{j}") for j in range(2)]
            down_loaded = [sem(f"down_loaded{j}") for j in range(2)]
            h_high, h_low = hT_r[:, :, S:2 * S], hT_r[:, :, 0:S]
            Y = [psum[i][:, :] for i in range(4)]
            GU = [[psum[4][:, :], psum[5][:, :]], [psum[6][:, :], psum[7][:, :]]]
            prep = scope.enter_context(ExitStack())
            ada_buf = sb("ada_buf3", [P, 2, 512], scope=prep)
            ada0, ada1 = Ada(ada_buf), Ada(ada_buf)
            block = prep.enter_context(nc.Block())

            @block.tensor
            def _(pe):
                ada0.tensor(pe)
                norm.tensor(pe)
                pe.wait_ge(wr_loaded, 32)
                for t in range(NT):
                    b = banks.open(("router", t), DVE)
                    if b.emptied:
                        pe.wait_ge(*b.emptied)
                    for k in range(KD):
                        norm.wait_chunk(pe, k)
                        i = pe.matmul(b.ap[:, 0:20], hT[:, k, t * P:(t + 1) * P], wr[:, k, :], start=(k == 0), stop=(k == KD - 1))
                    i.then_inc(bank_full, 1)
                ada1.tensor(pe)
                pe.wait_ge(comb_ready, 1)
                to_combT.tensor(pe)
                to_combT.wait_all(pe)
                for e in range(0, N_EXP, 2):
                    b = banks.open(("cb", e), (DVE, ACTE)[e // 2 % 2])
                    if b.emptied:
                        pe.wait_ge(*b.emptied)
                    for j in range(2):
                        i = pe.matmul(b.ap[:, j * S:(j + 1) * S], consts[0:16, e + j:e + j + 1].broadcast_to([16, P]),
                                      combT[:, :], start=True, stop=True)
                    i.then_inc(bank_full, 1)

            @block.gpsimd
            def _(pool):
                norm.pool(pool)

            @block.scalar
            def _(act):
                norm.scalar_squares(act)
                ada0.scalar(act)
                norm.evacuate(act, ACTE)
                act.wait_ge(sub_ready, 1)
                act.activation(R["m"][:, :, 0:4], R["m"][:, :, 0:4], ACT.Exp).then_inc(exp_ready, 1)
                act.activation(R["aff"][:, :, :], lg[:, :, 4:20], ACT.Sigmoid).then_inc(exp_ready, 1)
                ada1.scalar(act)
                for e in range(0, N_EXP, 2):
                    copy_out(act, ACTE, ("cb", e), cb[:, e:e + 2, :].rearrange("p e t -> p (e t)"), 512)

            @block.vector
            def _(dve):
                link = chain(dve, dve_step)
                norm.vector_scale(dve)
                ada0.vector(dve)
                norm.evacuate(dve, DVE)
                for t in range(NT):
                    copy_out(dve, DVE, ("router", t), lg[:, t, :], 20)
                dve.wait_ge(emptied[DVE], banks["router", NT - 1].done)
                v = {k: a[:, :, :] for k, a in R.items()}
                grp = v["m"][:, :, 0:4]
                top = v["d"][:, :, 0:1]

                def first_largest(dst, val, n):
                    link(dve.tensor_reduce(top, val, AX.X, ALU.max))
                    link(dve.tensor_tensor(dst, val, top.broadcast_to([P, NT, n]), ALU.is_equal))
                    down = const("down16")[:, 16 - n:16].unsqueeze(1).broadcast_to([P, NT, n])
                    link(dve.tensor_tensor(dst, dst, down, ALU.mult))
                    link(dve.tensor_reduce(v["d"][:, :, 1:2], dst, AX.X, ALU.max))
                    link(dve.tensor_tensor(dst, dst, v["d"][:, :, 1:2].broadcast_to([P, NT, n]), ALU.is_equal))

                link(dve.tensor_reduce(top, lg[:, :, 0:4], AX.X, ALU.max))
                link(dve.tensor_tensor(grp, lg[:, :, 0:4], top.broadcast_to([P, NT, 4]), ALU.subtract))
                dve.sem_inc(sub_ready, 1)
                dve.wait_ge(exp_ready, 2)
                link(dve.tensor_reduce(top, grp, AX.X, ALU.add))
                link(dve.reciprocal(top, top))
                link(dve.tensor_tensor(grp, grp, top.broadcast_to([P, NT, 4]), ALU.mult))
                pick = v["w"][:, :, 0:4]
                first_largest(pick, grp, 4)
                link(dve.tensor_copy(v["d"][:, :, 2:3], top))
                g16 = v["one"].rearrange("p t (g e) -> p t g e", g=4)
                link(dve.tensor_copy(g16, pick.unsqueeze(3).broadcast_to([P, NT, 4, 4])))
                bias16 = gain("moe_expert_bias").unsqueeze(1).broadcast_to([P, NT, 16])
                link(dve.tensor_tensor(v["score"], v["aff"], bias16, ALU.add))
                link(dve.tensor_tensor(v["score"], v["score"], v["one"], ALU.mult))
                link(dve.tensor_scalar(v["one"], v["one"], 1.0, BIG, ALU.subtract, ALU.mult))
                link(dve.tensor_tensor(v["score"], v["score"], v["one"], ALU.add))
                first_largest(v["both"], v["score"], 16)
                link(dve.tensor_scalar(v["one"], v["both"], -10 * BIG, None, ALU.mult))
                link(dve.tensor_tensor(v["score"], v["score"], v["one"], ALU.add))
                first_largest(v["w"], v["score"], 16)
                link(dve.tensor_tensor(v["both"], v["both"], v["w"], ALU.add))
                link(dve.tensor_tensor(v["aff"], v["aff"], v["both"], ALU.mult))
                link(dve.tensor_reduce(top, v["aff"], AX.X, ALU.add))
                link(dve.reciprocal(top, top))
                link(dve.tensor_tensor(top, top, v["d"][:, :, 2:3], ALU.mult))
                link(dve.tensor_tensor(comb[:, :, :], v["aff"], top.broadcast_to([P, NT, 16]), ALU.mult))
                dve.sem_inc(comb_ready, 1)
                link(split_high(dve, h_high, hT[:, :, 0:S]))
                link(split_low(dve, h_low, hT[:, :, 0:S], h_high))
                ada1.vector(dve)
                to_combT.evacuate(dve, DVE)
                for e in range(0, N_EXP, 2):
                    copy_out(dve, DVE, ("cb", e), cb[:, e:e + 2, :].rearrange("p e t -> p (e t)"), 512)
                dve.wait_ge(emptied[DVE], banks["adaT", 23].done)
                mod = modcol[:, :, :, :, :].rearrange("p l c b s -> p (l c b) s")
                c = VCOL["ada_b_2"]
                link(dve.tensor_tensor(mod, mod, vcols[:, c:c + 96].unsqueeze(2).broadcast_to([P, 96, 2]), ALU.add))
                for l in range(2):
                    for n, (name, v) in enumerate((("norm1_w_2", 1), ("norm2_w_2", 4))):
                        c = VCOL[name] + 8 * l
                        for s_ in range(2):
                            dve.scalar_tensor_tensor(ncol[:, l, n, s_, :].rearrange("p (a b) -> p a b", a=2),
                                                     modcol[:, l, 2 * v:2 * v + 2, :, s_], 1.0,
                                                     vcols[:, c:c + 8].rearrange("p (a b) -> p a b", a=2), ALU.add, ALU.mult)

            @block.sync
            def _(sp):
                for c, name, n in ((0, "moe_w_group", 4), (4, "moe_w_expert", 16)):
                    sp.dma_start(wr[:, :, c:c + n], A[name].rearrange("a (k p) n -> p (a k) n", p=P),
                                 allow_slow_non_contiguous=True).then_inc(wr_loaded, 16)
                load_weights(sp)
            prep.close()
            PAIRS = N_EXP // 2
            split_step, ctx_loaded = sem("split_step"), sem("ctx_loaded")

            def gu_parts(j, m):
                c = slice(2048 * m, 2048 * (m + 1))
                return [slots_r[:, first + MOE1_SLOTS[j], c].rearrange("p (k n) -> p k n", n=D_EXP) for first in (3, 0)]

            def down_parts(j):
                c = slice(2048 * j, 2048 * (j + 1))
                return [slots_r[:, first + MOE1_SLOTS[2], c].rearrange("p (k n) -> p k n", n=D) for first in (3, 0)]

            block = scope.enter_context(nc.Block())

            @block.tensor
            def _(pe):
                pe.sem_inc(down_done, 2)
                for t in range(NT):
                    for n in range(2):
                        pe.matmul(Y[2 * t + n], ident, X[:, t, n * 512:(n + 1) * 512], start=True, stop=False,
                                  skip_group_check=True)

                def gate_up(e, j):
                    pe.wait_ge(gu_split, e + 1)
                    pe.wait_ge(act_ready, e + 1)
                    for m in range(2):
                        high, low = gu_parts(j, m)
                        for f in range(2):
                            c = slice(f * P, (f + 1) * P)
                            for k in range(KD):
                                ins = matmul_split(pe, GU[j][m][:, f * S:(f + 1) * S], (high[:, k, c], low[:, k, c]),
                                                   (h_high[:, k, :], h_low[:, k, :]), k == 0, k == KD - 1)
                        ins.then_inc(gu_full, 1)

                def down(e, j):
                    pe.wait_ge(down_split, e + 1)
                    pe.wait_ge(act_ready, e + 3)
                    high, low = down_parts(j)
                    for t in range(NT):
                        for n in range(2):
                            for f in range(2):
                                a = slice(f * S + t * P, f * S + (t + 1) * P)
                                c = slice(n * 512, (n + 1) * 512)
                                ins = matmul_split(pe, Y[2 * t + n], (actT[:, 0, j, a], actT[:, 1, j, a]),
                                                   (high[:, f, c], low[:, f, c]), False, False)
                    ins.then_inc(down_done, 1)

                gate_up(0, 0)
                with pe.Fori(0, PAIRS - 1) as i:
                    gate_up(2 * i + 1, 1)
                    down(2 * i, 0)
                    gate_up(2 * i + 2, 0)
                    down(2 * i + 1, 1)
                gate_up(N_EXP - 1, 1)
                down(N_EXP - 2, 0)
                down(N_EXP - 1, 1)

            @block.scalar
            def _(act):
                act.dma_start(C[:, :, :], A["ctx_2"].rearrange("b (t p) d -> p (b t) d", p=P)).then_inc(ctx_loaded, 16)
                with act.Fori(0, PAIRS) as i:
                    for j in range(2):
                        e = 2 * i + j
                        act.wait_ge(gu_full, 2 * e + 1)
                        act.wait_ge(act_ready, e + 1)
                        act.activation(gated[:, j, :], GU[j][0], ACT.Silu).then_inc(silued, 1)

            @block.vector
            def _(dve):
                def activate(e, j):
                    dve.wait_ge(silued, e + 1)
                    dve.wait_ge(gu_full, 2 * e + 2)
                    g = gated[:, j, :]
                    dve.tensor_tensor(g, g, GU[j][1], ALU.mult).then_inc(gated_step, 1)
                    dve.wait_ge(gated_step, 4 * e + 1)
                    dve.wait_ge(down_done, e + 1)
                    high, low = actT[:, 0, j, :], actT[:, 1, j, :]
                    gf = g.rearrange("p (f s) -> p f s", f=2)
                    dve.tensor_tensor(gf, gf, cb[:, e, :].unsqueeze(1).broadcast_to([P, 2, S]), ALU.mult).then_inc(gated_step, 1)
                    dve.wait_ge(gated_step, 4 * e + 2)
                    split_high(dve, high, g).then_inc(gated_step, 2)
                    dve.wait_ge(gated_step, 4 * e + 4)
                    split_low(dve, low, g, high).then_inc(act_ready, 1)

                def split(which, j, n):
                    c = slice(0, SLOT) if which == "gu" else slice(2048 * j, 2048 * (j + 1))
                    slot = MOE1_SLOTS[j if which == "gu" else 2]
                    raw, high, low = slots[:, slot, c], slots_r[:, 3 + slot, c], slots_r[:, slot, c]
                    split_high(dve, high, raw).then_inc(split_step, 1)
                    dve.wait_ge(split_step, n + 1)
                    split_low(dve, low, raw, high).then_inc(gu_split if which == "gu" else down_split, 1)

                dve.sem_inc(act_ready, 2)
                for j in range(2):
                    piece = ring["moe1", j]
                    dve.wait_ge(piece.sem, piece.full)
                    split("gu", j, j)
                piece = ring["moe1", 2]
                dve.wait_ge(piece.sem, piece.full)
                split("down", 0, 2)
                with dve.Fori(0, PAIRS - 1) as i:
                    for j in range(2):
                        e = 2 * i + j
                        activate(e, j)
                        dve.wait_ge(gu_loaded[j], 32 * i + 32)
                        split("gu", j, 2 * e + 3)
                        dve.wait_ge(down_loaded[1 - j], 16 * (i + j) + 1)
                        split("down", 1 - j, 2 * e + 4)
                activate(N_EXP - 2, 0)
                dve.wait_ge(down_loaded[1], 16 * (PAIRS - 1) + 1)
                split("down", 1, 2 * N_EXP - 1)
                activate(N_EXP - 1, 1)
                dve.wait_ge(down_done, N_EXP + 2)
                for t in range(NT):
                    for n in range(2):
                        dve.tensor_copy(X[:, t, n * 512:(n + 1) * 512], Y[2 * t + n])

            @block.sync
            def _(sp):
                for j in range(2):
                    sp.sem_inc(down_loaded[j], 1)

                def load_gate_up(e, j):
                    sp.wait_ge(gu_full, 2 * e - 2)
                    raw = slots[:, MOE1_SLOTS[j], :]
                    for at, w_ in ((0, gate_v), (2048, up_v)):
                        sp.dma_start(raw[:, at:at + 2048].rearrange("p (k n) -> p k n", n=D_EXP),
                                     w_[:, e]).then_inc(gu_loaded[j], 16)

                def load_down(e, j):
                    sp.wait_ge(down_done, e + 1)
                    raw = slots[:, MOE1_SLOTS[2], 2048 * j:2048 * (j + 1)]
                    sp.dma_start(raw.rearrange("p (k n) -> p k n", n=D), down_v[:, e]).then_inc(down_loaded[j], 16)

                load_gate_up(2, 0)
                load_gate_up(3, 1)
                load_down(2, 0)
                with sp.Fori(2, PAIRS) as i:
                    load_gate_up(2 * i, 0)
                    load_down(2 * i - 1, 1)
                    load_gate_up(2 * i + 1, 1)
                    load_down(2 * i, 0)
                load_down(N_EXP - 1, 1)
                for j in range(3):
                    ring["moe1", j].freed = (gu_full, 2 * (N_EXP - 1 + j)) if j < 2 else (down_done, N_EXP + 2)
                load_weights(sp)

        gate_full = sem("gate_full")
        TT = 2 * NT
        streams = [C[:, t, :] for t in range(NT)] + [X[:, t, :] for t in range(NT)]

        def mod_segments(l, n):
            def segs(k):
                v = 3 * n
                bias = lambda s_: modcol[:, l, 2 * v + k // 4, k % 4, s_:s_ + 1]
                return [(0, S, ncol[:, l, n, 1, k:k + 1], bias(1)), (S, 2 * S, ncol[:, l, n, 0, k:k + 1], bias(0))]
            return segs

        def gate_banks(pe, tag, l, v, s_, by):
            for n in range(2):
                b = banks.open((tag, s_, n), by)
                if b.emptied:
                    pe.wait_ge(*b.emptied)
                for j in range(4):
                    i = pe.matmul(b.ap[:, j * P:(j + 1) * P],
                                  modcol[:, l, 2 * v + n, j, s_:s_ + 1].broadcast_to([P, P]), ident,
                                  start=True, stop=True)
                i.then_inc(bank_full, 1)

        acum_dram = nc.dram_tensor("acum_rows", (64, TT * P), F32, kind="Internal").ap()
        with ExitStack() as ssd:
            Yt_base = (nc.sbuf_base + 31) // 32 * 32
            Yt = sb("Yt", [P, TT, D_INNER], scope=ssd)
            Yt_r = nc.alloc_sbuf_tensor_at("Yt_r", [P, TT, D_INNER], F32R, offset=Yt_base)
            scratch = slots[:, 3:6, :].rearrange("p s n -> p (s n)")
            pos = [0]

            def carve(n):
                pos[0] += n
                return scratch[:, pos[0] - n:pos[0]]

            padded = carve(4 * 2 * 260).rearrange("p (c s n) -> p c s n", c=4, s=2)
            conv = carve(4 * 512).rearrange("p (c n) -> p c n", c=4)
            tok = carve(TT * 384).rearrange("p (t n) -> p t n", t=TT)
            xdt = carve(2 * TT * GW).rearrange("p (d t n) -> p d t n", d=2, t=TT)
            dt, acs, wst, ea, dec = (carve(TT * 64).rearrange("p (t n) -> p t n", t=TT) for _ in range(5))
            xst = sb("xst", [P, 2, TT, GW], scope=ssd)
            rowsB = sb("rowsB", [P, 2, HPG, TT * P], scope=ssd)
            with ExitStack() as scope:
                u, dtmp, lnu = (rowsB[:, 0, i, 0:TT * 64].rearrange("p (t n) -> p t n", t=TT) for i in range(3))
                ab = rowsB[:, 1, 0, 0:TT * 64].rearrange("p (t n) -> p t n", t=TT)
                negA = rowsB[:, 1, 1, 0:64]
                aT = rowsB[0:64, 1, 2, :]
                xn = Yt[:, 0:2, :].rearrange("p t (a d) -> p (t a) d", a=2)
                norm = NormT("s1", streams, xn, hT, mod_segments(0, 0))
                sp_step, a_ready, aT_stored = (sem(x) for x in ("sp_step", "a_ready", "aT_stored"))
                acum_ready = sem("acum_ready")
                block = scope.enter_context(nc.Block())

                @block.tensor
                def _(pe):
                    norm.tensor(pe)
                    for k in range(KD):
                        norm.wait_chunk(pe, k)
                    piece = ring["dt"]
                    pe.wait_ge(piece.sem, piece.full)
                    wv = view(piece, 0, KD, 64)
                    b = banks.open("dt", DVE)
                    pe.wait_ge(*b.emptied)
                    for t in range(TT):
                        for k in range(KD):
                            i = pe.matmul(b.ap[:, t * 64:(t + 1) * 64], hT[:, k, t * P:(t + 1) * P], wv[:, k, :],
                                          start=(k == 0), stop=(k == KD - 1))
                    i.then_inc(bank_full, 1)
                    piece.freed = (bank_full, b.full)
                    pe.wait_ge(a_ready, 1)
                    b = banks.open("acum", DVE)
                    pe.wait_ge(*b.emptied)
                    for t in range(TT):
                        for d in range(2):
                            c = slice(d * 32, (d + 1) * 32)
                            i = pe.matmul(b.ap[:, t * 64 + d * 32:t * 64 + d * 32 + 32], const(("upto", "from")[d]),
                                          ab[:, t, c], start=True, stop=True)
                    i.then_inc(bank_full, 1)
                    b = banks.open("last", DVE)
                    pe.wait_ge(*b.emptied)
                    pe.matmul(b.ap[:, 0:TT * 64], const("ones"), ab[:, :, :].rearrange("p t n -> p (t n)"),
                              start=True, stop=True).then_inc(bank_full, 1)
                    pe.wait_ge(emptied[DVE], banks["acum"].done)
                    b = banks.open("acumT", DVE)
                    pe.wait_ge(*b.emptied)
                    for t in range(TT):
                        i = pe.transpose(b.ap[0:64, t * P:(t + 1) * P], acs[:, t, :], ident)
                    i.then_inc(bank_full, 1)

                @block.gpsimd
                def _(pool):
                    norm.pool(pool)

                @block.scalar
                def _(act):
                    act.wait_ge(ctx_loaded, 16)
                    norm.scalar_squares(act)
                    norm.evacuate(act, ACTE)
                    act.activation(negA, gain("ssd_A_log_2"), ACT.Exp).then_inc(sp_step, 1)
                    act.wait_ge(sp_step, 2)
                    act.activation(u, u, ACT.Exp).then_inc(sp_step, 1)
                    act.wait_ge(sp_step, 4)
                    act.activation(lnu, dtmp, ACT.Ln).then_inc(sp_step, 1)
                    act.wait_ge(acum_ready, 1)
                    act.activation(wst, wst, ACT.Exp).then_inc(acum_ready, 1)
                    act.activation(ea, acs, ACT.Exp)
                    act.activation(dec, dec, ACT.Exp)

                @block.vector
                def _(dve):
                    link = chain(dve, dve_step)
                    norm.vector_scale(dve)
                    norm.evacuate(dve, DVE)
                    b = banks["dt"]
                    dve.wait_ge(bank_full, b.full)
                    bias = gain("ssd_dt_bias_2").unsqueeze(1).broadcast_to([P, TT, 64])
                    dve.tensor_tensor(dt, b.ap[:, 0:TT * 64].rearrange("p (t n) -> p t n", t=TT), bias,
                                      ALU.add).then_inc(emptied[DVE], 1)
                    dve.wait_ge(emptied[DVE], b.done)
                    dve.wait_ge(sp_step, 1)
                    link(dve.scalar_tensor_tensor(u, dt, -1.0, dt, ALU.mult, ALU.min))
                    dve.sem_inc(sp_step, 1)
                    dve.wait_ge(sp_step, 3)
                    link(dve.tensor_scalar(dtmp, u, 1.0, None, ALU.add))
                    dve.sem_inc(sp_step, 1)
                    dve.wait_ge(sp_step, 5)
                    link(dve.tensor_scalar(dtmp, dtmp, 1.0, None, ALU.subtract))
                    link(dve.tensor_tensor(lnu, lnu, u, ALU.mult))
                    link(dve.tensor_scalar(ab, dtmp, 0.0, None, ALU.is_equal))
                    link(dve.tensor_tensor(u, u, ab, ALU.mult))
                    link(dve.tensor_scalar(dtmp, dtmp, 1e-30, None, ALU.max))
                    link(dve.reciprocal(dtmp, dtmp))
                    link(dve.tensor_tensor(lnu, lnu, dtmp, ALU.mult))
                    link(dve.tensor_tensor(lnu, lnu, u, ALU.add))
                    link(dve.tensor_scalar(dt, dt, 0.0, None, ALU.max))
                    link(dve.tensor_tensor(dt, dt, lnu, ALU.add))
                    link(dve.tensor_tensor(ab, dt, negA.unsqueeze(1).broadcast_to([P, TT, 64]), ALU.mult))
                    link(dve.tensor_scalar(ab, ab, -1.0, None, ALU.mult))
                    dve.sem_inc(a_ready, 1)
                    flat_ = lambda ap: ap.rearrange("p t n -> p (t n)")
                    b = banks["acum"]
                    dve.wait_ge(bank_full, b.full)
                    dve.tensor_copy(flat_(acs), b.ap[:, 0:TT * 64]).then_inc(emptied[DVE], 1)
                    dve.wait_ge(emptied[DVE], b.done)
                    b = banks["last"]
                    dve.wait_ge(bank_full, b.full)
                    link(dve.tensor_tensor(flat_(wst), b.ap[:, 0:TT * 64], flat_(acs), ALU.subtract))
                    dve.tensor_copy(flat_(dec), b.ap[:, 0:TT * 64]).then_inc(emptied[DVE], 1)
                    dve.wait_ge(emptied[DVE], b.done)
                    dve.sem_inc(acum_ready, 1)
                    b = banks["acumT"]
                    dve.wait_ge(bank_full, b.full)
                    dve.tensor_copy(aT, b.ap[0:64, :]).then_inc(emptied[DVE], 1)
                    dve.wait_ge(acum_ready, 2)
                    link(dve.tensor_tensor(flat_(wst), flat_(wst), flat_(dt), ALU.mult))
                    dve.memset(padded, 0.0)

                @block.sync
                def _(sp):
                    load_weights(sp)
                    sp.wait_ge(emptied[DVE], banks["acumT"].done)
                    sp.dma_start(acum_dram, aT).then_inc(aT_stored, 16)
                    sp.wait_ge(aT_stored, 16)

            with ExitStack() as scope:
                hp = sb("hp", [P, 2, TT, GW], scope=scope)
                off = carve(2 * GW).rearrange("p (d n) -> p d n", d=2)
                rows_loaded = sem("rows_loaded")
                conv_done, silu_done, conv_step = sem("conv_done"), sem("silu_done"), sem("conv_step")
                exps_in, exps_out, m_ready, prod_ready, hp_ready, y_done = (
                    sem(x) for x in ("exps_in", "exps_out", "m_ready", "prod_ready", "hp_ready", "y_done"))
                cbm = carve(2 * TT * P).rearrange("p (d n) -> p d n", d=2)
                CH = lambda g: (2 * g, 2 * g + 1, 16 + g, 24 + g)
                block = scope.enter_context(nc.Block())

                def tap(j, c):
                    at = (1 * P + j * 32 + c) if j < 4 else 2 * P + c
                    return vcols[:, at:at + 1]

                ORDER_B = {0: 1, 3: 0, 2: 3}
                ORDER_F = {1: 0, 2: 1, 3: 2}

                @block.tensor
                def _(pe):
                    def project(g, cs):
                        piece = ring["grp", g]
                        pe.wait_ge(piece.sem, piece.full)
                        for c in cs:
                            b = banks.open(("ch", g, c), ACTE)
                            pe.wait_ge(*b.emptied)
                            wv = view(piece, 0, KD, 256)[:, :, c * P:(c + 1) * P] if c < 2 else \
                                view(piece, 2048 + 1024 * (c - 2), KD, P)
                            for k in range(KD):
                                i = pe.matmul(b.ap[:, :], wv[:, k, :], hT[:, k, :], start=(k == 0), stop=(k == KD - 1))
                            i.then_inc(bank_full, 1)
                        piece.freed = (bank_full, b.full)

                    def to_tokens(g):
                        pe.wait_ge(silu_done, g + 1)
                        b = banks.open(("cbs", g), DVE)
                        pe.wait_ge(*b.emptied)
                        for t in range(TT):
                            tt = slice(t * P, (t + 1) * P)
                            i = pe.matmul(b.ap[:, tt], conv[:, 2, tt], conv[:, 3, tt], start=True, stop=True)
                        i.then_inc(bank_full, 1)
                        for t in range(TT):
                            b = banks.open(("tok", g, t), ACTE)
                            pe.wait_ge(*b.emptied)
                            for c in range(3):
                                i = pe.transpose(b.ap[:, c * P:(c + 1) * P], conv[:, c, t * P:(t + 1) * P], ident)
                            i.then_inc(bank_full, 1)

                    def states(g):
                        pe.wait_ge(prod_ready, g + 1)
                        for n in range(3):
                            b = banks.open(("st", g, n), DVE)
                            pe.wait_ge(*b.emptied)
                            for d in range(2):
                                t = (ORDER_F[n + 1], ORDER_B[(0, 3, 2)[n]])[d]
                                i = pe.matmul(b.ap[:, d * GW:(d + 1) * GW], tok[:, t, 256:384], xst[:, d, t, :],
                                              start=True, stop=True)
                            i.then_inc(bank_full, 1)

                    def outputs(g):
                        for t in range(TT):
                            b = banks.open(("off", g, t), DVE)
                            pe.wait_ge(*b.emptied)
                            if t == 0:
                                pe.wait_ge(hp_ready, g + 1)
                            for d in range(2):
                                if t in (ORDER_F, ORDER_B)[d]:
                                    i = pe.matmul(b.ap[:, d * GW:(d + 1) * GW], conv[:, 3, t * P:(t + 1) * P],
                                                  hp[:, d, t, :], start=True, stop=True)
                            i.then_inc(bank_full, 1)
                            b = banks.open(("diag", g, t), DVE)
                            pe.wait_ge(*b.emptied)
                            if t == 0:
                                pe.wait_ge(m_ready, g + 1)
                            for h in range(HPG):
                                for d in range(2):
                                    i = pe.matmul(b.ap[:, h * 64:(h + 1) * 64], rowsB[:, d, h, t * P:(t + 1) * P],
                                                  xdt[:, d, t, h * 64:(h + 1) * 64], start=(d == 0), stop=(d == 1))
                            i.then_inc(bank_full, 1)

                    project(0, range(4))
                    for g in range(SSD_G):
                        more = g + 1 < SSD_G
                        if more:
                            project(g + 1, (0, 1))
                        to_tokens(g)
                        if more:
                            project(g + 1, (2,))
                        states(g)
                        if more:
                            project(g + 1, (3,))
                        outputs(g)

                @block.scalar
                def _(act):
                    def take(g, cs):
                        for c in cs:
                            b = banks["ch", g, c]
                            act.wait_ge(bank_full, b.full)
                            act.activation(padded[:, c, :, 2:2 + S], b.ap[:, :].rearrange("p (s n) -> p s n", s=2),
                                           ACT.Copy).then_inc(emptied[ACTE], 1)

                    take(0, range(4))
                    for g in range(SSD_G):
                        more = g + 1 < SSD_G
                        for c in range(4):
                            act.wait_ge(conv_done, 4 * g + c + 1)
                            col = 2 * P + 32 + CH(g)[c]
                            i = act.activation(conv[:, c, :], conv[:, c, :], ACT.Silu, bias=vcols[:, col:col + 1])
                        i.then_inc(silu_done, 1)
                        if more:
                            take(g + 1, (0, 1))
                        for t in range(TT):
                            copy_out(act, ACTE, ("tok", g, t), tok[:, t, :], 384)
                        if more:
                            take(g + 1, (2,))
                        for d in range(2):
                            act.wait_ge(exps_in, 2 * g + d + 1)
                            r = rowsB[:, d, :, :].rearrange("p h n -> p (h n)")
                            act.activation(r, r, ACT.Exp).then_inc(exps_out, 1)
                        if more:
                            take(g + 1, (3,))

                @block.vector
                def _(dve):
                    link = chain(dve, dve_step)
                    heads4 = lambda ap: ap.rearrange("p (h d) -> p h d", h=HPG)

                    def convolve(g, c):
                        dve.wait_ge(emptied[ACTE], banks["ch", g, c].done)
                        o = conv[:, c, :].rearrange("p (s n) -> p s n", s=2)
                        link(dve.tensor_scalar(o, padded[:, c, :, 0:S], tap(0, CH(g)[c]), None, ALU.mult))
                        for j in range(1, CONV_W):
                            i = dve.scalar_tensor_tensor(o, padded[:, c, :, j:j + S], tap(j, CH(g)[c]), o,
                                                         ALU.mult, ALU.add)
                            if j < CONV_W - 1:
                                link(i)
                        i.then_inc(conv_done, 1)

                    for c in range(4):
                        convolve(0, c)
                    for g in range(SSD_G):
                        hs = slice(g * HPG, (g + 1) * HPG)
                        dve.wait_ge(rows_loaded, 32 * (g + 1))
                        for d in range(2):
                            r = rowsB[:, d, :, :].rearrange("p h (t n) -> p h t n", t=TT)
                            a_s = acs[:, :, d * 32 + g * HPG:d * 32 + (g + 1) * HPG].rearrange("p t h -> p h t")
                            link(dve.tensor_tensor(r, r, a_s.unsqueeze(3).broadcast_to([P, HPG, TT, P]), ALU.subtract))
                            r = rowsB[:, d, :, :].rearrange("p h n -> p (h n)")
                            dve.tensor_scalar(r, r, 0.0, None, ALU.min).then_inc(exps_in, 1)
                        b = banks["cbs", g]
                        dve.wait_ge(bank_full, b.full)
                        for d in range(2):
                            mask = const(("upto", "from")[d]).unsqueeze(1).broadcast_to([P, TT, P])
                            i = dve.tensor_tensor(cbm[:, d, :].rearrange("p (t n) -> p t n", t=TT),
                                                  b.ap[:, :].rearrange("p (t n) -> p t n", t=TT), mask, ALU.mult)
                        i.then_inc(emptied[DVE], 1)
                        for t in range(TT):
                            dve.wait_ge(emptied[ACTE], banks["tok", g, t].done)
                        xs = tok[:, :, 0:GW].rearrange("p t (h d) -> p t h d", h=HPG)
                        for d in range(2):
                            hd = slice(d * 32 + g * HPG, d * 32 + (g + 1) * HPG)
                            for dst, f in ((xst, wst), (xdt, dt)):
                                i = dve.tensor_tensor(dst[:, d, :, :].rearrange("p t (h d) -> p t h d", h=HPG), xs,
                                                      f[:, :, hd].unsqueeze(3).broadcast_to([P, TT, HPG, 64]), ALU.mult)
                        i.then_inc(prod_ready, 1)
                        for n in range(3):
                            b = banks["st", g, n]
                            dve.wait_ge(bank_full, b.full)
                            for d in range(2):
                                t = (n + 1, (0, 3, 2)[n])[d]
                                if n == 0:
                                    i = dve.tensor_copy(hp[:, d, t, :], b.ap[:, d * GW:(d + 1) * GW])
                                else:
                                    before = (n, (0, 3, 2)[n - 1])[d]
                                    chunk = (n, (1, 0, 3)[n])[d]
                                    dd = dec[:, chunk, d * 32 + g * HPG:d * 32 + (g + 1) * HPG]
                                    link(dve.tensor_tensor(heads4(hp[:, d, t, :]), heads4(hp[:, d, before, :]),
                                                           dd.unsqueeze(2).broadcast_to([P, HPG, 64]), ALU.mult))
                                    i = dve.tensor_tensor(hp[:, d, t, :], hp[:, d, t, :], b.ap[:, d * GW:(d + 1) * GW], ALU.add)
                            i.then_inc(emptied[DVE], 1)
                            dve.wait_ge(emptied[DVE], b.done)
                        dve.sem_inc(hp_ready, 1)
                        dve.wait_ge(emptied[DVE], banks["cbs", g].done)
                        for d in range(2):
                            dve.wait_ge(exps_out, 2 * g + d + 1)
                            r = rowsB[:, d, :, :]
                            i = dve.tensor_tensor(r, r, cbm[:, d, :].unsqueeze(1).broadcast_to([P, HPG, TT * P]), ALU.mult)
                        i.then_inc(m_ready, 1)
                        for t in range(TT):
                            y = Yt[:, t, g * GW:(g + 1) * GW]
                            Db = gain("ssd_D_2")[:, hs].unsqueeze(2).broadcast_to([P, HPG, 64])
                            link(dve.tensor_tensor(heads4(y), heads4(tok[:, t, 0:GW]), Db, ALU.mult))
                            b = banks["off", g, t]
                            dve.wait_ge(bank_full, b.full)
                            ds = [d for d in range(2) if t in (ORDER_F, ORDER_B)[d]]
                            for d in ds:
                                e = ea[:, t, d * 32 + g * HPG:d * 32 + (g + 1) * HPG].unsqueeze(2).broadcast_to([P, HPG, 64])
                                i = dve.tensor_tensor(heads4(off[:, d, :]), heads4(b.ap[:, d * GW:(d + 1) * GW]), e, ALU.mult)
                            i.then_inc(emptied[DVE], 1)
                            dve.wait_ge(emptied[DVE], b.done)
                            for d in ds:
                                link(dve.tensor_tensor(y, y, off[:, d, :], ALU.add))
                            b = banks["diag", g, t]
                            dve.wait_ge(bank_full, b.full)
                            dve.tensor_tensor(y, y, b.ap[:, 0:GW], ALU.add).then_inc(emptied[DVE], 1)
                            if g + 1 < SSD_G:
                                convolve(g + 1, t)
                        dve.wait_ge(emptied[DVE], b.done)

                @block.gpsimd
                def _(pool):
                    for g in range(SSD_G):
                        if g:
                            pool.wait_ge(bank_full, banks["diag", g - 1, TT - 1].full)
                        for d in range(2):
                            src = acum_dram[d * 32 + g * HPG:d * 32 + (g + 1) * HPG, :].rearrange("h n -> (h n)")
                            pool.dma_start(rowsB[:, d, :, :].rearrange("p h n -> p (h n)"),
                                           src.partition_broadcast(P)).then_inc(rows_loaded, 16)

                @block.sync
                def _(sp):
                    load_weights(sp)

            with ExitStack() as scope:
                sz = sb("sz", [P, 2, 512], scope=scope)
                g1 = rowsB[:, :, :, :].rearrange("p d h n -> p (d h n)")[:, 0:2048].rearrange("p (s n) -> p s n", s=2)
                part = rowsB[:, :, :, :].rearrange("p d h n -> p (d h n)")[:, 2048:4096].rearrange("p (s n) -> p s n", s=4)
                h_high, h_low = slots_r[:, 3, :].rearrange("p (k n) -> p k n", k=KD), hT_r
                yT_high = slots_r[:, 3:5, :].rearrange("p s (k n) -> p (s k) n", n=512)
                z_high = [slots_r[:, 4 + j, :] for j in range(2)]
                out_high = [hT_r[:, :, :].rearrange("p k n -> p (k n)"), slots_r[:, 5, :]]
                sumsq = sb("sumsq", [P, TT, 4], scope=scope)
                z_used, y_squared, y_summed, y_rooted = (sem(x) for x in ("z_used", "y_squared", "y_summed", "y_rooted"))
                h_rounded, h_split, w_split, y_rounded = (sem(x) for x in ("h_rounded", "h_split", "w_split", "y_rounded"))
                ng = VCOL["ssd_norm_w_2"]
                y_gain = lambda n: vcols[:, ng + n:ng + n + 1]

                def low(piece):
                    return slots_r[:, [q for p_, _, q in stream if p_ is piece][0], :]
                block = scope.enter_context(nc.Block())

                @block.tensor
                def _(pe):
                    gate_banks(pe, "g1", 0, 2, 0, ACTE)
                    gate_banks(pe, "g1", 0, 2, 1, ACTE)
                    pe.wait_ge(h_split, 1)
                    for n in range(4):
                        piece = ring["z", n]
                        pe.wait_ge(w_split, n + 1)
                        wh, wl = (ap.rearrange("p (k n) -> p k n", k=KD) for ap in (z_high[n % 2], low(piece)))
                        for t in range(TT):
                            tt = slice(t * P, (t + 1) * P)
                            b = banks.open(("z", n, t), ACTE)
                            pe.wait_ge(*b.emptied)
                            for k in range(KD):
                                i = matmul_split(pe, b.ap[:, :], (h_high[:, k, tt], h_low[:, k, tt]), (wh[:, k, :], wl[:, k, :]),
                                                 k == 0, k == KD - 1)
                            i.then_inc(bank_full, 1)
                        piece.freed = (bank_full, b.full)
                    pe.wait_ge(z_used, 16)
                    for n in range(16):
                        b = banks.open(("yT", n), DVE)
                        pe.wait_ge(*b.emptied)
                        for t in range(TT):
                            i = pe.transpose(b.ap[:, t * P:(t + 1) * P], Yt[:, t, n * P:(n + 1) * P], ident)
                        i.then_inc(bank_full, 1)
                    pe.wait_ge(emptied[DVE], b.done)
                    outs = [(t, n, banks.open(("so", t, n), DVE)) for t in range(TT) for n in range(2)]
                    for q in range(4):
                        piece = ring["ssd_out", q]
                        pe.wait_ge(w_split, q + 5)
                        wh, wl = (ap.rearrange("p (k n) -> p k n", k=4) for ap in (out_high[q % 2], low(piece)))
                        for t, n, b in outs:
                            if q == 0:
                                pe.wait_ge(*b.emptied)
                            c = slice(n * 512, (n + 1) * 512)
                            for k in range(4):
                                kk = 4 * q + k
                                y = (yT_high[:, kk, t * P:(t + 1) * P], Yt_r[:, t, kk * P:(kk + 1) * P])
                                i = matmul_split(pe, b.ap[:, :], y, (wh[:, k, c], wl[:, k, c]),
                                                 q == 0 and k == 0, q == 3 and k == 3)
                            if q == 3:
                                i.then_inc(bank_full, 1)
                            elif (t, n) == (TT - 1, 1):
                                i.then_inc(gate_full, 1)
                        piece.freed = (gate_full, q + 1) if q < 3 else (bank_full, b.full)
                    scratch_use.freed = (bank_full, b.full)

                @block.gpsimd
                def _(pool):
                    pool.wait_ge(y_summed, 1)
                    root(pool, 0, TT, D_INNER, y_rooted)

                @block.scalar
                def _(act):
                    act.activation(h_high, hT[:, :, :], ACT.Copy).then_inc(h_rounded, 1)
                    for s_ in range(2):
                        for n in range(2):
                            copy_out(act, ACTE, ("g1", s_, n), g1[:, s_, n * 512:(n + 1) * 512], 512)
                    for i in range(16 + 2):
                        if i < 16:
                            b = banks["z", i // 4, i % 4]
                            act.wait_ge(bank_full, b.full)
                            if i >= 2:
                                act.wait_ge(z_used, i - 1)
                            act.activation(sz[:, i % 2, :], b.ap[:, :], ACT.Silu).then_inc(emptied[ACTE], 1)
                        if i >= 2:
                            n, t = (i - 2) // 4, (i - 2) % 4
                            act.wait_ge(z_used, i - 1)
                            if i > 2:
                                act.wait_ge(y_squared, i - 2)
                            act.activation(part[:, 0, :], Yt[:, t, n * 512:(n + 1) * 512], ACT.Square,
                                           accum_out=sumsq[:, t, n:n + 1]).then_inc(y_squared, 1)
                    for n in range(16):
                        act.wait_ge(bank_full, banks["yT", n].full)
                        act.activation(yT_high[:, n, :], banks["yT", n].ap[:, :], ACT.Identity,
                                       scale=y_gain(n)).then_inc(y_rounded, 1)

                @block.vector
                def _(dve):
                    link = chain(dve, dve_step)
                    order = [ring["z", n] for n in range(4)] + [ring["ssd_out", q] for q in range(4)]

                    def split(i, free):
                        piece = order[i]
                        high = z_high[i % 2] if i < 4 else out_high[i % 2]
                        dve.wait_ge(piece.sem, piece.full)
                        if free is not None:
                            dve.wait_ge(*free)
                        link(split_high(dve, high, piece.ap))
                        split_low(dve, low(piece), piece.ap, high).then_inc(w_split, 1)

                    dve.wait_ge(h_rounded, 1)
                    split_low(dve, h_low[:, :, :], hT[:, :, :], h_high).then_inc(h_split, 1)
                    split(0, None)
                    split(1, None)
                    for n in range(4):
                        for t in range(TT):
                            i = 4 * n + t
                            dve.wait_ge(emptied[ACTE], banks["z", n, t].done)
                            y = Yt[:, t, n * 512:(n + 1) * 512]
                            dve.tensor_tensor(y, y, sz[:, i % 2, :], ALU.mult).then_inc(z_used, 1)
                        if n < 2:
                            split(n + 2, (bank_full, banks["z", n, TT - 1].full))
                    split(4, (bank_full, banks["z", 3, TT - 1].full))
                    dve.wait_ge(y_squared, 16)
                    dve.tensor_reduce(eps_rows[:, 0:TT], sumsq[:, :, :], AX.X, ALU.add).then_inc(y_summed, 1)
                    for n in range(16):
                        b = banks["yT", n]
                        dve.wait_ge(y_rounded, n + 1)
                        y_low = Yt_r[:, :, n * P:(n + 1) * P]
                        dve.scalar_tensor_tensor(y_low, b.ap[:, :].rearrange("p (t q) -> p t q", t=TT), y_gain(n),
                                                 yT_high[:, n, :].bitcast(F32).rearrange("p (t q) -> p t q", t=TT),
                                                 ALU.mult, ALU.subtract).then_inc(emptied[DVE], 1)
                        if n == 7:
                            split(5, (bank_full, banks["z", 3, TT - 1].full))
                    split(6, (gate_full, 1))
                    split(7, (gate_full, 2))
                    dve.wait_ge(y_rooted, 1)
                    link(dve.tensor_scalar(rstd[:, 0:TT], rstd[:, 0:TT], float(D_INNER) ** 0.5, None, ALU.mult))
                    dve.wait_ge(emptied[ACTE], banks["g1", 1, 1].done)
                    for t in range(TT):
                        for n in range(2):
                            b = banks["so", t, n]
                            c = slice(n * 512, (n + 1) * 512)
                            dve.wait_ge(bank_full, b.full)
                            p_ = part[:, (2 * t + n) % 4, :]
                            dve.scalar_tensor_tensor(p_, b.ap[:, :], rstd[:, t:t + 1], g1[:, 1 - t // 2, c],
                                                     ALU.mult, ALU.mult).then_inc(emptied[DVE], 1)
                            dve.wait_ge(emptied[DVE], b.done)
                            dve.tensor_tensor(streams[t][:, c], streams[t][:, c], p_, ALU.add)

                @block.sync
                def _(sp):
                    load_weights(sp)

        def expert_choice(l):
            sid = (1, 0) if l == 0 else (0,)
            NJ = len(sid)
            res = [streams[2 * NT - NJ * NT + j * NT:][:NT] for j in range(NJ)]
            T = NJ * NT
            tag = f"e{l}"
            with ExitStack() as scope:
                xgT = sb("xgT" + tag, [P, N_EXP, KD, 2 * CAP], scope=scope)
                G = sb("G" + tag, [P, NJ, 4, S], scope=scope)
                shared = sb("xn" + tag, [P, 4, D], scope=scope)
                xn = shared[:, 0:T, :]
                with ExitStack() as route:
                    wr = routers[:, l]
                    lg = sb("lg" + tag, [P, T, N_EXP], scope=route)
                    aff = sb("aff" + tag, [P, NT, NJ * N_EXP], scope=route)
                    red = sb("red" + tag, [P, T], scope=route)
                    sv = sb("sv" + tag, [P, NT, NJ * N_EXP], scope=route)
                    R = NJ * N_EXP
                    affT = sb("affT" + tag, [R, S], scope=route)
                    ones = sb("ones" + tag, [R, S], scope=route)
                    top8 = sb("top8" + tag, [R, 8], scope=route)
                    hflat = hT[:, :, :].rearrange("p k n -> p (k n)")
                    onehot = hflat[:, 0:2048].rearrange("p (t j n) -> p t j n", t=NT, j=2)
                    gated = hflat[:, 2048:4096].rearrange("p (t j n) -> p t j n", t=NT, j=2)
                    if l == 0:
                        segs = mod_segments(0, 1)
                    else:
                        segs = lambda k: [(0, S, ncol[:, 1, 1, 0, k:k + 1], modcol[:, 1, 6 + k // 4, k % 4, 0:1])]
                    norm = NormT(tag, [r for rs in res for r in rs], xn, hT, segs)
                    sub_ready, exp_ready, aff_ready, sv_ready, onehot_ready = (
                        sem(x + tag) for x in ("sub_ready_", "exp_ready_", "aff_ready_", "sv_ready_", "onehot_ready_"))
                    block = route.enter_context(nc.Block())

                    @block.tensor
                    def _(pe):
                        norm.tensor(pe)
                        for k in range(KD):
                            norm.wait_chunk(pe, k)
                        pe.wait_ge(routers_loaded, 32)
                        b = banks.open((tag, "router"), DVE)
                        pe.wait_ge(*b.emptied)
                        for t in range(T):
                            for k in range(KD):
                                i = pe.matmul(b.ap[:, t * 16:(t + 1) * 16], hT[:, k, t * P:(t + 1) * P], wr[:, k, :],
                                              start=(k == 0), stop=(k == KD - 1))
                        i.then_inc(bank_full, 1)
                        pe.wait_ge(aff_ready, 1)
                        b = banks.open((tag, "affT"), DVE)
                        pe.wait_ge(*b.emptied)
                        for t in range(NT):
                            i = pe.transpose(b.ap[0:R, t * P:(t + 1) * P], aff[:, t, :], ident)
                        i.then_inc(bank_full, 1)
                        pe.wait_ge(sv_ready, 1)
                        b = banks.open((tag, "sv"), DVE)
                        pe.wait_ge(*b.emptied)
                        for t in range(NT):
                            i = pe.transpose(b.ap[:, t * R:(t + 1) * R], affT[:, t * P:(t + 1) * P], consts[0:R, 0:R])
                        i.then_inc(bank_full, 1)
                        pe.wait_ge(onehot_ready, 1)
                        for j in range(NJ):
                            for k in range(KD):
                                b = banks.open((tag, "xg", j, k), (DVE, ACTE)[k % 2])
                                pe.wait_ge(*b.emptied)
                                for t in range(NT):
                                    i = pe.matmul(b.ap[:, :], xn[:, j * NT + t, k * P:(k + 1) * P], onehot[:, t, j, :],
                                                  start=(t == 0), stop=(t == NT - 1))
                                i.then_inc(bank_full, 1)
                            for n in range(2):
                                b = banks.open((tag, "G", j, n), (DVE, ACTE)[n])
                                pe.wait_ge(*b.emptied)
                                for m in range(2):
                                    for t in range(NT):
                                        c = (2 * n + m) * P
                                        i = pe.transpose(b.ap[:, (2 * m + t) * P:(2 * m + t + 1) * P],
                                                         gated[:, t, j, c:c + P], ident)
                                i.then_inc(bank_full, 1)

                    @block.gpsimd
                    def _(pool):
                        norm.pool(pool)

                    def take(eng, by):
                        for j in range(NJ):
                            for k in range(KD):
                                b = banks[tag, "xg", j, k]
                                if b.by != by:
                                    continue
                                eng.wait_ge(bank_full, b.full)
                                g, bias = ncol[:, l, 1, sid[j], k:k + 1], modcol[:, l, 6 + k // 4, k % 4, sid[j]:sid[j] + 1]
                                dst = xgT[:, :, k, j * CAP:(j + 1) * CAP]
                                src = b.ap[:, :].rearrange("p (e c) -> p e c", c=CAP)
                                if by == DVE:
                                    i = eng.tensor_scalar(dst, src, g, bias, ALU.mult, ALU.add)
                                else:
                                    i = eng.activation(dst, src, ACT.Identity, scale=g, bias=bias)
                                i.then_inc(emptied[by], 1)
                            for n in range(2):
                                copy_out(eng, by, (tag, "G", j, n), G[:, j, 2 * n:2 * n + 2, :].rearrange("p m t -> p (m t)"), 512)

                    @block.scalar
                    def _(act):
                        norm.scalar_squares(act)
                        norm.evacuate(act, ACTE)
                        act.wait_ge(sub_ready, 1)
                        act.activation(lg[:, :, :], lg[:, :, :], ACT.Exp).then_inc(exp_ready, 1)
                        take(act, ACTE)

                    @block.vector
                    def _(dve):
                        link = chain(dve, dve_step)
                        if NJ == 1:
                            dve.memset(xgT[:, :, :, CAP:2 * CAP], 0.0)
                        dve.memset(ones[:, :], 1.0)
                        norm.vector_scale(dve)
                        norm.evacuate(dve, DVE)
                        b = banks[tag, "router"]
                        dve.wait_ge(bank_full, b.full)
                        lgt = b.ap[:, 0:T * 16].rearrange("p (t e) -> p t e", e=16)
                        link(dve.tensor_reduce(red[:, :], lgt, AX.X, ALU.max))
                        rb = red[:, :].unsqueeze(2).broadcast_to([P, T, 16])
                        dve.tensor_tensor(lg[:, :, :], lgt, rb, ALU.subtract).then_inc(emptied[DVE], 1)
                        dve.wait_ge(emptied[DVE], b.done)
                        dve.sem_inc(sub_ready, 1)
                        dve.wait_ge(exp_ready, 1)
                        link(dve.tensor_reduce(red[:, :], lg[:, :, :], AX.X, ALU.add))
                        link(dve.reciprocal(red[:, :], red[:, :]))
                        for j in range(NJ):
                            i = dve.tensor_tensor(aff[:, :, j * 16:(j + 1) * 16], lg[:, j * NT:(j + 1) * NT, :],
                                                  red[:, j * NT:(j + 1) * NT].unsqueeze(2).broadcast_to([P, NT, 16]), ALU.mult)
                        link(i)
                        dve.sem_inc(aff_ready, 1)
                        b = banks[tag, "affT"]
                        dve.wait_ge(bank_full, b.full)
                        dve.tensor_copy(affT[:, :], b.ap[0:R, 0:S]).then_inc(emptied[DVE], 1)
                        dve.wait_ge(emptied[DVE], b.done)
                        for r in range(CAP // 8):
                            link(dve.max(top8[:, :], affT[:, :]))
                            link(dve.match_replace(affT[:, :], top8[:, :], affT[:, :], TAKEN))
                        link(dve.tensor_scalar(affT[:, :], affT[:, :], TAKEN, None, ALU.is_equal))
                        link(dve.tensor_tensor_scan(ones[:, :], ones[:, :], affT[:, :], 0.0, ALU.mult, ALU.add))
                        link(dve.tensor_tensor(affT[:, :], affT[:, :], ones[:, :], ALU.mult))
                        link(dve.tensor_scalar(affT[:, :], affT[:, :], 1.0, None, ALU.subtract))
                        dve.sem_inc(sv_ready, 1)
                        b = banks[tag, "sv"]
                        dve.wait_ge(bank_full, b.full)
                        dve.tensor_copy(sv[:, :, :].rearrange("p t r -> p (t r)"), b.ap[:, 0:NT * R]).then_inc(emptied[DVE], 1)
                        dve.wait_ge(emptied[DVE], b.done)
                        for t in range(NT):
                            for j in range(NJ):
                                o = onehot[:, t, j, :].rearrange("p (e c) -> p e c", c=CAP)
                                place = const("slot").unsqueeze(1).broadcast_to([P, 16, CAP])
                                mine = sv[:, t, j * 16:(j + 1) * 16].unsqueeze(2).broadcast_to([P, 16, CAP])
                                link(dve.tensor_tensor(o, place, mine, ALU.is_equal))
                                link(dve.tensor_tensor(gated[:, t, j, :].rearrange("p (e c) -> p e c", c=CAP), o,
                                                       aff[:, t, j * 16:(j + 1) * 16].unsqueeze(2).broadcast_to([P, 16, CAP]),
                                                       ALU.mult))
                        dve.sem_inc(onehot_ready, 1)
                        take(dve, DVE)

                    @block.sync
                    def _(sp):
                        load_weights(sp)

                hflat = hT[:, :, :].rearrange("p k n -> p (k n)")
                xg = hflat[:, 0:512].rearrange("p (k c) -> p k c", k=KD)
                sg, acts, aT, Gs, g2 = (hflat[:, 512 * n:512 * (n + 1)] for n in (1, 2, 3, 4, 5))
                sflat = shared[:, 2:4, :].rearrange("p t d -> p (t d)")
                ye = [hflat[:, 3072:3584], hflat[:, 3584:4096], sflat[:, 0:512], sflat[:, 512:1024]]
                if NJ == 2:
                    Gs = Gs.rearrange("p (j t) -> p j t", j=2)
                else:
                    Gs = Gs[:, 0:S].unsqueeze(1)
                aTv = aT.rearrange("p (b c) -> p b c", b=4)
                Y2 = shared[:, 0:NJ, :]
                names = ("xg_ready_", "half_used_", "h1_full_", "h3_full_", "silued_", "a_ready_", "tr_full_", "aT_ready_",
                         "y_full_", "ye_ready_", "gs_ready_", "sc_full_", "sc_added_", "g2_full_", "g2_ready_")
                (xg_ready, half_used, h1_full, h3_full, silued, a_ready, tr_full, aT_ready, y_full, ye_ready,
                 gs_ready, sc_full, sc_added, g2_full, g2_ready) = (sem(n + tag) for n in names)
                moved = [sem(f"y2_moved{j}_{tag}") for j in range(4)]
                PIECES = [ring["moe2", l, j] for j in range(6)]
                SC = 4 * NJ
                TURNS = N_EXP // 4
                block = scope.enter_context(nc.Block())

                @block.tensor
                def _(pe):
                    for n in range(2):
                        for s_ in range(2):
                            row = 64 * n + 32 * s_
                            for j in range(4):
                                col = modcol[:, l, 10 + n, j, sid[s_ % NJ]:sid[s_ % NJ] + 1]
                                i = pe.matmul(psum[7][row:row + 32, j * P:(j + 1) * P], col.broadcast_to([P, 32]), ident,
                                              start=True, stop=True, tile_position=(0, row), skip_group_check=True)
                    i.then_inc(g2_full, 1)

                    def halves(bank, lhsT, first, e, done):
                        for h in range(2):
                            piece = PIECES[first + h]
                            pe.wait_ge(piece.sem, piece.full + 16 * e)
                            wv = view(piece, 0, 4, D)
                            for k in range(4):
                                for n in range(2):
                                    i = pe.matmul(bank[64 * n:64 * n + 64, :], lhsT(4 * h + k), wv[:, k, n * 512:(n + 1) * 512],
                                                  start=(h == 0 and k == 0), stop=(h == 1 and k == 3),
                                                  tile_position=(0, 64 * n), skip_group_check=True)
                            i.then_inc(half_used if h == 0 else done, 1)

                    def expert(e, first):
                        pe.wait_ge(xg_ready, e + 1)
                        if not first:
                            pe.wait_ge(a_ready, e)
                        halves(psum[0], lambda k: xg[:, k, :], 0, e, h1_full)
                        halves(psum[1], lambda k: xg[:, k, :], 2, e, h3_full)
                        pe.wait_ge(a_ready, e + 1)
                        if not first:
                            pe.wait_ge(aT_ready, e)
                        for b in range(4):
                            i = pe.transpose(psum[2][:, b * P:(b + 1) * P], acts[:, b * P:(b + 1) * P], ident)
                        i.then_inc(tr_full, 1)
                        pe.wait_ge(aT_ready, e + 1)
                        if not first:
                            pe.wait_ge(ye_ready, e)
                        halves(psum[3], lambda k: aTv[:, k % 4, 64 * (k // 4):64 * (k // 4) + 64], 4, e, y_full)

                    def scatter(turn, first):
                        for j in range(4):
                            pe.wait_ge(moved[j], 32 * NJ * (turn + 1))
                        pe.wait_ge(gs_ready, turn + 1)
                        for q in range(SC):
                            j, t, n = q // 4, q // 2 % 2, q % 2
                            if q >= 4 or not first:
                                pe.wait_ge(sc_added, SC * turn + q - 3)
                            pe.matmul(psum[4 + q % 4][:, :], Gs[:, j, t * P:(t + 1) * P], Y2[:, j, n * 512:(n + 1) * 512],
                                      start=True, stop=True, skip_group_check=True).then_inc(sc_full, 1)

                    for e in range(4):
                        expert(e, e == 0)
                    pe.wait_ge(g2_ready, 1)
                    expert(4, False)
                    expert(5, False)
                    scatter(0, True)
                    with pe.Fori(1, TURNS - 1) as turn:
                        for j in range(2, 6):
                            expert(4 * turn + j, False)
                        scatter(turn, False)
                    expert(N_EXP - 2, False)
                    expert(N_EXP - 1, False)
                    scatter(TURNS - 1, False)

                @block.scalar
                def _(act):
                    def gather(e):
                        act.activation(xg, xgT[:, e, :, :], ACT.Copy).then_inc(xg_ready, 1)

                    def silu(e):
                        act.wait_ge(h1_full, e + 1)
                        act.activation(sg, psum[0][:, :], ACT.Silu).then_inc(silued, 1)

                    def transposed(e):
                        act.wait_ge(tr_full, e + 1)
                        act.activation(aT, psum[2][:, :], ACT.Copy).then_inc(aT_ready, 1)

                    def move(e, j):
                        act.wait_ge(ye_ready, e + 1)
                        for s_ in range(NJ):
                            for n in range(2):
                                act.dma_start(Y2[32 * j:32 * j + 32, s_, n * 512:(n + 1) * 512],
                                              ye[j][64 * n + 32 * s_:64 * n + 32 * s_ + 32, :]).then_inc(moved[j], 16)

                    def gates(turn):
                        act.activation(Gs, G[:, :, turn, :], ACT.Copy).then_inc(gs_ready, 1)

                    def second_half(turn, first):
                        gather(4 * turn + 2)
                        silu(4 * turn + 2)
                        if not first:
                            act.wait_ge(sc_full, SC * turn)
                        move(4 * turn, 0)
                        move(4 * turn + 1, 1)
                        transposed(4 * turn + 2)
                        gates(turn)
                        gather(4 * turn + 3)
                        silu(4 * turn + 3)
                        move(4 * turn + 2, 2)
                        transposed(4 * turn + 3)

                    def next_half(turn):
                        gather(4 * turn + 4)
                        silu(4 * turn + 4)
                        move(4 * turn + 3, 3)
                        transposed(4 * turn + 4)
                        gather(4 * turn + 5)
                        silu(4 * turn + 5)
                        transposed(4 * turn + 5)

                    for e in range(2):
                        gather(e)
                        if e == 0:
                            act.wait_ge(g2_full, 1)
                            act.activation(g2, psum[7][:, :], ACT.Copy).then_inc(g2_ready, 1)
                        silu(e)
                        transposed(e)
                    second_half(0, True)
                    next_half(0)
                    with act.Fori(1, TURNS - 1) as turn:
                        second_half(turn, False)
                        next_half(turn)
                    second_half(TURNS - 1, False)
                    move(N_EXP - 1, 3)

                @block.vector
                def _(dve):
                    dve.wait_ge(g2_ready, 1)

                    def expert(e, j, turn):
                        dve.wait_ge(silued, e + 1)
                        dve.wait_ge(h3_full, e + 1)
                        dve.tensor_tensor(acts, sg, psum[1][:, :], ALU.mult).then_inc(a_ready, 1)
                        dve.wait_ge(y_full, e + 1)
                        if turn is not None:
                            dve.wait_ge(moved[j], 32 * NJ * turn)
                        dve.tensor_tensor(ye[j], psum[3][:, :], g2, ALU.mult).then_inc(ye_ready, 1)

                    def add(turn, first):
                        if not first:
                            dve.wait_ge(sc_added, SC * turn)
                        for q in range(SC):
                            j, t, n = q // 4, q // 2 % 2, q % 2
                            c = slice(n * 512, (n + 1) * 512)
                            dve.wait_ge(sc_full, SC * turn + q + 1)
                            dve.tensor_tensor(res[j][t][:, c], res[j][t][:, c], psum[4 + q % 4][:, :], ALU.add).then_inc(sc_added, 1)

                    for e in range(4):
                        expert(e, e, None)
                    expert(4, 0, 1)
                    expert(5, 1, 1)
                    add(0, True)
                    with dve.Fori(1, TURNS - 1) as turn:
                        for j in range(2, 6):
                            expert(4 * turn + j, j % 4, turn + j // 4)
                        add(turn, False)
                    expert(N_EXP - 2, 2, TURNS - 1)
                    expert(N_EXP - 1, 3, TURNS - 1)
                    add(TURNS - 1, False)

                @block.sync
                def _(sp):
                    with sp.Fori(1, N_EXP) as e:
                        for j in range(6):
                            if j % 2 == 0:
                                sp.wait_ge(half_used, 3 * e - 2 + j // 2)
                            else:
                                sp.wait_ge((h1_full, h3_full, y_full)[j // 2], e)
                            src = w_v[j // 2][:, l * N_EXP + e, 4 * (j % 2):4 * (j % 2) + 4]
                            sp.dma_start(view(PIECES[j], 0, 4, D), src).then_inc(PIECES[j].sem, 16)
                    for j in range(6):
                        PIECES[j].freed = (half_used, 3 * N_EXP - 2 + j // 2) if j % 2 == 0 else ((h1_full, h3_full, y_full)[j // 2], N_EXP)
                    load_weights(sp)

        expert_choice(0)

        with ExitStack() as scope:
            shared = sb("xn5", [P, 4, D], scope=scope)
            q = sb("q5", [P, NT, QH * 64], scope=scope)
            kk = sb("k5", [P, TT, KVH * 64], scope=scope)
            vv = sb("v5", [P, TT, KVH * 64], scope=scope)
            kT = sb("kT5", [64, KVH, TT * P], scope=scope)
            g1 = sb("g15", [P, D], scope=scope)
            part = sb("part5", [P, 2, 512], scope=scope)
            pT5 = sb("pT5", [P, 2048], scope=scope)
            bufs = (sb("probs5", [P, 4, 512], scope=scope), (pT5, hT[:, :, :].rearrange("p k n -> p (k n)")[:, 2048:4096]),
                    sb("negmax5", [P, 32], scope=scope), sb("sums5", [P, 32], scope=scope))
            qT = shared[0:64, :, :].rearrange("p t d -> p (t d)").rearrange("p (h n) -> p h n", h=QH)
            hflat = hT[:, :, :].rearrange("p k n -> p (k n)")
            sq = hflat[:, 0:2048].rearrange("p (h d) -> p h d", d=64)
            tmp = hflat[:, 2048:3072].rearrange("p (a h d) -> p a h d", a=2, h=16)
            oT = hflat[:, 0:2048].rearrange("p (k n) -> p k n", k=8)
            norm = NormT("n5", streams, shared, hT, mod_segments(1, 0))
            qh = q[:, :, :].rearrange("p t (h d) -> p t h d", d=64)
            kh = kk[:, :, :].rearrange("p t (h d) -> p t h d", d=64)
            kn, qn = HeadNorm("k5"), HeadNorm("q5")
            cos2 = const("cos2d").rearrange("p (t d) -> p t d", t=NT)
            sin2 = const("sin2d").rearrange("p (t d) -> p t d", t=NT)
            q_ready, k_ready = sem("q5_ready"), sem("k5_ready")
            to_qT = Transpose("qT5", lambda n, t: qh[:, t, n, :], QH, 64, lambda g, m: qT[:, g:g + m, :])
            to_kT = Transpose("kT5", lambda n, t: kh[:, t, n, :], KVH, 64, lambda g, m: kT[:, g:g + m, :], tiles=TT)
            att = Attention("att5", QH, lambda h: qT[:, h, :], lambda h: kT[:, h // QPK, :],
                            lambda h, kt: vv[:, kt, (h // QPK) * 64:(h // QPK + 1) * 64], TT * P, HD ** -0.5, lambda p: oT[:, p, :], bufs)
            block = scope.enter_context(nc.Block())

            @block.tensor
            def _(pe):
                gate_banks(pe, "g15", 1, 2, 0, ACTE)
                norm.tensor(pe)
                for k in range(KD):
                    norm.wait_chunk(pe, k)
                piece = ring["qkv", 2]
                pe.wait_ge(piece.sem, piece.full)
                wv = view(piece, 0, KD, 512)
                for t in range(TT):
                    b, _ = gemm(pe, ("kv5", t), lambda k: hT[:, k, t * P:(t + 1) * P], KD, t, lambda k: wv[:, k, :], 512, DVE)
                piece.freed = (bank_full, b.full)
                for n in range(2):
                    piece = ring["qkv", n]
                    pe.wait_ge(piece.sem, piece.full)
                    wv = view(piece, 0, KD, 512)
                    for t in range(NT):
                        b, _ = gemm(pe, ("q5", n, t), lambda k: hT[:, k, S + t * P:S + (t + 1) * P], KD, t,
                                    lambda k: wv[:, k, :], 512, ACTE)
                    piece.freed = (bank_full, b.full)
                pe.wait_ge(k_ready, 1)
                to_kT.tensor(pe)
                pe.wait_ge(q_ready, 1)
                to_qT.tensor(pe)
                to_qT.wait_all(pe)
                to_kT.wait_all(pe)
                att.tensor(pe)
                pe.wait_ge(emptied[DVE], banks["att5", "pv", QH // 2 - 1].done)
                w0, w1 = ring["attn_out", 0], ring["attn_out", 1]
                pe.wait_ge(w0.sem, w0.full)
                pe.wait_ge(w1.sem, w1.full)
                wv2 = (view(w0, 0, 4, D), view(w1, 0, 4, D))
                for t in range(NT):
                    for n in range(2):
                        b, _ = gemm(pe, ("ao5", t, n), lambda k: oT[:, k, t * P:(t + 1) * P], KD, t,
                                    lambda k: wv2[k // 4][:, k % 4, n * 512:(n + 1) * 512], 512, DVE)
                w0.freed = w1.freed = (bank_full, b.full)

            @block.gpsimd
            def _(pool):
                norm.pool(pool)
                kn.pool(pool, KVH, 64, T=TT)
                qn.pool(pool, QH, 64)

            @block.scalar
            def _(act):
                norm.scalar_squares(act)
                for n in range(2):
                    copy_out(act, ACTE, ("g15", 0, n), g1[:, n * 512:(n + 1) * 512], 512)
                norm.evacuate(act, ACTE)
                for n in range(2):
                    for t in range(NT):
                        copy_out(act, ACTE, ("q5", n, t), q[:, t, n * 512:(n + 1) * 512], 512)
                to_kT.evacuate(act, ACTE)
                to_qT.evacuate(act, ACTE)
                att.scalar(act)

            @block.vector
            def _(dve):
                link = chain(dve, dve_step)
                norm.vector_scale(dve)
                norm.evacuate(dve, DVE)
                for t in range(TT):
                    b = banks["kv5", t]
                    dve.wait_ge(bank_full, b.full)
                    dve.tensor_copy(kk[:, t, :], b.ap[:, 0:256])
                    dve.tensor_copy(vv[:, t, :], b.ap[:, 256:512]).then_inc(emptied[DVE], 1)
                dve.wait_ge(emptied[DVE], banks["kv5", TT - 1].done)
                k_sq = pT5[:, 0:1024].rearrange("p (h d) -> p h d", d=64)
                k_tmp = pT5[:, 1024:2048].rearrange("p (a h d) -> p a h d", a=2, h=16)
                kn.vector_sum(dve, link, kh, k_sq, KVH, 64, T=TT)
                kn.vector_scale(dve, link, kh, kh, [(0, KVH, gain("attn_k_norm_w_2"))], KVH, 64, T=TT)
                rope(dve, link, kh[:, NT:TT], kh[:, NT:TT], k_tmp, KVH, 32, 64, 0, cos2, sin2)
                dve.sem_inc(k_ready, 1)
                dve.wait_ge(emptied[ACTE], banks["q5", 1, NT - 1].done)
                qn.vector_sum(dve, link, qh, sq, QH, 64)
                qn.vector_scale(dve, link, qh, qh, [(0, QH, gain("attn_q_norm_w_2"))], QH, 64)
                rope(dve, link, qh, qh, tmp, QH, 32, 64, 0, cos2, sin2)
                dve.sem_inc(q_ready, 1)
                to_kT.evacuate(dve, DVE)
                to_qT.evacuate(dve, DVE)
                att.vector(dve, link)
                dve.wait_ge(emptied[ACTE], banks["g15", 0, 1].done)
                for t in range(NT):
                    for n in range(2):
                        c = slice(n * 512, (n + 1) * 512)
                        b = banks["ao5", t, n]
                        dve.wait_ge(bank_full, b.full)
                        dve.tensor_tensor(part[:, n, :], b.ap[:, :], g1[:, c], ALU.mult).then_inc(emptied[DVE], 1)
                        dve.wait_ge(emptied[DVE], b.done)
                        link(dve.tensor_tensor(X[:, t, c], X[:, t, c], part[:, n, :], ALU.add))

            @block.sync
            def _(sp):
                load_weights(sp)

        expert_choice(1)

        with ExitStack() as scope:
            fin = sb("fin", [P, D], scope=scope)
            y = sb("y_out", [P, NT, D], scope=scope)
            fin_loaded, f_squared, f_rooted, f_done, out_stored = (sem(x) for x in ("fin_loaded", "f_squared", "f_rooted", "f_done", "out_stored"))
            block = scope.enter_context(nc.Block())

            @block.scalar
            def _(act):
                for t in range(NT):
                    act.activation(y[:, t, :], X[:, t, :], ACT.Square, accum_out=eps_rows[:, t:t + 1]).then_inc(f_squared, 1)

            @block.gpsimd
            def _(pool):
                pool.wait_ge(f_squared, NT)
                root(pool, 0, NT, D, f_rooted)

            @block.vector
            def _(dve):
                link = chain(dve, dve_step)
                dve.wait_ge(f_rooted, 1)
                link(dve.tensor_scalar(rstd[:, 0:NT], rstd[:, 0:NT], float(D) ** 0.5, None, ALU.mult))
                dve.wait_ge(fin_loaded, 16)
                for t in range(NT):
                    dve.scalar_tensor_tensor(y[:, t, :], X[:, t, :], rstd[:, t:t + 1], fin[:, :],
                                             ALU.mult, ALU.mult).then_inc(f_done, 1)

            @block.sync
            def _(sp):
                sp.dma_start(fin[:, :], A["final_norm_w_2"].partition_broadcast(P)).then_inc(fin_loaded, 16)
                for t in range(NT):
                    sp.wait_ge(f_done, t + 1)
                    sp.dma_start(out["out"][0, t * P:(t + 1) * P, :], y[:, t, :]).then_inc(out_stored, 16)
                sp.wait_ge(out_stored, 16 * NT)



_CONST_TABLE = constant_table()
NAMES = ["x", "mem", "positions", "attn_norm_g", "w_in", "dsa_q_norm_g", "dsa_k_norm_g", "mla_cq_norm_g",
         "mla_ckv_norm_g", "mla_w_uq", "mla_w_ukv", "mla_q_norm_g", "mla_k_norm_g", "w_branch_dsa",
         "w_branch_mla", "w_out", "mem_x_norm_g", "mem_norm_g", "mem_w_q", "mem_w_kv", "mem_q_norm_g",
         "mem_k_norm_g", "mem_w_o", "moe_norm_g", "moe_w_group", "moe_w_expert", "moe_expert_bias",
         "moe_w_gate", "moe_w_up", "moe_w_down", "c_2", "ctx_2", "c_ctx_2", "ada_w_2", "ada_b_2",
         "norm1_w_2", "norm2_w_2", "ssd_in_w_2", "ssd_conv_w_2", "ssd_conv_b_2", "ssd_dt_bias_2",
         "ssd_A_log_2", "ssd_D_2", "ssd_norm_w_2", "ssd_out_w_2", "attn_qkv_w_2", "attn_q_norm_w_2",
         "attn_k_norm_w_2", "attn_out_w_2", "moe_router_w_2", "moe_w1_2", "moe_w3_2", "moe_w2_2",
         "final_norm_w_2"]


def kernel(**inputs):
    import concourse.bacc as bacc
    from concourse.bass_utils import run_bass_kernel_spmd

    nc = bacc.Bacc("TRN2", target_bir_lowering=False, num_devices=1)
    arrays = {"consts": _CONST_TABLE}
    for name in NAMES:
        arrays[name] = np.ascontiguousarray(inputs[name])
    A = {n: nc.dram_tensor("in_" + n, a.shape, mybir.dt.from_np(a.dtype), kind="ExternalInput").ap()
         for n, a in arrays.items()}
    out = {"out": nc.dram_tensor("out_x", (1, S, D), F32, kind="ExternalOutput").ap()}
    build(nc, A, out)
    r = run_bass_kernel_spmd(nc, [{"in_" + n: a for n, a in arrays.items()}], core_ids=[0])
    return r.results[0]["out_x"]
```
